# Optimizing a Trainium2 kernel written in Bass

```python
import math
import jax, jax.numpy as jnp
from jax import lax
import numpy as np

D_MODEL = 1024
BATCH = 1
SEQ = 1024
DEPTH = 1

HEAD_DIM = 64
SSM_WIDTH = 3 * D_MODEL // 8
FFT_WIDTH = D_MODEL // 4
ATT_WIDTH = D_MODEL - SSM_WIDTH - FFT_WIDTH
SSM_GROUP = 16
SSM_GROUPS = SSM_WIDTH // SSM_GROUP
SSM_STATE = 64
FFT_HEADS = FFT_WIDTH // HEAD_DIM
N_Q_HEADS = ATT_WIDTH // HEAD_DIM
N_KV_HEADS = 2
GQA_GROUP = N_Q_HEADS // N_KV_HEADS
KV_WIDTH = N_KV_HEADS * HEAD_DIM
IN_WIDTH = SSM_WIDTH + FFT_WIDTH + ATT_WIDTH + 2 * KV_WIDTH
WINDOW = 128
BLOCK = 128
KV_SPAN = 3 * BLOCK
D_FF = ((8 * D_MODEL // 3 + 255) // 256) * 256
DT_MIN = 1e-3
DT_MAX = 1e-1
RMS_EPS = 1e-6
NEG_INF = -1e30


def rms_norm(x, gain):
    xf = x.astype(jnp.float32)
    y = xf * lax.rsqrt(jnp.mean(xf * xf, axis=-1, keepdims=True) + RMS_EPS)
    return (y * gain.astype(jnp.float32)).astype(x.dtype)

def _scan_combine(left, right):
    a_l, h_l = left
    a_r, h_r = right
    return a_l * a_r, a_r * h_l + h_r

def s5_mixer(u, lam_re, lam_im, log_dt, b_re, b_im, c_re, c_im, d_skip, w_glu):
    bsz, seq, _ = u.shape
    f32 = jnp.float32
    uf = u.astype(f32).reshape(bsz, seq, SSM_GROUPS, SSM_GROUP)
    lam = lax.complex(lam_re.astype(f32), lam_im.astype(f32))
    dt = jnp.exp(log_dt.astype(f32))[..., None]
    lam_bar = jnp.exp(lam * dt)
    b = lax.complex(b_re.astype(f32), b_im.astype(f32))
    b_bar = ((lam_bar - 1.0) / lam)[..., None] * b
    states = []
    for d, rev in ((0, False), (1, True)):
        bu = lax.complex(jnp.einsum('bsgc,gpc->bsgp', uf, b_bar[d].real),
                         jnp.einsum('bsgc,gpc->bsgp', uf, b_bar[d].imag))
        a = jnp.broadcast_to(lam_bar[d], bu.shape)
        _, h_dir = lax.associative_scan(_scan_combine, (a, bu), reverse=rev, axis=1)
        states.append(h_dir)
    h = states[0] + states[1]
    y = (jnp.einsum('bsgp,gcp->bsgc', h.real, c_re.astype(f32))
         - jnp.einsum('bsgp,gcp->bsgc', h.imag, c_im.astype(f32)))
    y = y.reshape(bsz, seq, SSM_WIDTH) + d_skip.astype(f32) * u.astype(f32)
    y = jax.nn.gelu(y).astype(u.dtype)
    return y * jax.nn.sigmoid(y @ w_glu)

def fourier_mixer(f, w_fft):
    bsz, seq, _ = f.shape
    ff = f.astype(jnp.float32).reshape(bsz, seq, FFT_HEADS, HEAD_DIM)
    mixed = jnp.fft.fft2(ff, axes=(1, 3), norm='ortho').real.astype(f.dtype)
    return jnp.einsum('bshd,hde->bshe', mixed, w_fft).reshape(bsz, seq, FFT_WIDTH)

def window_attention(q, k, v, sink):
    bsz, seq, _ = q.shape
    nblk = seq // BLOCK
    qb = (q * HEAD_DIM ** -0.5).reshape(bsz, nblk, BLOCK, N_KV_HEADS, GQA_GROUP, HEAD_DIM)

    def band(t):
        t = t.reshape(bsz, seq, N_KV_HEADS, HEAD_DIM)
        t = jnp.pad(t, ((0, 0), (BLOCK, BLOCK), (0, 0), (0, 0)))
        t = t.reshape(bsz, nblk + 2, BLOCK, N_KV_HEADS, HEAD_DIM)
        return jnp.concatenate([t[:, :-2], t[:, 1:-1], t[:, 2:]], axis=2)

    kb, vb = band(k), band(v)
    qi = jnp.arange(BLOCK)[:, None]
    kj = jnp.arange(KV_SPAN)[None, :]
    dist = jnp.abs(qi + BLOCK - kj)
    key_pos = jnp.arange(nblk)[:, None] * BLOCK - BLOCK + kj
    valid = (dist <= WINDOW)[None] & ((key_pos >= 0) & (key_pos < seq))[:, None, :]
    slopes = jnp.exp2(-8.0 * jnp.arange(1, N_Q_HEADS + 1, dtype=jnp.float32) / N_Q_HEADS)
    slopes = slopes.reshape(N_KV_HEADS, GQA_GROUP)
    bias = -slopes[:, :, None, None] * dist.astype(jnp.float32)
    scores = jnp.einsum('bnqkgd,bnskd->bnkgqs', qb, kb).astype(jnp.float32) + bias
    scores = jnp.where(valid[None, :, None, None], scores, NEG_INF)
    sink_l = sink.astype(jnp.float32).reshape(1, 1, N_KV_HEADS, GQA_GROUP, 1, 1)
    m = jnp.maximum(jnp.max(scores, axis=-1, keepdims=True), sink_l)
    p = jnp.exp(scores - m)
    p = p / (jnp.sum(p, axis=-1, keepdims=True) + jnp.exp(sink_l - m))
    out = jnp.einsum('bnkgqs,bnskd->bnqkgd', p.astype(v.dtype), vb)
    return out.reshape(bsz, seq, ATT_WIDTH)

def dwconv3(h, w, b):
    hp = jnp.pad(h, ((0, 0), (1, 1), (0, 0)))
    return hp[:, :-2] * w[0] + hp[:, 1:-1] * w[1] + hp[:, 2:] * w[2] + b

def first_inputs(seed: int = 0) -> dict:
    key = jax.random.key(seed)
    ks = iter(jax.random.split(key, 32))
    nrm = lambda shape, scale: scale * jax.random.normal(next(ks), shape, jnp.float32)
    L, D, G, P = DEPTH, D_MODEL, SSM_GROUPS, SSM_STATE
    lam_im_base = jnp.pi * jnp.arange(P, dtype=jnp.float32)
    return {
        'x': nrm((BATCH, SEQ, D), 1.0),
        'c': nrm((BATCH, D), 1.0),
        'w_ada': nrm((L, D, 6 * D), 0.5 * D ** -0.5),
        'b_ada': nrm((L, 6 * D), 0.01),
        'g_pre_mix': 1.0 + nrm((L, D), 0.05),
        'g_post_mix': 1.0 + nrm((L, D), 0.05),
        'g_pre_ffn': 1.0 + nrm((L, D), 0.05),
        'g_post_ffn': 1.0 + nrm((L, D), 0.05),
        'w_in': nrm((L, D, IN_WIDTH), D ** -0.5),
        'lam_re': -0.5 + nrm((L, 2, G, P), 0.01),
        'lam_im': lam_im_base + nrm((L, 2, G, P), 0.01),
        'log_dt': jax.random.uniform(next(ks), (L, 2, G), jnp.float32,
                                     minval=math.log(DT_MIN), maxval=math.log(DT_MAX)),
        'b_re': nrm((L, 2, G, P, SSM_GROUP), (2 * SSM_GROUP) ** -0.5),
        'b_im': nrm((L, 2, G, P, SSM_GROUP), (2 * SSM_GROUP) ** -0.5),
        'c_re': nrm((L, G, SSM_GROUP, P), (2 * P) ** -0.5),
        'c_im': nrm((L, G, SSM_GROUP, P), (2 * P) ** -0.5),
        'd_skip': nrm((L, SSM_WIDTH), 1.0),
        'w_glu': nrm((L, SSM_WIDTH, SSM_WIDTH), SSM_WIDTH ** -0.5),
        'w_fft': nrm((L, FFT_HEADS, HEAD_DIM, HEAD_DIM), HEAD_DIM ** -0.5),
        'sink': nrm((L, N_Q_HEADS), 1.0),
        'w_out': nrm((L, D, D), D ** -0.5),
        'w_up': nrm((L, D, 2 * D_FF), D ** -0.5),
        'conv_w': nrm((L, 3, 2 * D_FF), 3 ** -0.5),
        'conv_b': nrm((L, 2 * D_FF), 0.01),
        'w_down': nrm((L, D_FF, D), D_FF ** -0.5),
    }

def first_block(x, c, w_ada, b_ada, g_pre_mix, g_post_mix, g_pre_ffn, g_post_ffn, w_in,
              lam_re, lam_im, log_dt, b_re, b_im, c_re, c_im, d_skip, w_glu, w_fft, sink,
              w_out, w_up, conv_w, conv_b, w_down):
    splits = [SSM_WIDTH, SSM_WIDTH + FFT_WIDTH, SSM_WIDTH + FFT_WIDTH + ATT_WIDTH,
              SSM_WIDTH + FFT_WIDTH + ATT_WIDTH + KV_WIDTH]
    for l in range(DEPTH):
        mod = (c @ w_ada[l] + b_ada[l])[:, None, :]
        sh_m, sc_m, gt_m, sh_f, sc_f, gt_f = jnp.split(mod, 6, axis=-1)

        h = rms_norm(x, g_pre_mix[l]) * (1.0 + sc_m) + sh_m
        z = h @ w_in[l]
        u, f, q, k, v = jnp.split(z, splits, axis=-1)
        y_ssm = s5_mixer(u, lam_re[l], lam_im[l], log_dt[l], b_re[l], b_im[l],
                         c_re[l], c_im[l], d_skip[l], w_glu[l])
        y_fft = fourier_mixer(f, w_fft[l])
        y_att = window_attention(q, k, v, sink[l])
        y = jnp.concatenate([y_ssm.astype(x.dtype), y_fft.astype(x.dtype), y_att.astype(x.dtype)], axis=-1) @ w_out[l]
        x = x + gt_m * rms_norm(y, g_post_mix[l])

        h = rms_norm(x, g_pre_ffn[l]) * (1.0 + sc_f) + sh_f
        up = dwconv3(h @ w_up[l], conv_w[l], conv_b[l])
        gate, val = jnp.split(up, 2, axis=-1)
        y = (jax.nn.gelu(gate) * val) @ w_down[l]
        x = x + gt_f * rms_norm(y, g_post_ffn[l])
    return x


N_ATT_HEADS = 8
ATT_HEAD_DIM = 64
ATT_WIDTH_2 = N_ATT_HEADS * ATT_HEAD_DIM
KV_LATENT = 128
IDX_HEADS = 4
IDX_DIM = 64
TOPK_MAX = 256
Q_BLOCK = 128
N_MLP_GROUPS = 8
MLP_GROUP_DIM = 64
MLP_WIDTH = N_MLP_GROUPS * MLP_GROUP_DIM
CHUNK = 128
MIX_WIDTH = ATT_WIDTH_2 + MLP_WIDTH
D_FF_2 = 2816
DEEPNORM_ALPHA = float((2 * DEPTH) ** 0.25)
DEEPNORM_BETA = float((8 * DEPTH) ** -0.25)
LN_EPS = 1e-5
IN_COLS = ATT_WIDTH_2 + KV_LATENT + IDX_HEADS * IDX_DIM + IDX_DIM + IDX_HEADS + 2 * MLP_WIDTH
SPLITS = tuple(np.cumsum([ATT_WIDTH_2, KV_LATENT, IDX_HEADS * IDX_DIM, IDX_DIM, IDX_HEADS]).tolist())


def _layernorm(x, g, b):
    xf = x.astype(jnp.float32)
    mu = jnp.mean(xf, axis=-1, keepdims=True)
    var = jnp.mean(jnp.square(xf - mu), axis=-1, keepdims=True)
    y = (xf - mu) * lax.rsqrt(var + LN_EPS)
    return (y * g.astype(jnp.float32) + b.astype(jnp.float32)).astype(x.dtype)

def _rmsnorm(x, g):
    xf = x.astype(jnp.float32)
    y = xf * lax.rsqrt(jnp.mean(jnp.square(xf), axis=-1, keepdims=True) + LN_EPS)
    return (y * g.astype(jnp.float32)).astype(x.dtype)

def _swiglu(x, w1, w3, w2):
    return (jax.nn.silu(x @ w1) * (x @ w3)) @ w2

def _sparse_attention(q, c, qi, ki, wi, w_uk, w_uv, topk):
    B, L = q.shape[0], q.shape[1]
    q_abs = jnp.einsum('blhd,hcd->blhc', q, w_uk) * (ATT_HEAD_DIM ** -0.5)
    wi_s = wi.astype(jnp.float32) * (IDX_HEADS ** -0.5)
    ki_f = ki.astype(jnp.float32)
    key_pos = jnp.arange(L)

    def block(i):
        start = i * Q_BLOCK
        qa = lax.dynamic_slice_in_dim(q_abs, start, Q_BLOCK, axis=1)
        qib = lax.dynamic_slice_in_dim(qi, start, Q_BLOCK, axis=1)
        wib = lax.dynamic_slice_in_dim(wi_s, start, Q_BLOCK, axis=1)
        t = start + jnp.arange(Q_BLOCK)
        causal = key_pos[None, :] <= t[:, None]
        logit = jnp.einsum('bqhd,bsd->bqhs', qib.astype(jnp.float32), ki_f) * (IDX_DIM ** -0.5)
        score = jnp.einsum('bqh,bqhs->bqs', wib, jax.nn.relu(logit))
        score = jnp.where(causal[None], score, -jnp.inf)
        _, sel = lax.top_k(score, topk)
        c_sel = jax.vmap(lambda cb, ib: cb[ib])(c, sel)
        valid = sel <= t[None, :, None]
        sc = jnp.einsum('bqhc,bqkc->bqhk', qa.astype(jnp.float32), c_sel.astype(jnp.float32))
        sc = jnp.where(valid[:, :, None, :], sc, -jnp.inf)
        p = jax.nn.softmax(sc, axis=-1).astype(c.dtype)
        o_lat = jnp.einsum('bqhk,bqkc->bqhc', p, c_sel)
        return jnp.einsum('bqhc,hcd->bqhd', o_lat, w_uv)

    out = lax.map(block, jnp.arange(L // Q_BLOCK))
    return out.transpose(1, 0, 2, 3, 4).reshape(B, L, ATT_WIDTH_2)

def _chunked_gmlp(z, gln_g, gln_b, ws, bs):
    B, L = z.shape[0], z.shape[1]
    z = jax.nn.gelu(z)
    u, v = jnp.split(z, 2, axis=-1)
    v = _layernorm(v, gln_g, gln_b)
    v = v.reshape(B, L // CHUNK, CHUNK, N_MLP_GROUPS, MLP_GROUP_DIM)
    tri = jnp.tril(jnp.ones((CHUNK, CHUNK), dtype=bool))
    ws_c = jnp.where(tri[None], ws, jnp.zeros_like(ws))
    sv = jnp.einsum('gts,bnsgd->bntgd', ws_c, v) + bs.T[None, None, :, :, None]
    return u * sv.reshape(B, L, MLP_WIDTH)

def _mixer(h, w_in, kv_norm_g, w_uk, w_uv, gln_g, gln_b, ws, bs, w_out, topk):
    B, L, _ = h.shape
    proj = h @ w_in
    q, c, qi, ki, wi, z = jnp.split(proj, SPLITS, axis=-1)
    q = q.reshape(B, L, N_ATT_HEADS, ATT_HEAD_DIM)
    c = _rmsnorm(c, kv_norm_g)
    qi = qi.reshape(B, L, IDX_HEADS, IDX_DIM)
    att = _sparse_attention(q, c, qi, ki, wi, w_uk, w_uv, topk)
    gm = _chunked_gmlp(z, gln_g, gln_b, ws, bs)
    return jnp.concatenate([att, gm], axis=-1) @ w_out

def second_inputs(seed: int = 0) -> dict:
    key = jax.random.key(seed)
    ks = jax.random.split(key, 24)
    f32 = jnp.float32

    def nrm(k, shape, scale):
        return jax.random.normal(k, shape, f32) * scale

    def gain(k, shape):
        return 1.0 + 0.01 * jax.random.normal(k, shape, f32)

    L_ = DEPTH
    return {
        "x": jax.random.normal(ks[0], (BATCH, SEQ, D_MODEL), f32),
        "ffn1_w1": nrm(ks[1], (L_, D_MODEL, D_FF_2), D_MODEL ** -0.5),
        "ffn1_w3": nrm(ks[2], (L_, D_MODEL, D_FF_2), D_MODEL ** -0.5),
        "ffn1_w2": nrm(ks[3], (L_, D_FF_2, D_MODEL), DEEPNORM_BETA * D_FF_2 ** -0.5),
        "ln1_g": gain(ks[4], (L_, D_MODEL)),
        "ln1_b": nrm(ks[5], (L_, D_MODEL), 0.01),
        "w_in": nrm(ks[6], (L_, D_MODEL, IN_COLS), D_MODEL ** -0.5),
        "kv_norm_g": gain(ks[7], (L_, KV_LATENT)),
        "w_uk": nrm(ks[8], (L_, N_ATT_HEADS, KV_LATENT, ATT_HEAD_DIM), KV_LATENT ** -0.5),
        "w_uv": nrm(ks[9], (L_, N_ATT_HEADS, KV_LATENT, ATT_HEAD_DIM), DEEPNORM_BETA * KV_LATENT ** -0.5),
        "gmlp_ln_g": gain(ks[10], (L_, MLP_WIDTH)),
        "gmlp_ln_b": nrm(ks[11], (L_, MLP_WIDTH), 0.01),
        "gmlp_ws": nrm(ks[12], (L_, N_MLP_GROUPS, CHUNK, CHUNK), 0.5 * CHUNK ** -0.5),
        "gmlp_bs": gain(ks[13], (L_, N_MLP_GROUPS, CHUNK)),
        "w_out": nrm(ks[14], (L_, MIX_WIDTH, D_MODEL), DEEPNORM_BETA * MIX_WIDTH ** -0.5),
        "ln2_g": gain(ks[15], (L_, D_MODEL)),
        "ln2_b": nrm(ks[16], (L_, D_MODEL), 0.01),
        "ffn2_w1": nrm(ks[17], (L_, D_MODEL, D_FF_2), D_MODEL ** -0.5),
        "ffn2_w3": nrm(ks[18], (L_, D_MODEL, D_FF_2), D_MODEL ** -0.5),
        "ffn2_w2": nrm(ks[19], (L_, D_FF_2, D_MODEL), DEEPNORM_BETA * D_FF_2 ** -0.5),
        "ln3_g": gain(ks[20], (L_, D_MODEL)),
        "ln3_b": nrm(ks[21], (L_, D_MODEL), 0.01),
    }

def second_block(x, ffn1_w1, ffn1_w3, ffn1_w2, ln1_g, ln1_b, w_in, kv_norm_g, w_uk, w_uv,
              gmlp_ln_g, gmlp_ln_b, gmlp_ws, gmlp_bs, w_out, ln2_g, ln2_b,
              ffn2_w1, ffn2_w3, ffn2_w2, ln3_g, ln3_b):
    L = x.shape[1]
    topk = min(TOPK_MAX, L // 4)
    for l in range(DEPTH):
        x = _layernorm(DEEPNORM_ALPHA * x + 0.5 * _swiglu(x, ffn1_w1[l], ffn1_w3[l], ffn1_w2[l]),
                       ln1_g[l], ln1_b[l])
        m = _mixer(x, w_in[l], kv_norm_g[l], w_uk[l], w_uv[l], gmlp_ln_g[l], gmlp_ln_b[l],
                   gmlp_ws[l], gmlp_bs[l], w_out[l], topk)
        x = _layernorm(DEEPNORM_ALPHA * x + m, ln2_g[l], ln2_b[l])
        x = _layernorm(DEEPNORM_ALPHA * x + 0.5 * _swiglu(x, ffn2_w1[l], ffn2_w3[l], ffn2_w2[l]),
                       ln3_g[l], ln3_b[l])
    return x


_first_inputs = second_inputs


def second_inputs(seed=0):
    import zlib

    import numpy as np

    out = dict(_first_inputs(seed))
    spreads = {}
    factors = {'ln1_g': 5.562,
     'ln1_b': 5.116,
     'kv_norm_g': 47.356,
     'gmlp_ln_g': 64.0,
     'gmlp_ln_b': 64.0,
     'gmlp_bs': 44.023,
     'ln2_g': 26.398,
     'ln2_b': 25.997,
     'ln3_g': 35.149,
     'ln3_b': 32.42}
    for name, (base, spread) in spreads.items():
        noise = np.random.default_rng([zlib.crc32(name.encode()), seed]).standard_normal(out[name].shape)
        drawn = base * np.exp(spread * noise) if base else spread * noise
        out[name] = __import__('jax').numpy.asarray(drawn.astype(out[name].dtype))
    for name, factor in factors.items():
        out[name] = (out[name] * factor).astype(out[name].dtype)
    return out


_narrow_inputs = second_inputs


def second_inputs(seed=0):

    out = dict(_narrow_inputs(seed))
    wider = {'gmlp_ln_g': 9.99,
     'gmlp_ln_b': 10.02,
     'gmlp_bs': 5.24,
     'ln2_g': 4.62,
     'ln2_b': 4.68,
     'ln3_g': 6.66,
     'ln3_b': 6.7}
    for name, times in wider.items():
        mean = out[name].mean()
        out[name] = (mean + times * (out[name] - mean)).astype(out[name].dtype)
    return out


def setup_inputs(seed=0):
    out = dict(first_inputs(seed))
    for name, value in second_inputs(seed + 1).items():
        if name != "x":
            out[name + "_2"] = value
    return out


def reference(
    x, c, w_ada, b_ada, g_pre_mix, g_post_mix, g_pre_ffn, g_post_ffn, w_in, lam_re, lam_im,
    log_dt, b_re, b_im, c_re, c_im, d_skip, w_glu, w_fft, sink, w_out, w_up, conv_w, conv_b,
    w_down, ffn1_w1_2, ffn1_w3_2, ffn1_w2_2, ln1_g_2, ln1_b_2, w_in_2, kv_norm_g_2, w_uk_2,
    w_uv_2, gmlp_ln_g_2, gmlp_ln_b_2, gmlp_ws_2, gmlp_bs_2, w_out_2, ln2_g_2, ln2_b_2,
    ffn2_w1_2, ffn2_w3_2, ffn2_w2_2, ln3_g_2, ln3_b_2,
):
    x = first_block(
        x, c, w_ada, b_ada, g_pre_mix, g_post_mix, g_pre_ffn, g_post_ffn, w_in, lam_re, lam_im,
        log_dt, b_re, b_im, c_re, c_im, d_skip, w_glu, w_fft, sink, w_out, w_up, conv_w, conv_b,
        w_down,
    )
    return second_block(
        x, ffn1_w1_2, ffn1_w3_2, ffn1_w2_2, ln1_g_2, ln1_b_2, w_in_2, kv_norm_g_2, w_uk_2,
        w_uv_2, gmlp_ln_g_2, gmlp_ln_b_2, gmlp_ws_2, gmlp_bs_2, w_out_2, ln2_g_2, ln2_b_2,
        ffn2_w1_2, ffn2_w3_2, ffn2_w2_2, ln3_g_2, ln3_b_2,
    )


_drawn_inputs = setup_inputs


def setup_inputs(seed=0):
    import zlib

    import numpy as np

    out = dict(_drawn_inputs(seed))
    spreads = {}
    factors = {'lam_re': 6.665, 'kv_norm_g_2': 2.704}
    for name, (base, spread) in spreads.items():
        noise = np.random.default_rng([zlib.crc32(name.encode()), seed]).standard_normal(out[name].shape)
        drawn = base * np.exp(spread * noise) if base else spread * noise
        out[name] = __import__('jax').numpy.asarray(drawn.astype(out[name].dtype))
    for name, factor in factors.items():
        out[name] = (out[name] * factor).astype(out[name].dtype)
    return out
```

```python
from contextlib import ExitStack
import math

import numpy as np

import concourse.bass as bass
from concourse import mybir

F32 = mybir.dt.float32
F32R = mybir.dt.float32r
ACT = mybir.ActivationFunctionType
ALU = mybir.AluOpType
AX_X = mybir.AxisListType.X

P = 128
SEQ = 1024
D = 1024
KD = D // P
NT = SEQ // P
HALF = 512
D_FF = 2816
NF = D_FF // P
SSM_W, FFT_W, ATT_W = 384, 256, 384
HEAD = 64
GROUPS, STATE, GC = 24, 64, 16
PAIRS = GROUPS // 2
CH = 8
NCH = SEQ // CH
Q_HEADS, KV_HEADS = 6, 2
SPAN = 3 * P
RMS_EPS, LN_EPS = 1e-6, 1e-5
NEG = -1e30
TWO_PI_HI = 6.28125
TWO_PI_LO = 2 * math.pi - TWO_PI_HI
ROUND = 1.5 * 2 ** 23
PI_DOWN = 3.1415925
LN2_HI = 0.693359375
LN2_LO = math.log(2) - LN2_HI
I32 = mybir.dt.int32


class Steps:

    def __init__(self, engine, sem):
        self.engine, self.sem, self.n = engine, sem, 0

    def add(self, ins):
        ins.then_inc(self.sem, 1)
        self.n += 1

    def settle(self):
        self.engine.wait_ge(self.sem, self.n)


def build(nc, a, out):
    with ExitStack() as ctx:
        body(ctx, nc, a, out)


def body(ctx, nc, a, out):
    sems = {}

    def sem(name):
        if name not in sems:
            sems[name] = ctx.enter_context(nc.semaphore(name))
        return sems[name]

    KB = 1024
    CONST = (nc.sbuf_base + 63) // 64 * 64
    XR = CONST + 12096
    GR = XR + 64 * KB
    RR = GR + 88 * KB
    at = {"next": CONST}

    def place(name, shape, offset, dt=F32):
        return nc.alloc_sbuf_tensor_at(name, shape, dt, offset=offset)

    def const(name, shape):
        n = 4 * int(np.prod(shape[1:]))
        t = place(name, shape, at["next"])
        at["next"] += (n + 31) // 32 * 32
        assert at["next"] <= XR
        return t

    psum = ctx.enter_context(nc.psum_tensor("psum", [P, 8 * HALF], F32))

    def bank(b, n=HALF, at=0):
        return psum[:, b * HALF + at:b * HALF + at + n]

    ident = const("ident", [P, P])
    row_a = const("row_a", [P, D])
    row_b = const("row_b", [P, D])
    conv_cols = const("conv_cols", [P, NF, 2, 4])
    norm_cols = const("norm_cols", [P, 2, KD])
    mod_cols = const("mod_cols", [P, 4, KD])
    stat_a = const("stat_a", [P, 2 * NT])
    stat_b = const("stat_b", [P, 2 * NT])
    stat_c = const("stat_c", [P, 2 * NT])
    sink_row = const("sink_row", [P, Q_HEADS])
    ones_row = const("ones_row", [1, P])
    dskip_cols = const("dskip_cols", [GC, GROUPS])
    c_cols = const("c_cols", [P, KD])
    log_dt_rows = const("log_dt_rows", [GROUPS, 2])

    x_rows = place("x_rows", [P, NT, D], GR)
    junk = place("junk", [P, D], GR + 32 * KB)
    junk2 = place("junk2", [P, P], GR + 39 * KB + 512)
    c_plain = place("c_plain", [P, 2, PAIRS, GC], GR + 36 * KB)
    ada_w = [place(f"ada_w{i}", [P, KD, HALF], XR + 16 * KB * i) for i in range(2)]
    c_bcast = place("c_bcast", [P, KD, P], RR + 40 * KB)
    ada_b = [place(f"ada_b{i}", [1, HALF], XR + 56 * KB + 2 * KB * i) for i in range(2)]
    vec_rows = [place(f"vec_rows{i}", [P, P], RR + 512 * i) for i in range(2)]
    lam_rows = place("lam_rows", [GROUPS, 3, P], RR + KB)
    dskip_rows = place("dskip_rows", [GROUPS, GC], RR + 2 * KB + 512)
    b_raw = place("b_raw", [P, 2, 2, PAIRS, GC], RR + 28 * KB)
    c_rows = place("c_rows", [P, 2, 3, 2, STATE], RR + 31 * KB)
    w_tmp = place("w_tmp", [P, 2, 4, PAIRS, GC], RR + 34 * KB)
    e_tmp = place("e_tmp", [P, 4, PAIRS, GC], RR + 4 * KB)
    c_pad = place("c_pad", [P, 2, PAIRS, 2, GC], XR + 60 * KB)
    lam_b = place("lam_b", [P, 2, 2, PAIRS, CH, GC], XR + 32 * KB)
    k_sum = place("k_sum", [P, 2, GROUPS * GC], RR + 7 * KB)
    k_shift = place("k_shift", [P, GROUPS * GC], RR + 10 * KB)
    prm = place("prm", [P, 26, 2 * PAIRS], RR + 12 * KB)
    prm_int = place("prm_int", [P, 2 * PAIRS], RR + 15 * KB + 896, I32)
    pw = place("pw", [P, 2, 7, 2 * PAIRS], RR + 14 * KB + 512)
    toep = place("toep", [P, CH, GROUPS * GC], RR + 16 * KB)
    carry_out = place("carry_out", [P, 2, 2, PAIRS, CH, GC], GR + 40 * KB)
    state_in = place("state_in", [P, 2, 2, PAIRS, P], GR + 64 * KB)
    h_t = place("h_t", [P, KD, SEQ], XR)
    win_raw = [place(f"win_raw{i}", [P, KD, P], RR + 4 * KB * i) for i in range(3)]
    u_t = place("u_t", [P, 3, SEQ], GR)
    f_t = place("f_t", [P, 2, SEQ], GR + 12 * KB)
    q_t = place("q_t", [P, 3, SEQ], GR + 20 * KB)
    k_t = place("k_t", [P, SEQ], GR + 32 * KB)
    v_t = place("v_t", [P, SEQ], GR + 36 * KB)
    toep_dram = nc.dram_tensor("toep_dram", (2 * CH - 1, GC, GROUPS * GC), F32).ap()

    ident_in, small_in, x_in, bc_in, ssm_in = (sem(n) for n in ("ident_in", "small_in", "x_in", "bc_in", "ssm_in"))
    vec_in = sem("vec_in")
    ada_in = [sem(f"ada_in{i}") for i in range(2)]
    c_spread, dt_spread, ada_mm, ada_used = (sem(n) for n in ("c_spread", "dt_spread", "ada_mm", "ada_used"))
    rows_turned, vec_used = sem("rows_turned"), sem("vec_used")
    lam_turned, c_turned, c_ready = sem("lam_turned"), sem("c_turned"), sem("c_ready")
    prm_angle, prm_trig, prm_lam = (sem(n) for n in ("prm_angle", "prm_trig", "prm_lam"))
    lam_b_ready, win_turned, win_ready, k_mm, k_ready = (sem(n) for n in ("lam_b_ready", "win_turned", "win_ready", "k_mm", "k_ready"))
    carry_ready, k_shift_in, k_low, k_in_dram, toep_in = (sem(n) for n in ("carry_ready", "k_shift_in", "k_low", "k_in_dram", "toep_in"))
    x_sq, x_var, x_std, x_scaled, x_turned, h_ready = (sem(n) for n in ("x_sq", "x_var", "x_std", "x_scaled", "x_turned", "h_ready"))
    win_in = [sem(f"win_in{i}") for i in range(3)]
    win_mm, z_ready = sem("win_mm"), sem("z_ready")
    dve_steps, pool_steps, act_steps = sem("dve_steps"), sem("pool_steps"), sem("act_steps")
    mod_ready = sem("mod_ready")

    f0, q0, k0 = SSM_W, SSM_W + FFT_W, SSM_W + FFT_W + ATT_W
    v0 = k0 + P
    win_units = [([(f0 + P * i, P)], f_t[:, i, :]) for i in range(2)]
    win_units += [([(P * i, P)], u_t[:, i, :]) for i in range(3)]
    win_units += [([(q0 + HEAD * j, HEAD), (q0 + HEAD * (j + 3), HEAD)], q_t[:, j, :]) for j in range(3)]
    win_units += [([(k0, P)], k_t[:, :]), ([(v0, P)], v_t[:, :])]
    win_counts, landed = [], [0, 0, 0]
    for n, (cols, _) in enumerate(win_units):
        landed[n % 3] += 16 * len(cols)
        win_counts.append(landed[n % 3])

    fw_rows = place("fw_rows", [P, 2, P], RR + 40 * KB)
    dft_d = place("dft_d", [P, 2, P], RR + 41 * KB)
    fw = place("fw", [P, 2, 2, P], RR + 42 * KB)
    f_mixed = place("f_mixed", [P, NT, 2, 2, P], XR + 32 * KB)
    dft_w = [place(f"dft_w{i}", [P, SEQ], XR + 48 * KB + 4 * KB * i) for i in range(4)]
    u_rows = place("u_rows", [P, GROUPS, CH, GC], RR)
    turn = place("turn", [P, 2, PAIRS, NCH], RR)
    u_chunk = place("u_chunk", [P, GROUPS, NCH], RR + 28 * KB)
    carry = place("carry", [P, 2, 2, PAIRS, NCH + 1], XR + 32 * KB)
    rot = [place(f"rot{i}", [P, 3, NCH], XR + 56 * KB + 512 + 1536 * i) for i in range(4)]
    rot.append(place("rot4", [P, 3, NCH], GR + 17 * KB + 512))
    y_rows = place("y_rows", [P, CH, GROUPS * GC], GR + 64 * KB)
    w_glu = place("w_glu", [P, 3, SSM_W], GR + 76 * KB)
    glu_tmp = [place(f"glu_tmp{i}", [P, HALF], GR + 82 * KB + 2 * KB * i) for i in range(2)]
    y_act = place("y_act", [P, 3, NCH, CH], RR)
    yc_t = place("yc_t", [P, KD, SEQ], XR)
    att_bias = place("att_bias", [P, Q_HEADS, SPAN], GR)
    v_rows = place("v_rows", [P, NT, P], GR + 9 * KB + 4608)
    probs = [place(f"probs{i}", [P, SPAN], GR + 9 * KB + 1536 * i) for i in range(3)]
    probs_t = [place(f"probs_t{i}", [P, SPAN], RR + 40 * KB + 1536 * i) for i in range(2)]
    att_max = place("att_max", [P, NT * Q_HEADS], RR + 43 * KB)
    att_sum = place("att_sum", [P, NT * Q_HEADS], RR + 43 * KB + 192)
    att_sink = place("att_sink", [P, NT * Q_HEADS], RR + 43 * KB + 384)

    fw_zero, fw_in, fw_mm, fw_ready = (sem(n) for n in ("fw_zero", "fw_in", "fw_mm", "fw_ready"))
    fm_mm, fm_ready, dft_mm, yf_mm, yf_ready = (sem(n) for n in ("fm_mm", "fm_ready", "dft_mm", "yf_mm", "yf_ready"))
    dft_in = [sem(f"dft_in{i}") for i in range(4)]
    u_turned, u_rows_ready, uc_turned, uc_ready = (sem(n) for n in ("u_turned", "u_rows_ready", "uc_turned", "uc_ready"))
    v_turned, v_ready, bias_in, glu_in = (sem(n) for n in ("v_turned", "v_ready", "bias_in", "glu_in"))
    states_mm, states_used, carry_done = (sem(n) for n in ("states_mm", "states_used", "carry_done"))
    scores_mm, max_ready, exp_ready, sink_ready, probs_ready = (sem(n) for n in ("scores_mm", "max_ready", "exp_ready", "sink_ready", "probs_ready"))
    probs_turned, probs_t_ready, att_mm, att_ready = (sem(n) for n in ("probs_turned", "probs_t_ready", "att_mm", "att_ready"))
    y_mm, y_rows_ready, y_turned, y_act_ready, glu_mm, glu_sig, glu_ready = (
        sem(n) for n in ("y_mm", "y_rows_ready", "y_turned", "y_act_ready", "glu_mm", "glu_sig", "glu_ready"))

    Z_F, Z_U, Z_Q, Z_ALL = 2, 5, 8, 10
    ITEMS = NT * Q_HEADS

    def item(i):
        n, h = i // Q_HEADS, i % Q_HEADS
        return n, h, h // 3, h % 3, range(max(n - 1, 0), min(n + 2, NT))

    def mix_sync(sp):
        sp.wait_ge(fw_zero, 1)
        for h in range(4):
            rows = slice(HEAD * (h % 2), HEAD * (h % 2 + 1))
            sp.dma_start(fw_rows[rows, h // 2, rows], a["w_fft"][0, h]).then_inc(fw_in, 16)
        sp.dma_start(dft_d[:], a["dft_d"]).then_inc(fw_in, 16)
        sp.wait_ge(win_turned, 12)
        for i in range(2 * NT):
            if i >= 4:
                sp.wait_ge(dft_mm, i - 3)
            sp.dma_start(dft_w[i % 4][:], a["dft"][P * (i // 2):P * (i // 2 + 1), i % 2, :]).then_inc(dft_in[i % 4], 16)
        sp.wait_ge(u_turned, 6)
        sp.dma_start(att_bias[:], a["att_bias"]).then_inc(bias_in, 16)
        sp.wait_ge(states_mm, NT)
        sp.dma_start(w_glu[:], a["w_glu"][0].rearrange("(k p) n -> p k n", p=P)).then_inc(glu_in, 16)
        blocks_sync(sp)

    def mix_tensor(pe, t):
        pe.wait_ge(fw_in, 16 * 5)
        pe.wait_ge(z_ready, Z_ALL)
        for pair in range(2):
            for cs in range(2):
                ins = t.matmul(bank(2, P, P * (2 * pair + cs)), dft_d[:, cs, :], fw_rows[:, pair, :], start=True, stop=True)
        ins.then_inc(fw_mm, 1)
        pe.wait_ge(fw_ready, 1)
        for n in range(NT):
            if n >= 2:
                pe.wait_ge(fm_ready, n - 1)
            for pair in range(2):
                ins = t.matmul(bank(4 + n % 2, 2 * P, 2 * P * pair), f_t[:, pair, P * n:P * (n + 1)],
                               fw[:, pair].rearrange("p c e -> p (c e)"), start=True, stop=True)
            ins.then_inc(fm_mm, 1)
        for i in range(6):
            b, sq = i // 2, i % 2
            if i >= 2:
                pe.wait_ge(u_rows_ready, i - 1)
            for s in range(4):
                ins = t.transpose(bank(6 + i % 2, P, P * s), u_t[:, b].rearrange("p (j s) -> p s j", s=CH)[:, 4 * sq + s, :], ident[:])
            ins.then_inc(u_turned, 1)
        pe.wait_ge(fm_ready, NT)
        for i in range(2 * NT):
            n, cs = i // 2, i % 2
            pe.wait_ge(dft_in[i % 4], 16 * (i // 4 + 1))
            for pair in range(2):
                for half in range(2):
                    ins = t.matmul(bank(2 * pair + half), f_mixed[:, n, pair, cs, :], dft_w[i % 4][:, HALF * half:HALF * (half + 1)],
                                   start=(i == 0), stop=(i == 2 * NT - 1))
            ins.then_inc(dft_mm, 1)
        pe.wait_ge(u_rows_ready, 6)
        for i in range(6):
            if i >= 2:
                pe.wait_ge(uc_ready, i - 1)
            for g in range(4):
                ins = t.transpose(bank(6 + i % 2, P, P * g), u_rows[:, 4 * i + g].rearrange("p s c -> p (s c)"), ident[:])
            ins.then_inc(uc_turned, 1)
        for i in range(2):
            for n in range(4):
                ins = t.transpose(bank(4 + i, P, P * n), v_t[:, P * (4 * i + n):P * (4 * i + n + 1)], ident[:])
            ins.then_inc(v_turned, 1)
        pe.wait_ge(yf_ready, 4)
        pe.wait_ge(v_ready, 2)
        pe.wait_ge(uc_ready, 6)

        def states(c):
            d, q3 = c // 4, 3 * (c % 4)
            if c >= 1:
                pe.wait_ge(states_used, c)
            for q in range(3):
                for ri in range(2):
                    for e in range(2):
                        half = slice(STATE * e, STATE * (e + 1))
                        ins = t.matmul(bank(5 + ri, NCH, NCH * q)[half], state_in[:, ri, d, q3 + q, half],
                                       u_chunk[:, 2 * (q3 + q) + e, :], start=True, stop=True)
            ins.then_inc(states_mm, 1)

        def scores(i):
            n, h, e, j, keys = item(i)
            if i >= 2:
                pe.wait_ge(max_ready, i - 1)
            rows = slice(HEAD * e, HEAD * (e + 1))
            t.matmul(bank(i % 2, P * len(keys)), q_t[rows, j, P * n:P * (n + 1)], k_t[rows, P * keys[0]:P * (keys[-1] + 1)],
                     start=True, stop=True).then_inc(scores_mm, 1)

        def turn_probs(i):
            n, h, e, j, keys = item(i)
            pe.wait_ge(probs_ready, i + 1)
            if i >= 2:
                pe.wait_ge(probs_t_ready, i - 1)
            for b in range(len(keys)):
                ins = t.transpose(bank(2 + i % 2, P, P * b), probs[i % 3][:, P * b:P * (b + 1)], ident[:])
            ins.then_inc(probs_turned, 1)

        def values(i):
            n, h, e, j, keys = item(i)
            pe.wait_ge(probs_t_ready, i + 1)
            if h == 0 and n:
                pe.wait_ge(att_ready, n)
            rows = slice(HEAD * (h % 2), HEAD * (h % 2 + 1))
            for b, key in enumerate(keys):
                ins = t.matmul(bank(4, P, P * (h // 2))[rows], v_rows[:, key, HEAD * e:HEAD * (e + 1)],
                               probs_t[i % 2][:, P * b:P * (b + 1)], start=(b == 0), stop=(b == len(keys) - 1))
            ins.then_inc(att_mm, 1)

        for i in range(ITEMS + 3):
            if i < ITEMS:
                if i % Q_HEADS == 0:
                    states(i // Q_HEADS)
                scores(i)
            if 2 <= i < ITEMS + 2:
                turn_probs(i - 2)
            if i >= 3:
                values(i - 3)
        pe.wait_ge(carry_done, NT)
        pe.wait_ge(toep_in, 16 * CH)
        for i in range(3):
            for e in range(2):
                b = 5 + e if i % 2 == 0 else (7 if e == 0 else 0)
                half = slice(STATE * e, STATE * (e + 1))
                if i == 2:
                    pe.wait_ge(y_rows_ready, e + 1)
                for q in range(4):
                    pair = 4 * i + q
                    g = 2 * pair + e
                    dst = bank(b, P, P * q)
                    t.matmul(dst, u_chunk[:, g, :], toep[:, :, GC * g:GC * (g + 1)], start=True, stop=False)
                    for d in range(2):
                        for ri in range(2):
                            ins = t.matmul(dst, carry[half, d, ri, pair, d:d + NCH],
                                           carry_out[half, d, ri, pair].rearrange("p t c -> p (t c)"),
                                           start=False, stop=(d == 1 and ri == 1))
                ins.then_inc(y_mm, 1)
        pe.wait_ge(y_rows_ready, 6)
        for i in range(6):
            tq, b = i // 3, i % 3
            if i >= 2:
                pe.wait_ge(y_act_ready, i - 1)
            for n in range(4):
                ins = t.transpose(bank(1 + i % 2, P, P * n), y_rows[:, 4 * tq + n, P * b:P * (b + 1)], ident[:])
            ins.then_inc(y_turned, 1)
        pe.wait_ge(y_act_ready, 6)
        pe.wait_ge(glu_in, 16)
        for i in range(6):
            b, half = i // 2, i % 2
            if i >= 2:
                pe.wait_ge(glu_sig, i - 1)
            for k in range(3):
                ins = t.matmul(bank(3 + i % 2), w_glu[:, k, P * b:P * (b + 1)],
                               y_act[:, k].rearrange("p j s -> p (j s)")[:, HALF * half:HALF * (half + 1)],
                               start=(k == 0), stop=(k == 2))
            ins.then_inc(glu_mm, 1)
        blocks_tensor(pe, t)

    def mix_scalar(act, steps):
        s = nc.scalar
        act.wait_ge(fw_mm, 1)
        s.copy(fw[:].rearrange("p a c e -> p (a c e)"), bank(2)).then_inc(fw_ready, 1)
        for n in range(NT):
            act.wait_ge(fm_mm, n + 1)
            s.copy(f_mixed[:, n].rearrange("p a c e -> p (a c e)"), bank(4 + n % 2)).then_inc(fm_ready, 1)
        for i in range(6):
            act.wait_ge(uc_turned, i + 1)
            s.copy(u_chunk[:, 4 * i:4 * i + 4, :], bank(6 + i % 2).rearrange("p (g j) -> p g j", g=4)).then_inc(uc_ready, 1)
        for i in range(2):
            act.wait_ge(v_turned, i + 1)
            s.copy(v_rows[:, 4 * i:4 * i + 4, :], bank(4 + i).rearrange("p (n c) -> p n c", n=4)).then_inc(v_ready, 1)
        act.wait_ge(dft_mm, 2 * NT)
        for i in range(4):
            s.copy(yc_t[:, 3 + i // 2, HALF * (i % 2):HALF * (i % 2 + 1)], bank(i)).then_inc(yf_ready, 1)

        def exponentials(i):
            n, h, e, j, keys = item(i)
            act.wait_ge(max_ready, i + 1)
            p = probs[i % 3][:, 0:P * len(keys)]
            s.activation(p, p, ACT.Exp, bias=att_max[:, i:i + 1], accum_out=att_sum[:, i:i + 1]).then_inc(exp_ready, 1)
            s.activation(att_sink[:, i:i + 1], sink_row[:, h:h + 1], ACT.Exp, bias=att_max[:, i:i + 1]).then_inc(sink_ready, 1)

        def copy_probs(i):
            n, h, e, j, keys = item(i)
            act.wait_ge(probs_turned, i + 1)
            if i >= 2:
                act.wait_ge(att_mm, i - 1)
            s.copy(probs_t[i % 2][:, 0:P * len(keys)], bank(2 + i % 2, P * len(keys))).then_inc(probs_t_ready, 1)
            if h == Q_HEADS - 1:
                pass

        for i in range(ITEMS + 4):
            if i < ITEMS:
                exponentials(i)
            if 2 <= i < ITEMS + 2:
                copy_probs(i - 2)
            if i >= 4 and (i - 4) % Q_HEADS == Q_HEADS - 1:
                n = (i - 4) // Q_HEADS
                act.wait_ge(att_mm, Q_HEADS * (n + 1))
                s.copy(yc_t[:, 5:8, P * n:P * (n + 1)], bank(4, 3 * P).rearrange("p (c q) -> p c q", c=3)).then_inc(att_ready, 1)
        for i in range(3):
            for e in range(2):
                b = 5 + e if i % 2 == 0 else (7 if e == 0 else 0)
                act.wait_ge(y_mm, 2 * i + e + 1)
                dst = y_rows[:].rearrange("p t (q e c) -> p q e t c", e=2, c=GC)
                for q in range(4):
                    ins = s.copy(dst[:, 4 * i + q, e], bank(b, P, P * q).rearrange("p (t c) -> p t c", t=CH))
                ins.then_inc(y_rows_ready, 1)
        for i in range(6):
            tq, b = i // 3, i % 3
            act.wait_ge(y_turned, i + 1)
            s.activation(y_act[:, b].rearrange("p j s -> p s j")[:, 4 * tq:4 * tq + 4, :],
                         bank(1 + i % 2).rearrange("p (s j) -> p s j", s=4), ACT.Gelu_apprx_tanh).then_inc(y_act_ready, 1)
        for i in range(6):
            act.wait_ge(glu_mm, i + 1)
            if i >= 2:
                act.wait_ge(glu_ready, i - 1)
            s.activation(glu_tmp[i % 2][:], bank(3 + i % 2), ACT.Sigmoid).then_inc(glu_sig, 1)
        blocks_scalar(act, steps)

    def mix_vector(dve, v, steps):
        steps.add(v.memset(fw_rows[:], 0.0))
        steps.settle()
        dve.sem_inc(fw_zero, 1)
        for i in range(6):
            b, sq = i // 2, i % 2
            dve.wait_ge(u_turned, i + 1)
            v.tensor_copy(u_rows[:, 8 * b:8 * b + 8, 4 * sq:4 * sq + 4, :].rearrange("p g s c -> p s g c"),
                          bank(6 + i % 2).rearrange("p (s g c) -> p s g c", s=4, g=8)).then_inc(u_rows_ready, 1)

        def turns(d):
            tr, ti = turn[:, 0], turn[:, 1]
            steps.add(v.memset(tr[:, :, 0:1], 1.0))
            steps.add(v.memset(ti[:, :, 0:1], 0.0))
            steps.settle()
            for m in range(7):
                w = 1 << m
                pr, pi = (pw[:, x, m, PAIRS * d:PAIRS * (d + 1)].unsqueeze(2).to_broadcast([P, PAIRS, w]) for x in range(2))
                halves = [r[:].rearrange("p a b -> p (a b)")[:, 0:0 + 3 * NCH] for r in rot]
                done = 0
                step = min(PAIRS, 3 * NCH // w)
                for q in range(0, PAIRS, step):
                    qs = slice(q, q + step)
                    tmp = [x[:, 0:step * w].rearrange("p (a b) -> p a b", a=step) for x in halves[:4]]
                    br, bi = pr[:, qs], pi[:, qs]
                    steps.add(v.tensor_tensor(tmp[0], tr[:, qs, 0:w], br, ALU.mult))
                    steps.add(v.tensor_tensor(tmp[1], ti[:, qs, 0:w], bi, ALU.mult))
                    steps.add(v.tensor_tensor(tmp[2], tr[:, qs, 0:w], bi, ALU.mult))
                    steps.add(v.tensor_tensor(tmp[3], ti[:, qs, 0:w], br, ALU.mult))
                    steps.settle()
                    steps.add(v.tensor_tensor(tr[:, qs, w:2 * w], tmp[0], tmp[1], ALU.subtract))
                    steps.add(v.tensor_tensor(ti[:, qs, w:2 * w], tmp[2], tmp[3], ALU.add))
                    steps.settle()

        def scan(c):
            d, q3 = c // 4, 3 * (c % 4)
            sr, si = (bank(5 + x, 3 * NCH).rearrange("p (q j) -> p q j", q=3) for x in range(2))
            tr, ti = turn[:, 0, q3:q3 + 3], turn[:, 1, q3:q3 + 3]
            back, forth = (ALU.add, ALU.subtract) if d == 0 else (ALU.subtract, ALU.add)
            dve.wait_ge(states_mm, c + 1)
            steps.add(v.tensor_tensor(rot[0][:], sr, tr, ALU.mult))
            steps.add(v.tensor_tensor(rot[1][:], si, ti, ALU.mult))
            steps.add(v.tensor_tensor(rot[2][:], si, tr, ALU.mult))
            steps.add(v.tensor_tensor(rot[3][:], sr, ti, ALU.mult))
            steps.settle()
            dve.sem_inc(states_used, 1)
            steps.add(v.tensor_tensor(rot[0][:], rot[0][:], rot[1][:], back))
            steps.add(v.tensor_tensor(rot[2][:], rot[2][:], rot[3][:], forth))
            steps.settle()
            for q in range(3):
                decay = prm[:, 9, PAIRS * d + q3 + q:PAIRS * d + q3 + q + 1].to_broadcast([P, NCH])
                for x in (0, 2):
                    src, dst = rot[x][:, q, :], rot[x + 1][:, q, :]
                    if d:
                        src, dst = src[:, ::-1], dst[:, ::-1]
                    steps.add(v.tensor_tensor_scan(dst, decay, src, 0.0, ALU.mult, ALU.add))
            steps.settle()
            steps.add(v.tensor_tensor(rot[0][:], rot[1][:], tr, ALU.mult))
            steps.add(v.tensor_tensor(rot[2][:], rot[1][:], ti, ALU.mult))
            steps.add(v.tensor_tensor(rot[4][:], rot[3][:], ti, ALU.mult))
            steps.settle()
            steps.add(v.tensor_tensor(rot[1][:], rot[3][:], tr, ALU.mult))
            dst = [carry[:, d, x, q3:q3 + 3, 1 - d:1 - d + NCH] for x in range(2)]
            steps.add(v.tensor_tensor(dst[0], rot[0][:], rot[4][:], forth))
            steps.settle()
            steps.add(v.tensor_tensor(dst[1], rot[1][:], rot[2][:], back))
            steps.settle()
            dve.sem_inc(carry_done, 1)

        def maximum(i):
            n, h, e, j, keys = item(i)
            dve.wait_ge(scores_mm, i + 1)
            if i >= 3:
                dve.wait_ge(probs_turned, i - 2)
            w = P * len(keys)
            at = P if n == 0 else 0
            steps.add(v.tensor_tensor_reduce(probs[i % 3][:, 0:w], bank(i % 2, w), att_bias[:, h, at:at + w], 1.0 / 8, NEG,
                                             ALU.add, ALU.max, att_max[:, i:i + 1]))
            steps.settle()
            v.tensor_scalar(att_max[:, i:i + 1], att_max[:, i:i + 1], sink_row[:, h:h + 1], -1.0, ALU.max, ALU.mult).then_inc(max_ready, 1)

        def normalise(i):
            n, h, e, j, keys = item(i)
            dve.wait_ge(exp_ready, i + 1)
            dve.wait_ge(sink_ready, i + 1)
            one = slice(i, i + 1)
            steps.add(v.tensor_tensor(att_sum[:, one], att_sum[:, one], att_sink[:, one], ALU.add))
            steps.settle()
            steps.add(v.reciprocal(att_sum[:, one], att_sum[:, one]))
            steps.settle()
            p = probs[i % 3][:, 0:P * len(keys)]
            v.tensor_scalar(p, p, att_sum[:, one], None, ALU.mult).then_inc(probs_ready, 1)

        dve.wait_ge(uc_turned, 6)
        dve.wait_ge(yf_ready, 4)
        steps.add(v.memset(carry[:, 0, :, :, 0:1], 0.0))
        steps.add(v.memset(carry[:, 1, :, :, NCH:NCH + 1], 0.0))
        turns(0)
        dve.wait_ge(bias_in, 16)
        for i in range(ITEMS + 1):
            if i < ITEMS:
                maximum(i)
            if i:
                normalise(i - 1)
            if i % Q_HEADS == Q_HEADS - 1:
                if i // Q_HEADS == 4:
                    turns(1)
                scan(i // Q_HEADS)
        for i in range(6):
            b, half = i // 2, i % 2
            dve.wait_ge(glu_sig, i + 1)
            v.tensor_tensor(yc_t[:, b, HALF * half:HALF * (half + 1)],
                            y_act[:, b].rearrange("p j s -> p (j s)")[:, HALF * half:HALF * (half + 1)],
                            glu_tmp[i % 2][:], ALU.mult).then_inc(glu_ready, 1)
        blocks_vector(dve, v, steps)

    def mix_gpsimd(pool, steps):
        blocks_gpsimd(pool, steps)

    x_hi = place("x_hi", [P, KD, SEQ], XR, F32R)
    x_lo = place("x_lo", [P, KD, SEQ], XR + 32 * KB, F32R)
    up_raw = [place(f"up_raw{i}", [P, KD, P], RR + 4 * KB * i) for i in range(2)]
    split_hi = [place(f"split_hi{i}", [P, SEQ], RR + 8 * KB + 8 * KB * i, F32R) for i in range(2)]
    split_lo = [place(f"split_lo{i}", [P, SEQ], RR + 12 * KB + 8 * KB * i, F32R) for i in range(2)]
    down_raw = [place(f"down_raw{i}", [P, HALF], RR + 24 * KB + 2 * KB * i) for i in range(2)]
    down_hi = [place(f"down_hi{i}", [P, HALF], RR + 4 * KB * i, F32R) for i in range(2)]
    down_lo = [place(f"down_lo{i}", [P, HALF], RR + 2 * KB + 4 * KB * i, F32R) for i in range(2)]
    y_left = place("y_left", [P, NT, HALF], RR + 28 * KB)
    gate = [place(f"gate{i}", [P, SEQ], RR + 28 * KB + 4 * KB * i) for i in range(4)]
    hidden = place("hidden", [P, NF, SEQ], GR)
    res = place("res", [P, NT, D], GR)
    scaled = [place(f"scaled{i}", [P, D], RR + 8 * KB + 4 * KB * i) for i in range(4)]
    post_tmp = [place(f"post_tmp{i}", [P, HALF], RR + 2 * KB * i) for i in range(2)]
    split_tmp = [place(f"split_tmp{i}", [P, HALF], RR + 4 * KB + 2 * KB * i) for i in range(2)]
    sq_junk = place("sq_junk", [P, D], RR + 24 * KB)
    sq_two = place("sq_two", [P, D], RR + 28 * KB)
    conv_now = const("conv_now", [P, 2, 2, 4])
    moments = const("moments", [P, NT, 2, 6])
    mean_var = const("mean_var", [P, NT, 2])
    res_dram = [nc.dram_tensor(f"res_dram{i}", (SEQ, D), F32).ap() for i in range(4)]
    ALPHA = 2 ** 0.25

    MIX_STEPS = [3, 4, 5, 6, 7, 0, 1, 2]
    row_view = lambda ap: ap.rearrange("(n p) d -> p n d", p=P)
    tiles = lambda ap: ap.rearrange("(k p) (f c) -> f p k c", p=P, c=P)

    before = {"down": 0, "down_stages": 0, "up": 0, "act": 0}
    down_sems = {n: sem("down_" + n) for n in ("in0", "in1", "hi", "lo", "mm", "evac", "evac2")}
    up_sems = {n: sem("up_" + n) for n in ("in0", "in1", "hi", "lo", "mm", "act", "prod", "coef", "shift")}

    class Down:
        def __init__(self, kt, src, w):
            self.kt, self.src = kt, src
            self.w = w.rearrange("(k p) (h c) -> h k p c", p=P, h=2)
            self.order = MIX_STEPS if kt == KD else range(kt)
            self.landed = (down_sems["in0"], down_sems["in1"])
            self.hi, self.lo, self.mm = down_sems["hi"], down_sems["lo"], down_sems["mm"]
            self.evac, self.evac2 = down_sems["evac"], down_sems["evac2"]
            self.base, self.evacs = before["down"], NT // 2 * before["down_stages"]
            self.end = self.base + 2 * kt
            before["down"] = self.end
            before["down_stages"] += 1

    class Up:
        def __init__(self, w_gate, w_val, conv):
            self.w, self.conv = (w_gate, w_val), conv
            self.landed = (up_sems["in0"], up_sems["in1"])
            self.hi, self.lo, self.mm = up_sems["hi"], up_sems["lo"], up_sems["mm"]
            self.act, self.prod = up_sems["act"], up_sems["prod"]
            self.coef, self.shift = up_sems["coef"], up_sems["shift"]
            self.base, self.pairs, self.acts = before["up"], before["up"] // 2, before["act"]
            self.end, self.pairs_end = self.base + 2 * NF, self.pairs + NF
            before["up"] = self.end
            before["act"] += (3 if conv else 1) * NF

    down_mix = Down(KD, yc_t, a["w_out"][0])
    up_conv = Up(tiles(a["w_up"][0][:, 0:D_FF]), tiles(a["w_up"][0][:, D_FF:2 * D_FF]), True)
    down_conv = Down(NF, hidden, a["w_down"][0])
    up_1 = Up(tiles(a["ffn1_w1_2"][0]), tiles(a["ffn1_w3_2"][0]), False)
    down_1 = Down(NF, hidden, a["ffn1_w2_2"][0])
    down_mix2 = Down(KD, yc_t, a["w_out_2"][0])
    up_2 = Up(tiles(a["ffn2_w1_2"][0]), tiles(a["ffn2_w3_2"][0]), False)
    down_2 = Down(NF, hidden, a["ffn2_w2_2"][0])

    res_in, sq_done, var_ready, std_ready, row_ready = (sem(n) for n in ("res_in", "sq_done", "var_ready", "std_ready", "row_ready"))
    row_scaled, cols_turned, cols_tmp, cols_hi, cols_ready = (sem(n) for n in ("row_scaled", "cols_turned", "cols_tmp", "cols_hi", "cols_ready"))
    res_out, gain_in, row_centred, row_prep, row_gained = (sem(n) for n in ("res_out", "gain_in", "row_centred", "row_prep", "row_gained"))


    def down_steps(st, engine, step, between):
        for half in range(2):
            base = st.base + half * st.kt
            if st.kt == KD:
                for k in range(st.kt):
                    step(half, k, st.order[k], base + k, k % 2)
                    if half == 1 and k == 0:
                        between()
                continue
            for k in range(2):
                step(half, k, k, base + k, k)
                if half == 1 and k == 0:
                    between()
            with engine.Fori(0, (st.kt - 4) // 2) as i:
                for u in range(2):
                    step(half, None, 2 * i + 2 + u, base + 2 * i + 2 + u, u)
            for k in range(st.kt - 2, st.kt):
                step(half, k, k, base + k, k % 2)

    def first(half, k):
        return half == 0 and k is not None and k < 2

    def down_sync(sp, st):
        def step(half, k, kk, j, slot):
            if not first(half, k):
                sp.wait_ge(st.lo, j - 1)
            sp.dma_start(down_raw[slot][:], st.w[half, kk]).then_inc(st.landed[slot], 16)
        down_steps(st, sp, step, lambda: None)

    def down_scalar(act, st):
        s = nc.scalar

        def step(half, k, kk, j, slot):
            if not first(half, k):
                act.wait_ge(st.mm, j - 1)
            s.copy(split_hi[slot][:], st.src[:, kk, :])
            act.wait_ge(st.landed[slot], (j - slot) * 8 + 16)
            s.copy(down_hi[slot][:], down_raw[slot][:]).then_inc(st.hi, 1)

        def between():
            act.wait_ge(st.mm, st.base + st.kt)
            for n in range(0, NT, 2):
                s.copy(y_left[:, n, :], bank(n)).then_inc(st.evac, 1)
        down_steps(st, act, step, between)

    def down_vector(dve, st):
        v = nc.vector

        def step(half, k, kk, j, slot):
            dve.wait_ge(st.hi, j + 1)
            v.tensor_tensor(split_lo[slot][:], st.src[:, kk, :], split_hi[slot][:], ALU.subtract)
            v.tensor_tensor(down_lo[slot][:], down_raw[slot][:], down_hi[slot][:], ALU.subtract).then_inc(st.lo, 1)

        def between():
            dve.wait_ge(st.mm, st.base + st.kt)
            for n in range(1, NT, 2):
                v.tensor_copy(y_left[:, n, :], bank(n)).then_inc(st.evac2, 1)
        down_steps(st, dve, step, between)

    def down_tensor(pe, st):
        t = nc.tensor

        def step(half, k, kk, j, slot):
            pe.wait_ge(st.lo, j + 1)
            for n in range(NT):
                if half == 1 and k == 0:
                    pe.wait_ge((st.evac, st.evac2)[n % 2], st.evacs + n // 2 + 1)
                rows = slice(P * n, P * (n + 1))
                parts = ((split_hi, down_hi), (split_hi, down_lo), (split_lo, down_hi))
                for m, (l, r) in enumerate(parts):
                    ins = t.matmul(bank(n), l[slot][:, rows], r[slot][:], start=(k == 0 and m == 0),
                                   stop=(k == st.kt - 1 and m == 2))
            ins.then_inc(st.mm, 1)
        down_steps(st, pe, step, lambda: None)


    def up_pairs(engine, pair, last):
        pair(0, 0, True)
        with engine.Fori(0, (NF - 2) // 2) as i:
            pair(2 * i + 1, 1, False)
            pair(2 * i + 2, 0, False)
        pair(NF - 1, 1, False)
        last(NF, 0)

    def up_sync(sp, st):
        def pair(p, par, is_first):
            for u in range(2):
                if is_first:
                    continue
                sp.wait_ge(st.lo, st.base + 2 * p + u - 1)
                sp.dma_start(up_raw[u][:], st.w[u][p]).then_inc(st.landed[u], 16)
        up_pairs(sp, pair, lambda p, par: None)

    def up_first(sp, st):
        for u in range(2):
            sp.dma_start(up_raw[u][:], st.w[u][0]).then_inc(st.landed[u], 16)

    def up_scalar(act, st):
        s = nc.scalar

        def split(p, u, is_first):
            if not is_first:
                act.wait_ge(st.mm, st.base + 2 * p + u - 1)
            act.wait_ge(st.landed[u], 8 * st.base + 16 * p + 16)
            s.copy(split_hi[u][:], up_raw[u][:].rearrange("p k c -> p (k c)")).then_inc(st.hi, 1)

        def finish(p, par):
            banks = 4 * (1 - par)
            act.wait_ge(st.mm, st.base + 2 * p - 1)
            if not st.conv:
                s.activation(gate[1 - par][:], psum[:, HALF * banks:HALF * (banks + 2)], ACT.Silu).then_inc(st.act, 1)
                return
            act.wait_ge(st.coef, p)
            for u in range(2):
                if u:
                    act.wait_ge(st.mm, st.base + 2 * p)
                w = conv_now[:, 1 - par, u]
                s.activation(gate[2 * (1 - par) + u][:], psum[:, HALF * (banks + 2 * u):HALF * (banks + 2 * u + 2)],
                             ACT.Identity, scale=w[:, 1:2], bias=w[:, 3:4]).then_inc(st.act, 1)

        def activate(p, par):
            act.wait_ge(st.shift, 4 * p - 2)
            s.activation(gate[2 * (1 - par)][:], gate[2 * (1 - par)][:], ACT.Gelu_apprx_tanh).then_inc(st.act, 1)

        def pair(p, par, is_first):
            split(p, 0, is_first)
            if not is_first:
                finish(p, par)
            split(p, 1, is_first)
            if not is_first and st.conv:
                activate(p, par)

        def last(p, par):
            finish(p, par)
            if st.conv:
                activate(p, par)
        up_pairs(act, pair, last)

    def up_vector(dve, st):
        v = nc.vector

        def split(p, u):
            dve.wait_ge(st.hi, st.base + 2 * p + u + 1)
            v.tensor_tensor(split_lo[u][:], up_raw[u][:].rearrange("p k c -> p (k c)"), split_hi[u][:], ALU.subtract).then_inc(st.lo, 1)

        def shifts(p, par):
            for u in range(2):
                dve.wait_ge(st.act, 3 * p - 2 + u)
                b = HALF * (4 * (1 - par) + 2 * u)
                g, w = gate[2 * (1 - par) + u], conv_now[:, 1 - par, u]
                v.scalar_tensor_tensor(g[:, 1:SEQ], psum[:, b:b + SEQ - 1], w[:, 0:1], g[:, 1:SEQ], ALU.mult, ALU.add).then_inc(st.shift, 1)
                dve.wait_ge(st.shift, 4 * p - 3 + 2 * u)
                v.scalar_tensor_tensor(g[:, 0:SEQ - 1], psum[:, b + 1:b + SEQ], w[:, 2:3], g[:, 0:SEQ - 1], ALU.mult, ALU.add).then_inc(st.shift, 1)

        def product(p, par):
            b = HALF * (4 * (1 - par) + 2)
            if st.conv:
                dve.wait_ge(st.act, 3 * p)
                dve.wait_ge(st.shift, 4 * p)
                left, right = gate[2 * (1 - par)][:], gate[2 * (1 - par) + 1][:]
            else:
                dve.wait_ge(st.act, st.acts + p)
                dve.wait_ge(st.mm, st.base + 2 * p)
                left, right = gate[1 - par][:], psum[:, b:b + SEQ]
            v.tensor_tensor(hidden[:, p - 1, :], left, right, ALU.mult).then_inc(st.prod, 1)

        def pair(p, par, is_first):
            split(p, 0)
            if st.conv:
                v.tensor_copy(conv_now[:, par], conv_cols[:, p]).then_inc(st.coef, 1)
                if not is_first:
                    shifts(p, par)
            elif not is_first:
                product(p, par)
            split(p, 1)
            if st.conv and not is_first:
                product(p, par)

        def last(p, par):
            if st.conv:
                shifts(p, par)
            product(p, par)
        up_pairs(dve, pair, last)

    def up_tensor(pe, st):
        t = nc.tensor
        freed, per, done = (st.shift, 4, 0) if st.conv else (st.prod, 1, st.pairs)

        def pair(p, par):
            for u in range(2):
                pe.wait_ge(st.lo, st.base + 2 * p + u + 1)
                for k in range(KD):
                    cols = slice(P * k, P * (k + 1))
                    for m, (l, r) in enumerate(((split_hi, x_hi), (split_hi, x_lo), (split_lo, x_hi))):
                        for half in range(2):
                            ins = t.matmul(bank(4 * par + 2 * u + half), l[u][:, cols], r[:, k, HALF * half:HALF * (half + 1)],
                                           start=(k == 0 and m == 0), stop=(k == KD - 1 and m == 2))
                ins.then_inc(st.mm, 1)

        pair(0, 0)
        pair(1, 1)
        with pe.Fori(0, (NF - 2) // 2) as i:
            for u in range(2):
                pe.wait_ge(freed, done + per * (2 * i + u + 1))
                pair(2 * i + 2 + u, u)


    Y_SCALE = {2: 0.5, 3: 1.0, 4: 0.5}

    def end_load(sp, e, st):
        sp.wait_ge(st.mm, st.base + (1 if st.kt == KD else st.kt + NT))
        if e:
            sp.wait_ge(res_out, 16 * NT * e)
        src = row_view(a["x"][0] if e == 0 else res_dram[e - 1])
        for n in range(NT):
            sp.dma_start(res[:, n, :], src[:, n, :]).then_inc(res_in, 16)

    def end_store(sp, e):
        dst = row_view(res_dram[e] if e < 4 else out[0])
        for n in range(NT):
            sp.wait_ge(row_ready, NT * e + n + 1)
            sp.dma_start(dst[:, n, :], res[:, n, :]).then_inc(res_out, 16)

    def load_gains(sp, g_name, b_name):
        sp.dma_start(row_a[:], a[g_name].to_broadcast([P, D])).then_inc(gain_in, 16)
        sp.dma_start(row_b[:], a[b_name].to_broadcast([P, D])).then_inc(gain_in, 16)

    def end_scalar(act, e, st):
        s = nc.scalar
        squares = 3 * NT * e
        if e < 2:
            act.wait_ge(st.mm, st.end)
            for n in range(NT):
                for half in range(2):
                    src = y_left[:, n, :] if half == 0 else bank(n)
                    m = squares + 2 * n + half
                    if m >= 2:
                        act.wait_ge(sq_done, m - 1)
                    s.activation(sq_junk[:, HALF * half:HALF * (half + 1)], src, ACT.Square,
                                 accum_out=(stat_a, stat_c)[half][:, n:n + 1]).then_inc(sq_done, 1)
            act.wait_ge(var_ready, 1 + 2 * e)
            s.activation(stat_b[:, 0:NT], stat_a[:, NT:2 * NT], ACT.Sqrt).then_inc(std_ready, 1)
            if e == 0:
                for n in range(NT):
                    act.wait_ge(row_ready, n + 1)
                    act.wait_ge(sq_done, 2 * NT + n)
                    s.activation(sq_junk[:], res[:, n, :], ACT.Square, accum_out=stat_c[:, NT + n:NT + n + 1]).then_inc(sq_done, 1)
                act.wait_ge(var_ready, 2)
                s.activation(stat_b[:, 0:NT], stat_a[:, NT:2 * NT], ACT.Sqrt).then_inc(std_ready, 1)
        else:
            act.wait_ge(res_in, 16 * NT * (e + 1))
            for n in range(NT):
                s.mul(res[:, n, :], res[:, n, :], ALPHA).then_inc(row_prep, 1)
            act.wait_ge(var_ready, 2 + e if e == 2 else 4 + e)
            s.activation(stat_b[:, 0:NT], stat_a[:, NT:2 * NT], ACT.Sqrt).then_inc(std_ready, 1)
            act.wait_ge(row_scaled, NT + e - 1)
            for n in range(NT):
                s.activation(res[:, n, :], res[:, n, :], ACT.Identity, scale=stat_b[:, NT + n:NT + n + 1],
                             bias=stat_c[:, n:n + 1]).then_inc(row_centred, 1)
        if e == 4:
            return
        for i in range(2 * KD):
            half, k = i // KD, i % KD
            dst = x_hi[:, k, HALF * half:HALF * (half + 1)]
            if e == 0:
                act.wait_ge(cols_tmp, i + 1)
                s.copy(dst, split_tmp[i % 2][:]).then_inc(cols_hi, 1)
            else:
                act.wait_ge(cols_turned, 2 * KD * e + i + 1)
                s.copy(dst, bank(i % 4)).then_inc(cols_hi, 1)

    def end_vector(dve, v, steps, e, st):
        if e < 2:
            row = row_a if e == 0 else row_b
            dve.wait_ge(sq_done, 3 * NT * e + 2 * NT)
            steps.add(v.tensor_tensor(stat_a[:, 0:NT], stat_a[:, 0:NT], stat_c[:, 0:NT], ALU.add))
            steps.settle()
            norm_factors(dve, v, steps, stat_a[:, 0:NT], e)
            dve.wait_ge(res_in, 16 * NT * (e + 1))
            for n in range(NT):
                r = stat_b[:, NT + n:NT + n + 1]
                left, right, tmp = slice(0, HALF), slice(HALF, D), post_tmp[n % 2]
                steps.add(v.scalar_tensor_tensor(y_left[:, n, :], y_left[:, n, :], r, row[:, left], ALU.mult, ALU.mult))
                steps.add(v.scalar_tensor_tensor(tmp[:], bank(n), r, row[:, right], ALU.mult, ALU.mult))
                steps.settle()
                steps.add(v.tensor_tensor(res[:, n, left], res[:, n, left], y_left[:, n, :], ALU.add))
                v.tensor_tensor(res[:, n, right], res[:, n, right], tmp[:], ALU.add).then_inc(row_ready, 1)
                steps.settle()
            if e == 0:
                dve.wait_ge(sq_done, 3 * NT)
                norm_factors(dve, v, steps, stat_c[:, NT:2 * NT], 0)
                for n in range(NT):
                    if n == 4:
                        split_columns(dve, v, 0, range(KD), steps)
                        dve.wait_ge(cols_turned, KD)
                    v.tensor_scalar(scaled[n % 4][:], res[:, n, :], stat_b[:, NT + n:NT + n + 1], None, ALU.mult).then_inc(row_scaled, 1)
                split_columns(dve, v, 0, range(KD, 2 * KD), steps)
                return
        else:
            dve.wait_ge(st.mm, st.end)
            for n in range(NT):
                dve.wait_ge(row_prep, NT * (e - 2) + n + 1)
                steps.add(v.scalar_tensor_tensor(res[:, n, 0:HALF], y_left[:, n, :], Y_SCALE[e], res[:, n, 0:HALF], ALU.mult, ALU.add))
                steps.add(v.scalar_tensor_tensor(res[:, n, HALF:D], bank(n), Y_SCALE[e], res[:, n, HALF:D], ALU.mult, ALU.add))
                steps.settle()
                steps.add(v.bn_stats(moments[:, n, 0, :], res[:, n, 0:HALF]))
                steps.add(v.bn_stats(moments[:, n, 1, :], res[:, n, HALF:D]))
                steps.settle()
                steps.add(v.bn_aggr(mean_var[:, n, :], moments[:, n].rearrange("p a b -> p (a b)")))
            steps.settle()
            layer_factors(dve, v, steps, LN_EPS)
            dve.sem_inc(row_scaled, 1)
            dve.wait_ge(gain_in, GAINS_IN[e])
            for n in range(NT):
                dve.wait_ge(row_centred, NT * (e - 2) + n + 1)
                v.tensor_tensor(res[:, n, :], res[:, n, :], row_a[:], ALU.mult).then_inc(row_gained, 1)
        if e < 4:
            split_columns(dve, v, e, range(2 * KD), steps)

    GAINS_IN = {2: 32, 3: 96, 4: 128}

    def norm_factors(dve, v, steps, sums, e):
        steps.add(v.tensor_scalar(stat_a[:, NT:2 * NT], sums, 1.0 / D, RMS_EPS, ALU.mult, ALU.add))
        steps.settle()
        end_root(dve, v, steps)

    def end_root(dve, v, steps):
        steps.roots += 1
        dve.sem_inc(var_ready, 1)
        dve.wait_ge(std_ready, steps.roots)
        inverse_root(v, steps, stat_a[:, NT:2 * NT])

    def layer_factors(dve, v, steps, eps):
        steps.add(v.tensor_scalar(stat_a[:, NT:2 * NT], mean_var[:, :, 1], eps, None, ALU.add))
        steps.settle()
        end_root(dve, v, steps)
        steps.add(v.scalar_tensor_tensor(stat_c[:, 0:NT], mean_var[:, :, 0], -1.0, stat_b[:, NT:2 * NT], ALU.mult, ALU.mult))
        steps.settle()

    def split_columns(dve, v, e, which, steps):
        def rest(i):
            half, k = i // KD, i % KD
            dst = slice(HALF * half, HALF * (half + 1))
            dve.wait_ge(cols_hi, 2 * KD * e + i + 1)
            src = split_tmp[i % 2][:] if e == 0 else bank(i % 4)
            v.tensor_tensor(x_lo[:, k, dst], src, x_hi[:, k, dst], ALU.subtract).then_inc(cols_ready, 1)
        for i in which:
            if e == 0:
                k = i % KD
                dve.wait_ge(cols_turned, i + 1)
                if i >= 2:
                    dve.wait_ge(cols_ready, i - 1)
                v.tensor_scalar(split_tmp[i % 2][:], bank(i % 4), mod_cols[:, 3, k:k + 1], mod_cols[:, 2, k:k + 1],
                                ALU.mult, ALU.add).then_inc(cols_tmp, 1)
                if i > which[0]:
                    rest(i - 1)
            else:
                rest(i)
        if e == 0:
            rest(which[-1])

    def end_gpsimd(pool, e):
        if e < 2:
            return
        for n in range(NT):
            pool.wait_ge(row_gained, NT * (e - 2) + n + 1)
            nc.gpsimd.tensor_tensor(res[:, n, :], res[:, n, :], row_b[:], ALU.add).then_inc(row_ready, 1)

    def end_tensor(pe, e):
        t = nc.tensor
        for i in range(2 * KD):
            half, k = i // KD, i % KD
            if e == 0:
                pe.wait_ge(row_scaled, 4 * (half + 1))
            else:
                pe.wait_ge(row_ready, NT * e + 4 * (half + 1))
            if i >= 4:
                pe.wait_ge(cols_ready, 2 * KD * e + i - 3)
            for n in range(4):
                row = scaled[n][:, P * k:P * (k + 1)] if e == 0 else res[:, 4 * half + n, P * k:P * (k + 1)]
                ins = t.transpose(bank(i % 4, P, P * n), row, ident[:])
            ins.then_inc(cols_turned, 1)
        pe.wait_ge(cols_ready, 2 * KD * (e + 1))


    def blocks_sync(sp):
        sp.wait_ge(y_mm, 6)
        down_sync(sp, down_mix)
        end_load(sp, 0, down_mix)
        sp.wait_ge(down_mix.mm, down_mix.end)
        sp.wait_ge(cols_ready, 2 * KD)
        up_first(sp, up_conv)
        end_store(sp, 0)
        up_sync(sp, up_conv)
        down_sync(sp, down_conv)
        end_load(sp, 1, down_conv)
        sp.wait_ge(row_ready, 2 * NT)
        up_first(sp, up_1)
        end_store(sp, 1)
        load_gains(sp, "ln1_g_2", "ln1_b_2")
        up_sync(sp, up_1)
        down_sync(sp, down_1)
        end_load(sp, 2, down_1)
        mix2_first(sp)
        end_store(sp, 2)
        mix2_sync(sp)
        down_sync(sp, down_mix2)
        end_load(sp, 3, down_mix2)
        sp.wait_ge(down_mix2.mm, down_mix2.end)
        up_first(sp, up_2)
        end_store(sp, 3)
        load_gains(sp, "ln3_g_2", "ln3_b_2")
        up_sync(sp, up_2)
        down_sync(sp, down_2)
        end_load(sp, 4, down_2)
        end_store(sp, 4)
        sp.wait_ge(res_out, 16 * NT * 5)

    def blocks_scalar(act, steps):
        act.wait_ge(glu_ready, 6)
        down_scalar(act, down_mix)
        end_scalar(act, 0, down_mix)
        act.wait_ge(res_out, 16 * NT)
        up_scalar(act, up_conv)
        act.wait_ge(up_conv.prod, up_conv.pairs_end)
        act.wait_ge(up_conv.mm, up_conv.end)
        down_scalar(act, down_conv)
        end_scalar(act, 1, down_conv)
        up_scalar(act, up_1)
        act.wait_ge(up_1.prod, up_1.pairs_end)
        act.wait_ge(up_1.mm, up_1.end)
        down_scalar(act, down_1)
        end_scalar(act, 2, down_1)
        mix2_scalar(act, steps)
        down_scalar(act, down_mix2)
        end_scalar(act, 3, down_mix2)
        up_scalar(act, up_2)
        act.wait_ge(up_2.prod, up_2.pairs_end)
        act.wait_ge(up_2.mm, up_2.end)
        down_scalar(act, down_2)
        end_scalar(act, 4, down_2)

    def blocks_vector(dve, v, steps):
        steps.roots = 0
        down_vector(dve, down_mix)
        end_vector(dve, v, steps, 0, down_mix)
        dve.wait_ge(res_out, 16 * NT)
        up_vector(dve, up_conv)
        down_vector(dve, down_conv)
        end_vector(dve, v, steps, 1, down_conv)
        dve.wait_ge(res_out, 16 * NT * 2)
        up_vector(dve, up_1)
        down_vector(dve, down_1)
        end_vector(dve, v, steps, 2, down_1)
        mix2_vector(dve, v, steps)
        down_vector(dve, down_mix2)
        end_vector(dve, v, steps, 3, down_mix2)
        dve.wait_ge(res_out, 16 * NT * 4)
        up_vector(dve, up_2)
        down_vector(dve, down_2)
        end_vector(dve, v, steps, 4, down_2)

    def blocks_gpsimd(pool, steps):
        pool.wait_ge(gain_in, 32)
        end_gpsimd(pool, 2)
        mix2_gpsimd(pool, steps)
        pool.wait_ge(gain_in, 96)
        end_gpsimd(pool, 3)
        pool.wait_ge(gain_in, 128)
        end_gpsimd(pool, 4)

    def blocks_tensor(pe, t):
        down_tensor(pe, down_mix)
        end_tensor(pe, 0)
        up_tensor(pe, up_conv)
        down_tensor(pe, down_conv)
        end_tensor(pe, 1)
        up_tensor(pe, up_1)
        down_tensor(pe, down_1)
        end_tensor(pe, 2)
        mix2_tensor(pe, t)
        down_tensor(pe, down_mix2)
        end_tensor(pe, 3)
        up_tensor(pe, up_2)
        down_tensor(pe, down_2)

    TOP = 256
    A_HEADS, I_HEADS = 8, 4
    LAT = 128
    MLP = 512
    q2, c2 = 0, A_HEADS * HEAD
    qi2 = c2 + LAT
    ki2 = qi2 + I_HEADS * HEAD
    wi2 = ki2 + HEAD
    u2 = wi2 + I_HEADS
    v2 = u2 + MLP
    qi_t = place("qi_t", [P, 2, SEQ], GR + 32 * KB)
    ki_t = place("ki_t", [P, SEQ], GR + 40 * KB)
    wi_t = place("wi_t", [I_HEADS, SEQ], GR + 44 * KB)
    lat_t = place("lat_t", [P, SEQ], GR + 48 * KB)
    q2_t = place("q2_t", [P, 4, SEQ], GR + 52 * KB)
    mlp_v_t = place("mlp_v_t", [P, 4, SEQ], GR)
    mlp_u_t = place("mlp_u_t", [P, 4, SEQ], GR + 16 * KB)
    mlp_v = place("mlp_v", [P, NT, MLP], GR + 32 * KB)
    q_abs = [place(f"q_abs{i}", [P, 4, SEQ], GR + 32 * KB * i) for i in range(2)]
    sel_at = [P * b * (b + 1) // 2 for b in range(NT + 1)]
    select = place("select", [P, sel_at[NT]], GR + 68 * KB)
    count_junk = [place(f"count_junk{i}", [P, SEQ], GR + 48 * KB + 2 * KB * i, mybir.dt.bfloat16) for i in range(2)]
    relu_tmp = [place(f"relu_tmp{i}", [P, SEQ], RR + 28 * KB + 4 * KB * i) for i in range(2)]
    equal, ranks = (place(n, [P, SEQ], RR + 28 * KB + 4 * KB * i) for i, n in enumerate(("equal", "ranks")))
    lat = place("lat", [P, NT, LAT], RR + 24 * KB)
    lat_n_t = place("lat_n_t", [P, SEQ], RR + 40 * KB)
    kv_gain = place("kv_gain", [P, LAT], RR + 38 * KB)
    causal = place("causal", [P, P], RR + 38 * KB + 512)
    wi_rows = place("wi_rows", [P, NT, I_HEADS], RR + 39 * KB)
    limit = place("limit", [P, 6], RR + 39 * KB + 128, I32)
    trial = place("trial", [P, 6], RR + 39 * KB + 160, I32)
    keep = place("keep", [P, 6], RR + 39 * KB + 192, I32)
    bit = place("bit", [P, 2], RR + 39 * KB + 224, I32)
    counts = place("counts", [P, 6], RR + 39 * KB + 256)
    wanted = place("wanted", [P, 6], RR + 39 * KB + 288)
    one_col = place("one_col", [P, 1], RR + 39 * KB + 320)
    v_sum = place("v_sum", [P, NT], RR + 39 * KB + 352)
    v_mean_neg = place("v_mean_neg", [P, NT], RR + 39 * KB + 384)
    row_max = place("row_max", [P, NT * A_HEADS], RR + 39 * KB + 416)
    row_sum = place("row_sum", [P, NT * A_HEADS], RR + 39 * KB + 672)
    uk_raw = place("uk_raw", [P, A_HEADS, HEAD], RR)
    w_uv = place("w_uv", [P, A_HEADS, HEAD], RR + 2 * KB)
    ws_raw = place("ws_raw", [P, 8, P], RR + 4 * KB)
    ws_t = place("ws_t", [P, 8, P], RR + 8 * KB)
    bs_rows = place("bs_rows", [P, 4, P], RR + 12 * KB)
    upper = place("upper", [P, P], RR + 14 * KB)
    gm_tmp = [place(f"gm_tmp{i}", [P, 4, P], RR + 16 * KB + 2 * KB * i) for i in range(2)]
    uk_t = place("uk_t", [P, 4, LAT], RR + 36 * KB)
    p2 = [place(f"p2_{i}", [P, SEQ], XR + 32 * KB + 4 * KB * i) for i in range(3)]
    p2_t = place("p2_t", [P, NT, 4, P], XR + 44 * KB)
    o_lat = [place(f"o_lat{i}", [P, 4, P], XR + 60 * KB + 2 * KB * i) for i in range(2)]

    a_hi, a_lo, a_mm, a_evac = (sem(n) for n in ("a_hi", "a_lo", "a_mm", "a_evac"))
    a_in = [sem(f"a_in{i}") for i in range(2)]
    small2_in, lat_turned, lat_sq, lat_ready, lat_back = (sem(n) for n in ("small2_in", "lat_turned", "lat_sq", "lat_ready", "lat_back"))
    logit_mm, relu_done, score_added, bits_done, chosen, mask_ready = (
        sem(n) for n in ("logit_mm", "relu_done", "score_added", "bits_done", "chosen", "mask_ready"))
    mix2_in, mix2_turned, ws_copied, ws_ready = (sem(n) for n in ("mix2_in", "mix2_turned", "ws_copied", "ws_ready"))
    mv_turned, mv_copied, mv_mean, mv_sq, mv_scaled, mv_ready = (
        sem(n) for n in ("mv_turned", "mv_copied", "mv_mean", "mv_sq", "mv_scaled", "mv_ready"))
    sv_mm, sv_copied, gm_ready, qa_mm, qa_ready = (sem(n) for n in ("sv_mm", "sv_copied", "gm_ready", "qa_mm", "qa_ready"))
    bs_in = sem("bs_in")
    ol_mm, ol_ready, sum_ready = sem("ol_mm"), sem("ol_ready"), sem("sum_ready")

    GELU = ACT.Gelu_apprx_tanh
    a_units = [([(qi2 + P * i, P)], qi_t[:, i, :], None) for i in range(2)]
    a_units += [([(ki2, HEAD), (ki2, HEAD)], ki_t[:, :], None), ([(wi2, I_HEADS)], wi_t[:, :], None),
                ([(c2, LAT)], lat_t[:, :], None)]
    a_units += [([(q2 + P * i, P)], q2_t[:, i, :], None) for i in range(4)]
    a_units += [([(v2 + P * i, P)], mlp_v_t[:, i, :], GELU) for i in range(4)]
    a_units += [([(u2 + P * i, P)], mlp_u_t[:, i, :], GELU) for i in range(4)]
    A_UNITS = len(a_units)
    A_V = 9
    a_counts, a_landed = [], [0, 0]
    for n, (cols, _, _) in enumerate(a_units):
        a_landed[n % 2] += 16 * len(cols)
        a_counts.append(a_landed[n % 2])
    LOGITS = [(h, b) for h in range(I_HEADS) for b in range(2, NT)]
    BITS_FIRST = 20
    SEARCHED = range(2, NT)

    def width(b):
        return P * (b + 1)

    def sel(b):
        return select[:, sel_at[b]:sel_at[b + 1]]

    def a_load(sp, n):
        at_col = 0
        for c, m in a_units[n][0]:
            sp.dma_start(up_raw[n % 2][:, :, at_col:at_col + m],
                         a["w_in_2"][0].rearrange("(k p) n -> p k n", p=P)[:, :, c:c + m]).then_inc(a_in[n % 2], 16)
            at_col += m

    def a_width(n):
        return sum(m for _, m in a_units[n][0])

    def tile_of(buf, m):
        return buf[:].rearrange("p (k c) -> p k c", c=P)[:, :, 0:m]

    def mix2_first(sp):
        sp.wait_ge(down_1.mm, down_1.end)
        for n in range(2):
            a_load(sp, n)

    def mix2_sync(sp):
        sp.dma_start(kv_gain[:], a["kv_norm_g_2"].to_broadcast([P, LAT])).then_inc(small2_in, 16)
        sp.dma_start(causal[:], a["causal"]).then_inc(small2_in, 16)
        sp.dma_start(row_a[:, 0:MLP], a["gmlp_ln_g_2"].to_broadcast([P, MLP])).then_inc(gain_in, 16)
        sp.dma_start(row_b[:, 0:MLP], a["gmlp_ln_b_2"].to_broadcast([P, MLP])).then_inc(gain_in, 16)
        for n in range(2, A_UNITS):
            sp.wait_ge(a_lo, n - 1)
            a_load(sp, n)
        sp.wait_ge(a_lo, A_UNITS)
        sp.dma_start(uk_raw[:], a["w_uk_2"][0].rearrange("h c d -> c h d")).then_inc(mix2_in, 16)
        sp.dma_start(w_uv[:], a["w_uv_2"][0].rearrange("h c d -> c h d")).then_inc(mix2_in, 16)
        sp.dma_start(ws_raw[:], a["gmlp_ws_2"][0].rearrange("g t s -> t g s")).then_inc(mix2_in, 16)
        sp.wait_ge(a_mm, A_UNITS)
        sp.dma_start(upper[:], a["upper"]).then_inc(bs_in, 16)
        for g in range(8):
            sp.dma_start(bs_rows[HEAD * (g % 2):HEAD * (g % 2 + 1), g // 2, :],
                         a["gmlp_bs_2"][0, g:g + 1, :].to_broadcast([HEAD, P])).then_inc(bs_in, 16)
        sp.wait_ge(mv_ready, NT)
        load_gains(sp, "ln2_g_2", "ln2_b_2")
        sp.wait_ge(att_ready, 2 * NT)

    def mix2_tensor(pe, t):
        def unit(n):
            m, slot = a_width(n), n % 2
            pe.wait_ge(a_lo, n + 1)
            if n >= 2:
                pe.wait_ge(a_evac, n - 1)
            for k in range(KD):
                for i, (l, r) in enumerate(((split_hi, x_hi), (split_hi, x_lo), (split_lo, x_hi))):
                    for half in range(2):
                        ins = t.matmul(bank(2 * slot + half)[0:m], l[slot][:, P * k:P * k + m], r[:, k, HALF * half:HALF * (half + 1)],
                                       start=(k == 0 and i == 0), stop=(k == KD - 1 and i == 2))
            ins.then_inc(a_mm, 1)

        def turn_values(n):
            if n >= 4:
                pe.wait_ge(mv_copied, n - 3)
            for i in range(4):
                ins = t.transpose(bank(4 + n % 4, P, P * i), mlp_v_t[:, i, P * n:P * (n + 1)], ident[:])
            ins.then_inc(mv_turned, 1)

        for n in range(5):
            unit(n)
        pe.wait_ge(a_evac, 4)
        for b in range(NT):
            ins = t.transpose(bank(6, I_HEADS, I_HEADS * b), wi_t[:, P * b:P * (b + 1)], ident[0:I_HEADS, 0:I_HEADS])
        ins.then_inc(lat_turned, 1)
        pe.wait_ge(a_evac, 5)
        for b in range(NT):
            ins = t.transpose(bank(4 + b // 4, P, P * (b % 4)), lat_t[:, P * b:P * (b + 1)], ident[:])
        ins.then_inc(lat_turned, 1)
        unit(5)
        pe.wait_ge(lat_ready, NT + 1)
        for i, (h, b) in enumerate(LOGITS):
            if i >= 2:
                pe.wait_ge(relu_done, i - 1)
            rows = slice(HEAD * (h % 2), HEAD * (h % 2 + 1))
            for s0 in range(0, width(b), HALF):
                n = min(HALF, width(b) - s0)
                ins = t.matmul(bank(4 + 2 * (i % 2) + s0 // HALF, n), qi_t[rows, h // 2, P * b:P * (b + 1)], ki_t[rows, s0:s0 + n],
                               start=True, stop=True)
            ins.then_inc(logit_mm, 1)
        unit(6)
        pe.wait_ge(relu_done, len(LOGITS))
        for b in range(NT):
            ins = t.transpose(bank(4 + b // 4, P, P * (b % 4)), lat[:, b, :], ident[:])
        ins.then_inc(lat_turned, 1)
        for n in range(7, A_UNITS):
            unit(n)
            if n == 13:
                pe.wait_ge(lat_back, 2)
                pe.wait_ge(a_evac, 13)
                for b in range(4):
                    turn_values(b)
            elif n == 14:
                for b in range(4, NT):
                    turn_values(b)
        pe.wait_ge(mix2_in, 16 * 3)
        pe.wait_ge(mv_copied, NT)
        for i in range(4):
            ins = t.transpose(bank(6, P, P * i), uk_raw[:, 2 * i:2 * i + 2, :].rearrange("c h d -> c (h d)"), ident[:])
        ins.then_inc(mix2_turned, 1)
        for g in range(8):
            ins = t.transpose(bank(4 + g // 4, P, P * (g % 4)), ws_raw[:, g, :], ident[:])
        ins.then_inc(mix2_turned, 1)
        pe.wait_ge(a_evac, A_UNITS)
        pe.wait_ge(ws_copied, 2)

        def queries(h):
            rows = slice(HEAD * (h % 2), HEAD * (h % 2 + 1))
            for half in range(2):
                i = 2 * h + half
                if i >= 4:
                    pe.wait_ge(qa_ready, i - 3)
                t.matmul(bank(i % 4), uk_t[rows, h // 2, :], q2_t[rows, h // 2, HALF * half:HALF * (half + 1)],
                         start=True, stop=True).then_inc(qa_mm, 1)

        for h in range(4):
            queries(h)
        pe.wait_ge(ws_ready, 1)
        for n in range(NT):
            pe.wait_ge(mv_ready, n + 1)
            if n >= 4:
                pe.wait_ge(sv_copied, n - 3)
            for g in range(8):
                ins = t.matmul(bank(4 + n % 4, P, P * (g // 2))[HEAD * (g % 2):HEAD * (g % 2 + 1)],
                               mlp_v[:, n, HEAD * g:HEAD * (g + 1)], ws_t[:, g, :], start=True, stop=True)
            ins.then_inc(sv_mm, 1)
        for h in range(4, A_HEADS):
            queries(h)

        def scores(i):
            b, h = i // A_HEADS, i % A_HEADS
            if i >= 2:
                pe.wait_ge(max_ready, ITEMS + i - 1)
            for s0 in range(0, width(b), HALF):
                n = min(HALF, width(b) - s0)
                ins = t.matmul(bank(2 * (i % 2) + s0 // HALF, n), q_abs[h // 4][:, h % 4, P * b:P * (b + 1)], lat_n_t[:, s0:s0 + n],
                               start=True, stop=True)
            ins.then_inc(scores_mm, 1)

        def turn_probs(i):
            b = i // A_HEADS
            pe.wait_ge(probs_ready, ITEMS + i + 1)
            if i:
                pe.wait_ge(probs_t_ready, ITEMS + i)
            for k in range(b + 1):
                ins = t.transpose(bank(4 + k // 4, P, P * (k % 4)), p2[i % 3][:, P * k:P * (k + 1)], ident[:])
            ins.then_inc(probs_turned, 1)

        def values(i):
            b, half = i // 2, i % 2
            pe.wait_ge(probs_t_ready, ITEMS + 4 * i + 4)
            if i:
                pe.wait_ge(ol_ready, i)
            for k in range(b + 1):
                ins = t.matmul(bank(6), lat[:, k, :], p2_t[:, k].rearrange("p h q -> p (h q)"), start=(k == 0), stop=(k == b))
            ins.then_inc(ol_mm, 1)

        def outputs(i):
            b, half = i // 2, i % 2
            pe.wait_ge(ol_ready, i + 1)
            if b and half == 0:
                pe.wait_ge(att_ready, NT + b)
            for h in range(4 * half, 4 * half + 4):
                ins = t.matmul(bank(7, P, P * (h // 2))[HEAD * (h % 2):HEAD * (h % 2 + 1)], w_uv[:, h, :], o_lat[half][:, h % 4, :],
                               start=True, stop=True)
            ins.then_inc(att_mm, 1)

        pe.wait_ge(qa_ready, 2 * A_HEADS)
        pe.wait_ge(sv_copied, NT)
        for i in range(ITEMS2 + 4):
            if i < ITEMS2:
                scores(i)
            if 2 <= i < ITEMS2 + 2:
                turn_probs(i - 2)
            if i >= 6 and (i - 6) % 4 == 0:
                values((i - 6) // 4)
            if i >= 7 and (i - 7) % 4 == 0:
                outputs((i - 7) // 4)

    ITEMS2 = NT * A_HEADS

    def mix2_scalar(act, steps):
        s = nc.scalar

        def split(n):
            m, slot = a_width(n), n % 2
            if n >= 2:
                act.wait_ge(a_mm, n - 1)
            act.wait_ge(a_in[slot], a_counts[n])
            s.copy(tile_of(split_hi[slot], m), up_raw[slot][:, :, 0:m]).then_inc(a_hi, 1)

        def store(n):
            m, slot = a_width(n), n % 2
            act.wait_ge(a_mm, n + 1)
            if n == A_V:
                act.wait_ge(res_out, 16 * NT * 3)
            src = psum[0:m, 2 * HALF * slot:2 * HALF * (slot + 1)]
            if a_units[n][2] is None:
                s.copy(a_units[n][1], src).then_inc(a_evac, 1)
            else:
                s.activation(a_units[n][1], src, a_units[n][2]).then_inc(a_evac, 1)

        for n in range(A_UNITS):
            split(n)
            if n:
                store(n - 1)
            if n == 5:
                act.wait_ge(lat_turned, 2)
                for b in range(NT):
                    s.activation(relu_tmp[0][:, P * b:P * (b + 1)], bank(4 + b // 4, P, P * (b % 4)), ACT.Square,
                                 accum_out=stat_a[:, b:b + 1]).then_inc(lat_sq, 1)
                act.wait_ge(var_ready, 5)
                s.activation(stat_b[:, 0:NT], stat_a[:, NT:2 * NT], ACT.Sqrt).then_inc(std_ready, 1)
            elif n == 6:
                act.wait_ge(lat_sq, NT)
                for i, (h, b) in enumerate(LOGITS):
                    act.wait_ge(logit_mm, i + 1)
                    if i >= 2:
                        act.wait_ge(score_added, i - 1)
                    src = psum[:, HALF * (4 + 2 * (i % 2)):HALF * (4 + 2 * (i % 2)) + width(b)]
                    s.activation(relu_tmp[i % 2][:, 0:width(b)], src, ACT.Relu, scale=HEAD ** -0.5).then_inc(relu_done, 1)
            elif n == 7:
                act.wait_ge(lat_turned, 3)
                for i in range(2):
                    s.copy(lat_n_t[:, HALF * i:HALF * (i + 1)], bank(4 + i)).then_inc(lat_back, 1)
            elif n in (14, 15):
                for b in range(4 * (n - 14), 4 * (n - 13)):
                    act.wait_ge(mv_turned, b + 1)
                    s.activation(mlp_v[:, b, :], bank(4 + b % 4), ACT.Copy, accum_out=v_sum[:, b:b + 1]).then_inc(mv_copied, 1)
                if n == 15:
                    act.wait_ge(mv_mean, 1)
                    act.wait_ge(score_added, len(LOGITS))
                    for b in range(NT):
                        if b >= 2:
                            act.wait_ge(mv_sq, b - 1)
                        s.activation(sq_two[:, MLP * (b % 2):MLP * (b % 2 + 1)], mlp_v[:, b, :], ACT.Square,
                                     bias=v_mean_neg[:, b:b + 1], accum_out=stat_a[:, b:b + 1]).then_inc(mv_sq, 1)
        store(A_UNITS - 1)
        act.wait_ge(mix2_turned, 1)
        s.copy(uk_t[:].rearrange("p a c -> p (a c)"), bank(6)).then_inc(ws_copied, 2)
        act.wait_ge(mix2_turned, 2)
        s.copy(ws_t[:].rearrange("p g t -> p (g t)"), psum[:, 4 * HALF:6 * HALF]).then_inc(ws_copied, 1)

        def queries(h):
            for half in range(2):
                i = 2 * h + half
                act.wait_ge(qa_mm, i + 1)
                s.mul(q_abs[h // 4][:, h % 4, HALF * half:HALF * (half + 1)], bank(i % 4), HEAD ** -0.5).then_inc(qa_ready, 1)

        for h in range(4):
            queries(h)
        act.wait_ge(var_ready, 6)
        s.activation(stat_b[:, 0:NT], stat_a[:, NT:2 * NT], ACT.Sqrt).then_inc(std_ready, 1)
        act.wait_ge(mv_scaled, 1)
        for n in range(NT):
            s.activation(mlp_v[:, n, :], mlp_v[:, n, :], ACT.Identity, scale=stat_b[:, NT + n:NT + n + 1],
                         bias=stat_c[:, n:n + 1]).then_inc(mv_scaled, 1)
        for n in range(NT):
            act.wait_ge(sv_mm, n + 1)
            if n >= 2:
                act.wait_ge(gm_ready, n - 1)
            s.copy(gm_tmp[n % 2][:].rearrange("p a t -> p (a t)"), bank(4 + n % 4)).then_inc(sv_copied, 1)
        for h in range(4, A_HEADS):
            queries(h)

        def exponentials(i):
            w = width(i // A_HEADS)
            act.wait_ge(max_ready, ITEMS + i + 1)
            p = p2[i % 3][:, 0:w]
            s.activation(p, p, ACT.Exp, bias=row_max[:, i:i + 1], accum_out=row_sum[:, i:i + 1]).then_inc(exp_ready, 1)

        def copy_probs(i):
            b, h = i // A_HEADS, i % A_HEADS
            act.wait_ge(probs_turned, ITEMS + i + 1)
            if h % 4 == 0 and i:
                act.wait_ge(ol_mm, i // 4)
            s.copy(p2_t[:, 0:b + 1, h % 4, :], psum[:, 4 * HALF:4 * HALF + width(b)].rearrange("p (k q) -> p k q", q=P)).then_inc(probs_t_ready, 1)

        def finish(i):
            b, half = i // 2, i % 2
            act.wait_ge(ol_mm, i + 1)
            if i >= 2:
                act.wait_ge(att_mm, ITEMS + i - 1)
            s.copy(o_lat[half][:].rearrange("p h q -> p (h q)"), bank(6)).then_inc(ol_ready, 1)
            if i % 2 == 0 and i:
                last(b - 1)

        def last(b):
            act.wait_ge(att_mm, ITEMS + 2 * b + 2)
            s.copy(yc_t[:, 0:4, P * b:P * (b + 1)], bank(7).rearrange("p (k q) -> p k q", q=P)).then_inc(att_ready, 1)

        for i in range(ITEMS2 + 4):
            if i < ITEMS2:
                exponentials(i)
            if 2 <= i < ITEMS2 + 2:
                copy_probs(i - 2)
            if i >= 6 and (i - 6) % 4 == 0:
                finish((i - 6) // 4)
        last(NT - 1)
        act.wait_ge(gm_ready, NT)
        act.wait_ge(att_ready, 2 * NT)

    def mix2_vector(dve, v, steps):
        one = steps.add
        dve.wait_ge(lat_turned, 1)
        one(v.tensor_scalar(wi_rows[:].rearrange("p n h -> p (n h)"), bank(6, NT * I_HEADS), I_HEADS ** -0.5, None, ALU.mult))
        one(v.memset(one_col[:], 1.0))
        dve.wait_ge(lat_sq, NT)
        one(v.tensor_scalar(stat_a[:, NT:2 * NT], stat_a[:, 0:NT], 1.0 / LAT, LN_EPS, ALU.mult, ALU.add))
        steps.settle()
        dve.sem_inc(lat_ready, 1)
        end_root(dve, v, steps)
        dve.wait_ge(small2_in, 32)
        for b in range(NT):
            v.scalar_tensor_tensor(lat[:, b, :], bank(4 + b // 4, P, P * (b % 4)), stat_b[:, NT + b:NT + b + 1], kv_gain[:],
                                   ALU.mult, ALU.mult).then_inc(lat_ready, 1)
        n_b = len(SEARCHED)
        for i, (h, b) in enumerate(LOGITS):
            dve.wait_ge(relu_done, i + 1)
            r, w = relu_tmp[i % 2][:, 0:width(b)], wi_rows[:, b, h:h + 1]
            if h == 0:
                v.tensor_scalar(sel(b), r, w, None, ALU.mult).then_inc(score_added, 1)
            else:
                dve.wait_ge(score_added, i - n_b + 1)
                v.scalar_tensor_tensor(sel(b), r, w, sel(b), ALU.mult, ALU.add).then_inc(score_added, 1)
        dve.wait_ge(score_added, len(LOGITS))
        for b in SEARCHED:
            diagonal = select[:, sel_at[b + 1] - P:sel_at[b + 1]]
            one(v.tensor_tensor(diagonal, diagonal, causal[:], ALU.add))
        steps.settle()
        limits = limit[:].bitcast(F32)

        def count_all(op, against):
            for j, b in enumerate(SEARCHED):
                if j >= 2:
                    dve.wait_ge(dve_steps, steps.n - 1)
                one(v.tensor_scalar(count_junk[j % 2][:, 0:width(b)], sel(b), against[j], 0.0, op, ALU.add, counts[:, j:j + 1]))

        count_all(ALU.is_ge, [0.0] * n_b)
        one(v.memset(bit[:, 0:1], 1 << 30))
        steps.settle()
        one(v.tensor_scalar(limit[:], counts[:], float(TOP), -1.0, ALU.is_lt, ALU.mult))
        steps.settle()
        per = n_b + 4

        def next_bit(i):
            done = per * i
            v.tensor_tensor(trial[:], limit[:], bit[:, 0:1].to_broadcast([P, n_b]), ALU.bitwise_xor).then_inc(bits_done, 1)
            dve.wait_ge(bits_done, done + 1)
            for j, b in enumerate(SEARCHED):
                if j >= 2:
                    dve.wait_ge(bits_done, done + j)
                v.tensor_scalar(count_junk[j % 2][:, 0:width(b)], sel(b), trial[:, j:j + 1].bitcast(F32), 0.0, ALU.is_ge, ALU.add,
                                counts[:, j:j + 1]).then_inc(bits_done, 1)
            dve.wait_ge(bits_done, done + n_b + 1)
            v.tensor_scalar(keep[:], counts[:], float(TOP), -1.0, ALU.is_ge, ALU.mult).then_inc(bits_done, 1)
            dve.wait_ge(bits_done, done + n_b + 2)
            v.tensor_tensor(keep[:], keep[:], bit[:, 0:1].to_broadcast([P, n_b]), ALU.bitwise_and).then_inc(bits_done, 1)
            dve.wait_ge(bits_done, done + n_b + 3)
            v.tensor_tensor(limit[:], limit[:], keep[:], ALU.bitwise_xor)
            v.tensor_scalar(bit[:, 0:1], bit[:, 0:1], 1, None, ALU.logical_shift_right).then_inc(bits_done, 1)
            dve.wait_ge(bits_done, done + n_b + 4)

        with dve.Fori(0, BITS_FIRST) as i:
            next_bit(i)
        dve.wait_ge(mv_sq, NT)
        one(v.tensor_scalar(stat_a[:, NT:2 * NT], stat_a[:, 0:NT], 1.0 / MLP, LN_EPS, ALU.mult, ALU.add))
        steps.settle()
        end_root(dve, v, steps)
        one(v.tensor_tensor(stat_c[:, 0:NT], v_mean_neg[:], stat_b[:, NT:2 * NT], ALU.mult))
        steps.settle()
        dve.sem_inc(mv_scaled, 1)
        with dve.Fori(BITS_FIRST, 31) as i:
            next_bit(i)
        count_all(ALU.is_gt, [limits[:, j:j + 1] for j in range(n_b)])
        steps.settle()
        one(v.tensor_scalar(wanted[:], counts[:], -1.0, float(TOP), ALU.mult, ALU.add))
        steps.settle()
        for j, b in enumerate(SEARCHED):
            eq, rank, lim = equal[:, 0:width(b)], ranks[:, 0:width(b)], limits[:, j:j + 1]
            one(v.tensor_scalar(eq, sel(b), lim, None, ALU.is_equal))
            steps.settle()
            one(v.tensor_tensor_scan(rank, one_col[:].to_broadcast([P, width(b)]), eq, 0.0, ALU.mult, ALU.add))
            steps.settle()
            one(v.scalar_tensor_tensor(eq, rank, wanted[:, j:j + 1], eq, ALU.is_le, ALU.mult))
            steps.settle()
            v.scalar_tensor_tensor(sel(b), sel(b), lim, eq, ALU.is_gt, ALU.add).then_inc(chosen, 1)
            dve.wait_ge(chosen, j + 1)

        def maximum(i):
            b = i // A_HEADS
            w = width(b)
            dve.wait_ge(scores_mm, ITEMS + i + 1)
            if i >= 3:
                dve.wait_ge(probs_turned, ITEMS + i - 2)
            if i % A_HEADS == 0:
                dve.wait_ge(mask_ready, max(b - 1, 0) + 1)
            one(v.tensor_tensor_reduce(p2[i % 3][:, 0:w], psum[:, 2 * HALF * (i % 2):2 * HALF * (i % 2) + w], sel(b), 1.0, NEG,
                                       ALU.add, ALU.max, row_max[:, i:i + 1]))
            steps.settle()
            v.tensor_scalar(row_max[:, i:i + 1], row_max[:, i:i + 1], -1.0, None, ALU.mult).then_inc(max_ready, 1)

        def reciprocal(i):
            dve.wait_ge(exp_ready, ITEMS + i + 1)
            v.reciprocal(row_sum[:, i:i + 1], row_sum[:, i:i + 1]).then_inc(sum_ready, 1)

        for i in range(ITEMS2 + 1):
            if i < ITEMS2:
                maximum(i)
            if i:
                reciprocal(i - 1)

    def mix2_gpsimd(pool, steps):
        g = nc.gpsimd
        pool.wait_ge(small2_in, 32)
        steps.add(g.memset(select[:, sel_at[1]:sel_at[1] + P], 0.0))
        steps.add(g.tensor_copy(select[:, 0:P], causal[:]))
        steps.add(g.tensor_copy(select[:, sel_at[1] + P:sel_at[2]], causal[:]))
        steps.settle()
        pool.sem_inc(mask_ready, 1)
        for n in range(A_UNITS):
            m, slot = a_width(n), n % 2
            pool.wait_ge(a_hi, n + 1)
            g.tensor_tensor(tile_of(split_lo[slot], m), up_raw[slot][:, :, 0:m], tile_of(split_hi[slot], m), ALU.subtract).then_inc(a_lo, 1)
            if n == 15:
                pool.wait_ge(mv_copied, NT)
                g.tensor_scalar(v_mean_neg[:], v_sum[:], -1.0 / MLP, 1.0, ALU.mult, ALU.mult).then_inc(mv_mean, 1)
        pool.wait_ge(ws_copied, 3)
        pool.wait_ge(bs_in, 16 * 9)
        g.tensor_tensor(ws_t[:], ws_t[:], upper[:].unsqueeze(1).to_broadcast([P, 8, P]), ALU.mult).then_inc(ws_ready, 1)
        pool.wait_ge(gain_in, 64)
        for n in range(NT):
            pool.wait_ge(mv_scaled, n + 2)
            steps.add(g.tensor_tensor(mlp_v[:, n, :], mlp_v[:, n, :], row_a[:, 0:MLP], ALU.mult))
            steps.settle()
            g.tensor_tensor(mlp_v[:, n, :], mlp_v[:, n, :], row_b[:, 0:MLP], ALU.add).then_inc(mv_ready, 1)
        for n in range(NT):
            pool.wait_ge(sv_copied, n + 1)
            tmp = gm_tmp[n % 2]
            steps.add(g.tensor_tensor(tmp[:], tmp[:], bs_rows[:], ALU.add))
            steps.settle()
            g.tensor_tensor(yc_t[:, 4:8, P * n:P * (n + 1)], tmp[:], mlp_u_t[:, :, P * n:P * (n + 1)], ALU.mult).then_inc(gm_ready, 1)
        for j, b in enumerate(SEARCHED):
            pool.wait_ge(chosen, j + 1)
            g.tensor_scalar(sel(b), sel(b), -NEG, NEG, ALU.mult, ALU.add).then_inc(mask_ready, 1)
        for i in range(ITEMS2):
            w = width(i // A_HEADS)
            pool.wait_ge(sum_ready, i + 1)
            p = p2[i % 3][:, 0:w]
            g.tensor_scalar(p, p, row_sum[:, i:i + 1], 1.0, ALU.mult, ALU.mult).then_inc(probs_ready, 1)

    block = ctx.enter_context(nc.Block())

    N_ADA = 6 * D // HALF

    @block.sync
    def _(sp):
        sp.dma_start(c_cols[:], a["c"].rearrange("o (p k) -> (o p) k", k=KD)).then_inc(small_in, 16)
        sp.dma_start(ident[:], a["ident"]).then_inc(ident_in, 16)
        w_ada = a["w_ada"][0].rearrange("(p k) n -> p k n", k=KD)
        for j in range(N_ADA):
            if j >= 2:
                sp.wait_ge(ada_mm, j - 1)
            cols = slice(HALF * j, HALF * (j + 1))
            sp.dma_start(ada_w[j % 2][:], w_ada[:, :, cols]).then_inc(ada_in[j % 2], 16)
            sp.dma_start(ada_b[j % 2][:], a["b_ada"][:, cols]).then_inc(ada_in[j % 2], 16)
        taps = GROUPS * GC
        sp.wait_ge(k_ready, 1)
        sp.dma_start(k_shift[7 * GC:8 * GC, :], k_sum[0:GC, 1, :]).then_inc(k_shift_in, 16)
        sp.wait_ge(k_ready, 2)
        for s in range(CH):
            sp.dma_start(toep_dram[14 - s], k_sum[GC * s:GC * (s + 1), 0, :]).then_inc(k_in_dram, 16)
            if s:
                sp.dma_start(toep_dram[7 - s], k_sum[GC * s:GC * (s + 1), 1, :]).then_inc(k_in_dram, 16)
        sp.wait_ge(k_in_dram, 16 * 15)
        for s in range(CH):
            sp.dma_start(toep[GC * s:GC * (s + 1), :, :],
                         toep_dram[7 - s:15 - s].rearrange("t c n -> c t n")).then_inc(toep_in, 16)
        w_in = a["w_in"][0].rearrange("(k p) n -> p k n", p=P)
        for n, (cols, _) in enumerate(win_units):
            if n >= 3:
                sp.wait_ge(win_mm, n - 2)
            elif n == 0:
                sp.wait_ge(vec_used, 1)
            elif n == 1:
                sp.wait_ge(carry_ready, 2)
            at_col = 0
            for c, m in cols:
                sp.dma_start(win_raw[n % 3][:, :, at_col:at_col + m], w_in[:, :, c:c + m]).then_inc(win_in[n % 3], 16)
                at_col += m
        mix_sync(sp)

    @block.scalar
    def _(act):
        steps = Steps(act, act_steps)
        lam = lam_rows
        act.dma_start(lam[:, 0, :], a["lam_re"][0].rearrange("d (q e) p -> (d q) (e p)", e=2)).then_inc(ssm_in, 16)
        act.dma_start(lam[:, 1, :], a["lam_im"][0].rearrange("d (q e) p -> (d q) (e p)", e=2)).then_inc(ssm_in, 16)
        act.dma_start(log_dt_rows[:], a["log_dt"][0].rearrange("d (q e) -> (d q) e", e=2)).then_inc(ssm_in, 16)
        for i, name in enumerate(("b_re", "b_im")):
            for d in range(2):
                act.dma_start(b_raw[:, i, d, :, :],
                              a[name][0, d].rearrange("(q e) p c -> (e p) q c", e=2)).then_inc(ssm_in, 16)
        for i, name in enumerate(("c_re", "c_im")):
            for twice in range(2):
                act.dma_start(c_rows[:, i, :, twice, :],
                              a[name][0].rearrange("(b g) c p -> (g c) b p", b=3)).then_inc(ssm_in, 16)
        act.dma_start(dskip_rows[:], a["d_skip"][0].rearrange("(g c) -> g c", c=GC)).then_inc(ssm_in, 16)
        wide = 2 * D_FF // P
        for i, src in enumerate((a["conv_w"][0, 0], a["conv_w"][0, 1])):
            act.dma_start(vec_rows[0][wide * i:wide * (i + 1), :], src.rearrange("(f p) -> f p", p=P)).then_inc(vec_in, 16)
        for i, src in enumerate((a["conv_w"][0, 2], a["conv_b"][0])):
            act.dma_start(vec_rows[1][wide * i:wide * (i + 1), :], src.rearrange("(f p) -> f p", p=P)).then_inc(vec_in, 16)
        for i, name in enumerate(("g_pre_mix", "g_pre_ffn")):
            at_row = 2 * wide + KD * i
            act.dma_start(vec_rows[0][at_row:at_row + KD, :], a[name][0].rearrange("(k p) -> k p", p=P)).then_inc(vec_in, 16)
        x = a["x"][0].rearrange("(n p) d -> p n d", p=P)
        for n in range(NT):
            act.dma_start(x_rows[:, n, :], x[:, n, :]).then_inc(x_in, 16)
        act.dma_start(row_a[:], a["g_post_mix"].to_broadcast([P, D])).then_inc(bc_in, 16)
        act.dma_start(row_b[:], a["g_post_ffn"].to_broadcast([P, D])).then_inc(bc_in, 16)
        act.dma_start(sink_row[:], a["sink"].to_broadcast([P, Q_HEADS])).then_inc(bc_in, 16)

        act.wait_ge(prm_angle, 1)
        nc.scalar.activation(prm[:, 10, :], prm[:, 7, :], ACT.Sin).then_inc(prm_trig, 1)
        nc.scalar.activation(prm[:, 11, :], prm[:, 7, :], ACT.Sin, scale=0.5).then_inc(prm_trig, 1)

        act.wait_ge(x_in, 16 * NT)
        for n in range(NT):
            if n:
                act.wait_ge(x_sq, n)
            nc.scalar.activation(junk[:], x_rows[:, n, :], ACT.Square, accum_out=stat_a[:, n:n + 1]).then_inc(x_sq, 1)
        for i in range(12):
            act.wait_ge(win_turned, i + 1)
            ri, d, q = i // 6, i // 3 % 2, 4 * (i % 3)
            nc.scalar.copy(state_in[:, ri, d, q:q + 4, :], bank(4 + i % 2).rearrange("p (q m) -> p q m", q=4)).then_inc(win_ready, 1)
        act.wait_ge(x_var, 1)
        nc.scalar.activation(stat_b[:, 0:NT], stat_a[:, NT:2 * NT], ACT.Sqrt).then_inc(x_std, 1)
        act.wait_ge(mod_ready, 1)
        for i in range(2 * KD):
            k, half = i // 2, i % 2
            act.wait_ge(x_turned, i + 1)
            nc.scalar.activation(h_t[:, k, HALF * half:HALF * (half + 1)], bank(i % 2), ACT.Identity,
                                 scale=mod_cols[:, 1, k:k + 1], bias=mod_cols[:, 0, k:k + 1]).then_inc(h_ready, 1)
        for n, (_, dst) in enumerate(win_units):
            act.wait_ge(win_mm, n + 1)
            nc.scalar.copy(dst, psum[:, 2 * HALF * (1 + n % 3):2 * HALF * (2 + n % 3)]).then_inc(z_ready, 1)
        mix_scalar(act, steps)

    def inverse_root(v, steps, var):
        root, y = stat_b[:, 0:NT], stat_b[:, NT:2 * NT]
        steps.add(v.reciprocal(y, root))
        steps.settle()
        steps.add(v.tensor_tensor(root, y, y, ALU.mult))
        steps.settle()
        steps.add(v.tensor_tensor(root, root, var, ALU.mult))
        steps.settle()
        steps.add(v.tensor_scalar(root, root, -0.5, 1.5, ALU.mult, ALU.add))
        steps.settle()
        steps.add(v.tensor_tensor(y, y, root, ALU.mult))
        steps.settle()

    def x_norm(dve, v, steps):
        dve.wait_ge(x_sq, NT)
        steps.add(v.tensor_scalar(stat_a[:, NT:2 * NT], stat_a[:, 0:NT], 1.0 / D, RMS_EPS, ALU.mult, ALU.add))
        steps.settle()
        dve.sem_inc(x_var, 1)
        dve.wait_ge(x_std, 1)
        inverse_root(v, steps, stat_a[:, NT:2 * NT])
        for n in range(NT):
            v.tensor_scalar(x_rows[:, n, :], x_rows[:, n, :], stat_b[:, NT + n:NT + n + 1], None, ALU.mult).then_inc(x_scaled, 1)


    @block.vector
    def _(dve):
        steps = Steps(dve, dve_steps)
        v = nc.vector
        v.memset(ones_row[:], 1.0).then_inc(c_spread, 1)
        dve.wait_ge(small_in, 16)
        v.tensor_copy(c_bcast[:], c_cols[:].unsqueeze(2).to_broadcast([P, KD, P])).then_inc(c_spread, 1)
        dve.wait_ge(ssm_in, 16 * 12)
        v.tensor_copy(lam_rows[:, 2, :].rearrange("r (e p) -> r e p", e=2),
                      log_dt_rows[:].unsqueeze(2).to_broadcast([GROUPS, 2, STATE])).then_inc(dt_spread, 1)
        dve.wait_ge(rows_turned, 1)
        wide = 2 * D_FF // P
        for i in range(4):
            src = bank(2 + i // 2, wide, wide * (i % 2)).rearrange("p (g f) -> p f g", g=2)
            steps.add(v.tensor_copy(conv_cols[:, :, :, i], src))
        steps.add(v.tensor_copy(norm_cols[:].rearrange("p a k -> p (a k)"), bank(2, 2 * KD, 2 * wide)))
        steps.settle()
        dve.sem_inc(vec_used, 1)
        dve.wait_ge(c_turned, 2)
        steps.add(v.memset(c_pad[:], 0.0))
        steps.settle()
        for e in range(2):
            half = slice(STATE * e, STATE * (e + 1))
            for i, sign in enumerate((1.0, -1.0)):
                src = bank(4 + i, GROUPS * GC)[half].rearrange("p (q e c) -> p q e c", e=2, c=GC)[:, :, e, :]
                steps.add(v.tensor_scalar(c_plain[half, i], src, sign, None, ALU.mult))
                steps.add(v.tensor_scalar(c_pad[half, i, :, e, :], src, sign, None, ALU.mult))
        steps.settle()
        dve.sem_inc(c_ready, 2)
        dve.wait_ge(lam_turned, 1)
        steps.add(v.tensor_copy(dskip_cols[:], bank(7, GROUPS, 96)[0:GC]))
        steps.add(v.tensor_copy(prm[:, 0:3, :], bank(7, 96).rearrange("p (a c) -> p a c", a=3)[:, :, 0:2 * PAIRS]))
        steps.settle()
        col = lambda i: prm[:, i, :]

        def exponential(dst, src, t0, t1, t_int):
            one = steps.add
            one(v.tensor_scalar(t0, src, -87.0, 88.0, ALU.max, ALU.min))
            steps.settle()
            one(v.tensor_scalar(t1, t0, 1 / math.log(2), ROUND, ALU.mult, ALU.add))
            steps.settle()
            one(v.tensor_scalar(t1, t1, -ROUND, None, ALU.add))
            steps.settle()
            one(v.scalar_tensor_tensor(t0, t1, -LN2_HI, t0, ALU.mult, ALU.add))
            one(v.tensor_scalar(t_int, t1, 127.0, None, ALU.add))
            steps.settle()
            one(v.scalar_tensor_tensor(t0, t1, -LN2_LO, t0, ALU.mult, ALU.add))
            one(v.tensor_scalar(t_int, t_int, 23, None, ALU.logical_shift_left))
            steps.settle()
            one(v.tensor_scalar(dst, t0, 1 / math.factorial(8), 1 / math.factorial(7), ALU.mult, ALU.add))
            for n in range(6, -1, -1):
                steps.settle()
                one(v.tensor_tensor(dst, dst, t0, ALU.mult))
                steps.settle()
                one(v.tensor_scalar(dst, dst, 1 / math.factorial(n), None, ALU.add))
            steps.settle()
            one(v.tensor_tensor(dst, dst, t_int.bitcast(F32), ALU.mult))
            steps.settle()

        exponential(col(3), col(2), col(22), col(23), prm_int[:])
        steps.add(v.tensor_tensor(col(4), col(0), col(3), ALU.mult))
        steps.add(v.tensor_tensor(col(5), col(1), col(3), ALU.mult))
        steps.settle()
        steps.add(v.tensor_scalar(col(6), col(5), 1 / (2 * math.pi), ROUND, ALU.mult, ALU.add))
        steps.settle()
        steps.add(v.tensor_scalar(col(6), col(6), -ROUND, None, ALU.add))
        steps.settle()
        steps.add(v.scalar_tensor_tensor(col(7), col(6), -TWO_PI_HI, col(5), ALU.mult, ALU.add))
        steps.settle()
        steps.add(v.scalar_tensor_tensor(col(7), col(6), -TWO_PI_LO, col(7), ALU.mult, ALU.add))
        steps.settle()
        v.tensor_scalar(col(7), col(7), PI_DOWN, -PI_DOWN, ALU.min, ALU.max).then_inc(prm_angle, 1)
        exponential(col(8), col(4), col(22), col(23), prm_int[:])
        steps.add(v.tensor_tensor(col(9), col(8), col(8), ALU.mult))
        for _ in range(2):
            steps.settle()
            steps.add(v.tensor_tensor(col(9), col(9), col(9), ALU.mult))
        dve.wait_ge(prm_trig, 2)
        steps.add(v.tensor_tensor(col(12), col(11), col(11), ALU.mult))
        steps.settle()
        steps.add(v.tensor_scalar(col(12), col(12), -2.0, 1.0, ALU.mult, ALU.add))
        steps.add(v.tensor_tensor(col(14), col(8), col(10), ALU.mult))
        steps.settle()
        steps.add(v.tensor_tensor(col(13), col(8), col(12), ALU.mult))
        steps.settle()
        dve.sem_inc(prm_lam, 1)
        steps.add(v.tensor_tensor(col(15), col(0), col(0), ALU.mult))
        steps.add(v.tensor_tensor(col(16), col(1), col(1), ALU.mult))
        steps.add(v.tensor_scalar(col(17), col(13), -1.0, None, ALU.add))
        steps.settle()
        steps.add(v.tensor_tensor(col(15), col(15), col(16), ALU.add))
        steps.add(v.tensor_tensor(col(18), col(17), col(0), ALU.mult))
        steps.add(v.tensor_tensor(col(19), col(14), col(1), ALU.mult))
        steps.add(v.tensor_tensor(col(20), col(14), col(0), ALU.mult))
        steps.add(v.tensor_tensor(col(21), col(17), col(1), ALU.mult))
        steps.settle()
        steps.add(v.reciprocal(col(15), col(15)))
        steps.add(v.tensor_tensor(col(18), col(18), col(19), ALU.add))
        steps.add(v.tensor_tensor(col(20), col(20), col(21), ALU.subtract))
        steps.settle()
        steps.add(v.tensor_tensor(col(18), col(18), col(15), ALU.mult))
        steps.add(v.tensor_tensor(col(20), col(20), col(15), ALU.mult))
        steps.settle()

        def spread(i, d):
            return prm[:, i, PAIRS * d:PAIRS * (d + 1)].unsqueeze(2).to_broadcast([P, PAIRS, GC])

        def complex_step(dst, src, re, im):
            for d in range(2):
                t = w_tmp[:, d]
                sr, si = src[d]
                steps.add(v.tensor_tensor(t[:, 0], sr, spread(re, d), ALU.mult))
                steps.add(v.tensor_tensor(t[:, 1], si, spread(im, d), ALU.mult))
                steps.add(v.tensor_tensor(t[:, 2], sr, spread(im, d), ALU.mult))
                steps.add(v.tensor_tensor(t[:, 3], si, spread(re, d), ALU.mult))
            steps.settle()
            for d in range(2):
                t = w_tmp[:, d]
                dr, di = dst[d]
                steps.add(v.tensor_tensor(dr, t[:, 0], t[:, 1], ALU.subtract))
                steps.add(v.tensor_tensor(di, t[:, 2], t[:, 3], ALU.add))
            steps.settle()

        def modulation_used(j):
            dve.wait_ge(ada_mm, j + 1)
            part, half = j // 2, j % 2
            ps = bank(j % 2)
            if part in (2, 5):
                row = row_a if part == 2 else row_b
                cols = slice(HALF * half, HALF * (half + 1))
                v.tensor_tensor(row[:, cols], row[:, cols], ps, ALU.mult).then_inc(ada_used, 1)
                return
            kind = {0: 0, 1: 1, 3: 2, 4: 3}[part]
            for k in range(4):
                kk = 4 * half + k
                dst = stat_c[:, kk:kk + 1] if kind % 2 else mod_cols[:, kind, kk:kk + 1]
                ins = v.tensor_tensor_reduce(junk2[:], ps[:, P * k:P * (k + 1)], ident[:], 1.0, 0.0, ALU.mult, ALU.add, dst)
                if k < 3:
                    steps.add(ins)
                    steps.settle()
            ins.then_inc(ada_used, 1)
            dve.wait_ge(ada_used, j + 1)
            if kind % 2 and half == 1:
                steps.add(v.scalar_tensor_tensor(mod_cols[:, kind, :], stat_c[:, 0:KD], 1.0,
                                                 norm_cols[:, kind // 2, :], ALU.add, ALU.mult))
                steps.settle()

        dve.wait_ge(bc_in, 48)
        def lam_b_at(k):
            return [(lam_b[:, 0, d, :, s, :], lam_b[:, 1, d, :, s, :]) for d, s in ((0, CH - 1 - k), (1, k))]

        complex_step(lam_b_at(0), [(b_raw[:, 0, d], b_raw[:, 1, d]) for d in range(2)], 18, 20)
        for k in range(1, CH):
            modulation_used(k - 1)
            complex_step(lam_b_at(k), lam_b_at(k - 1), 13, 14)
        modulation_used(CH - 1)
        dve.sem_inc(lam_b_ready, 1)
        def square(dr, di, sr, si):
            steps.add(v.tensor_tensor(col(22), sr, sr, ALU.mult))
            steps.add(v.tensor_tensor(col(23), si, si, ALU.mult))
            steps.add(v.scalar_tensor_tensor(col(24), sr, 2.0, si, ALU.mult, ALU.mult))
            steps.settle()
            steps.add(v.tensor_tensor(dr, col(22), col(23), ALU.subtract))
            steps.add(v.tensor_copy(di, col(24)))
            steps.settle()

        square(pw[:, 0, 1], pw[:, 1, 1], col(12), col(10))
        square(pw[:, 0, 2], pw[:, 1, 2], pw[:, 0, 1], pw[:, 1, 1])
        square(pw[:, 0, 0], pw[:, 1, 0], pw[:, 0, 2], pw[:, 1, 2])
        for m in range(6):
            square(pw[:, 0, m + 1], pw[:, 1, m + 1], pw[:, 0, m], pw[:, 1, m])
        x_norm(dve, v, steps)
        dve.wait_ge(k_mm, 1)
        taps = GROUPS * GC
        steps.add(v.memset(k_shift[:], 0.0))
        dsk = k_sum[0:GC, 0, :].rearrange("c (g o) -> c g o", g=GROUPS)
        steps.add(v.tensor_tensor(dsk, ident[0:GC, 0:GC].unsqueeze(1).to_broadcast([GC, GROUPS, GC]),
                                  dskip_cols[:].unsqueeze(2).to_broadcast([GC, GROUPS, GC]), ALU.mult))
        steps.add(v.tensor_copy(k_sum[:, 1, :], bank(7, taps)))
        steps.settle()
        steps.add(v.tensor_tensor(k_sum[0:GC, 1, :], k_sum[0:GC, 1, :], k_sum[0:GC, 0, :], ALU.add))
        steps.settle()
        dve.sem_inc(k_ready, 1)
        dve.wait_ge(k_shift_in, 16)
        v.tensor_tensor(k_sum[:, 0, :], bank(6, taps), k_shift[:], ALU.add).then_inc(k_ready, 1)

        for j in range(CH, N_ADA):
            modulation_used(j)
        dve.wait_ge(ada_used, N_ADA)
        dve.sem_inc(mod_ready, 1)
        mix_vector(dve, v, steps)

    @block.gpsimd
    def _(pool):
        steps = Steps(pool, pool_steps)
        g = nc.gpsimd
        pool.wait_ge(prm_lam, 1)
        pool.wait_ge(c_ready, 2)
        for d in range(2):
            re = prm[:, 13, PAIRS * d:PAIRS * (d + 1)].unsqueeze(2).to_broadcast([P, PAIRS, GC])
            im = prm[:, 14, PAIRS * d:PAIRS * (d + 1)].unsqueeze(2).to_broadcast([P, PAIRS, GC])
            src_r, src_n = c_plain[:, 0], c_plain[:, 1]
            for k in range(1, CH + 1):
                t = k - 1 if d == 0 else CH - k
                dst_r, dst_n = carry_out[:, d, 0, :, t, :], carry_out[:, d, 1, :, t, :]
                steps.add(g.tensor_tensor(e_tmp[:, 0], src_r, re, ALU.mult))
                steps.add(g.tensor_tensor(e_tmp[:, 1], src_n, im, ALU.mult))
                steps.add(g.tensor_tensor(e_tmp[:, 2], src_n, re, ALU.mult))
                steps.add(g.tensor_tensor(e_tmp[:, 3], src_r, im, ALU.mult))
                steps.settle()
                steps.add(g.tensor_tensor(dst_r, e_tmp[:, 0], e_tmp[:, 1], ALU.add))
                steps.add(g.tensor_tensor(dst_n, e_tmp[:, 2], e_tmp[:, 3], ALU.subtract))
                steps.settle()
                src_r, src_n = dst_r, dst_n
            pool.sem_inc(carry_ready, 1)
        mix_gpsimd(pool, steps)

    @block.tensor
    def _(pe):
        t = nc.tensor
        pe.wait_ge(ident_in, 16)
        pe.wait_ge(vec_in, 16 * 6)
        wide = 2 * D_FF // P
        t.transpose(bank(2, 2 * wide + 2 * KD), vec_rows[0][0:2 * wide + 2 * KD, :], ident[0:2 * wide + 2 * KD, 0:2 * wide + 2 * KD])
        t.transpose(bank(3, 2 * wide), vec_rows[1][0:2 * wide, :], ident[0:2 * wide, 0:2 * wide]).then_inc(rows_turned, 1)
        pe.wait_ge(ssm_in, 16 * 12)
        pe.wait_ge(dt_spread, 1)
        for i in range(3):
            t.transpose(bank(7, GROUPS, 32 * i), lam_rows[:, i, :], ident[0:GROUPS, 0:GROUPS])
        ins = t.transpose(bank(7, GROUPS, 96)[0:GC], dskip_rows[:], ident[0:GROUPS, 0:GROUPS])
        ins.then_inc(lam_turned, 1)
        for i in range(2):
            for b in range(3):
                ins = t.transpose(bank(4 + i, P, P * b), c_rows[:, i, b].rearrange("r t p -> r (t p)"), ident[:])
            ins.then_inc(c_turned, 1)

        def modulation(j):
            pe.wait_ge(ada_in[j % 2], 32 * (j // 2 + 1))
            if j >= 2:
                pe.wait_ge(ada_used, j - 1)
            for k in range(KD):
                t.matmul(bank(j % 2), c_bcast[:, k, :], ada_w[j % 2][:, k, :], start=(k == 0), stop=False)
            t.matmul(bank(j % 2), ones_row[:], ada_b[j % 2][:], start=False, stop=True).then_inc(ada_mm, 1)

        pe.wait_ge(c_spread, 2)
        for j in range(CH):
            modulation(j)
        pe.wait_ge(lam_b_ready, 1)
        pe.wait_ge(c_ready, 2)
        for d in range(2):
            for q in range(PAIRS):
                for ri in range(2):
                    ins = t.matmul(bank(6 + d, 2 * GC, 2 * GC * q), lam_b[:, ri, d, q].rearrange("p s c -> p (s c)"),
                                   c_pad[:, ri, q].rearrange("p e c -> p (e c)"), start=(ri == 0), stop=(ri == 1))
        ins.then_inc(k_mm, 1)
        for i in range(12):
            ri, d, q = i // 6, i // 3 % 2, 4 * (i % 3)
            if i >= 2:
                pe.wait_ge(win_ready, i - 1)
            for n in range(4):
                ins = t.transpose(bank(4 + i % 2, P, P * n), lam_b[:, ri, d, q + n].rearrange("p s c -> p (s c)"), ident[:])
            ins.then_inc(win_turned, 1)
        for j in range(CH, N_ADA):
            modulation(j)
        pe.wait_ge(ada_used, N_ADA)
        for i in range(2 * KD):
            k, half = i // 2, i % 2
            pe.wait_ge(x_scaled, 4 * (half + 1))
            if i >= 2:
                pe.wait_ge(h_ready, i - 1)
            for n in range(4):
                ins = t.transpose(bank(i % 2, P, P * n), x_rows[:, 4 * half + n, P * k:P * (k + 1)], ident[:])
            ins.then_inc(x_turned, 1)
        pe.wait_ge(h_ready, 2 * KD)
        pe.wait_ge(k_ready, 2)
        pe.wait_ge(win_ready, 12)
        for n in range(len(win_units)):
            pe.wait_ge(win_in[n % 3], win_counts[n])
            if n >= 3:
                pe.wait_ge(z_ready, n - 2)
            for k in range(KD):
                for half in range(2):
                    ins = t.matmul(bank(2 + 2 * (n % 3) + half), win_raw[n % 3][:, k, :], h_t[:, k, HALF * half:HALF * (half + 1)],
                                   start=(k == 0), stop=(k == KD - 1))
            ins.then_inc(win_mm, 1)
        mix_tensor(pe, t)


def constants():
    n = np.arange(SEQ, dtype=np.int64)
    turn = 2 * np.pi / SEQ * ((n[:, None] * n[None, :]) % SEQ)
    m = np.arange(HEAD, dtype=np.int64)
    turn_d = 2 * np.pi / HEAD * ((m[:, None] * m[None, :]) % HEAD)
    dft = np.stack([np.cos(turn), np.sin(turn)], 1) / 32.0
    eye2 = np.eye(2)
    dft_d = np.stack([np.kron(eye2, np.cos(turn_d)), np.kron(eye2, -np.sin(turn_d))], 1) / 8.0
    dist = np.abs(np.arange(P)[:, None] + P - np.arange(SPAN)[None, :])
    slopes = np.exp2(np.float32(-8.0) * np.arange(1, Q_HEADS + 1, dtype=np.float32) / np.float32(Q_HEADS)).astype(np.float32)
    bias = -slopes[None, :, None] * dist[:, None, :].astype(np.float32)
    bias = np.where(dist[:, None, :] <= P, bias * np.float32(8.0), np.float32(8 * NEG))
    row, col = np.arange(P)[:, None], np.arange(P)[None, :]
    return {
        "ident": np.eye(P, dtype=np.float32),
        "dft": dft.astype(np.float32),
        "dft_d": dft_d.astype(np.float32),
        "att_bias": bias.astype(np.float32),
        "causal": np.where(col <= row, 0.0, NEG).astype(np.float32),
        "upper": (row <= col).astype(np.float32),
    }


_INS = ["x", "c", "w_ada", "b_ada", "g_pre_mix", "g_post_mix", "g_pre_ffn", "g_post_ffn", "w_in", "lam_re", "lam_im",
        "log_dt", "b_re", "b_im", "c_re", "c_im", "d_skip", "w_glu", "w_fft", "sink", "w_out", "w_up", "conv_w", "conv_b",
        "w_down", "ffn1_w1_2", "ffn1_w3_2", "ffn1_w2_2", "ln1_g_2", "ln1_b_2", "w_in_2", "kv_norm_g_2", "w_uk_2",
        "w_uv_2", "gmlp_ln_g_2", "gmlp_ln_b_2", "gmlp_ws_2", "gmlp_bs_2", "w_out_2", "ln2_g_2", "ln2_b_2",
        "ffn2_w1_2", "ffn2_w3_2", "ffn2_w2_2", "ln3_g_2", "ln3_b_2"]


def kernel(**inputs):
    import concourse.bacc as bacc
    from concourse.bass_utils import run_bass_kernel_spmd

    nc = bacc.Bacc("TRN2", target_bir_lowering=False, num_devices=1)
    arrays = {name: np.ascontiguousarray(inputs[name]) for name in _INS}
    arrays.update(constants())
    arrays = {f"in_{name}": array for name, array in arrays.items()}
    a = {name[3:]: nc.dram_tensor(name, array.shape, mybir.dt.from_np(array.dtype), kind="ExternalInput").ap()
         for name, array in arrays.items()}
    out = nc.dram_tensor("out", (1, SEQ, D), F32, kind="ExternalOutput").ap()
    build(nc, a, out)
    got = run_bass_kernel_spmd(nc, [arrays], core_ids=[0])
    return got.results[0]["out"]
```

```python
from contextlib import ExitStack
import math

import numpy as np

import concourse.bass as bass
from concourse import mybir

F32 = mybir.dt.float32
F32R = mybir.dt.float32r
ACT = mybir.ActivationFunctionType
ALU = mybir.AluOpType
AX_X = mybir.AxisListType.X

P = 128
SEQ = 1024
D = 1024
KD = D // P
NT = SEQ // P
HALF = 512
D_FF = 2816
NF = D_FF // P
SSM_W, FFT_W, ATT_W = 384, 256, 384
HEAD = 64
GROUPS, STATE, GC = 24, 64, 16
PAIRS = GROUPS // 2
CH = 8
NCH = SEQ // CH
Q_HEADS, KV_HEADS = 6, 2
SPAN = 3 * P
RMS_EPS, LN_EPS = 1e-6, 1e-5
NEG = -1e30
TWO_PI_HI = 6.28125
TWO_PI_LO = 2 * math.pi - TWO_PI_HI
ROUND = 1.5 * 2 ** 23
PI_DOWN = 3.1415925
LN2_HI = 0.693359375
LN2_LO = math.log(2) - LN2_HI
I32 = mybir.dt.int32


class Steps:

    def __init__(self, engine, sem):
        self.engine, self.sem, self.n = engine, sem, 0

    def add(self, ins):
        ins.then_inc(self.sem, 1)
        self.n += 1

    def settle(self):
        self.engine.wait_ge(self.sem, self.n)


def build(nc, a, out):
    with ExitStack() as ctx:
        body(ctx, nc, a, out)


def body(ctx, nc, a, out):
    sems = {}

    def sem(name):
        if name not in sems:
            sems[name] = ctx.enter_context(nc.semaphore(name))
        return sems[name]

    KB = 1024
    CONST = (nc.sbuf_base + 63) // 64 * 64
    XR = CONST + 12096
    GR = XR + 64 * KB
    RR = GR + 88 * KB
    at = {"next": CONST}

    def place(name, shape, offset, dt=F32):
        return nc.alloc_sbuf_tensor_at(name, shape, dt, offset=offset)

    def const(name, shape):
        n = 4 * int(np.prod(shape[1:]))
        t = place(name, shape, at["next"])
        at["next"] += (n + 31) // 32 * 32
        assert at["next"] <= XR
        return t

    psum = ctx.enter_context(nc.psum_tensor("psum", [P, 8 * HALF], F32))

    def bank(b, n=HALF, at=0):
        return psum[:, b * HALF + at:b * HALF + at + n]

    ident = const("ident", [P, P])
    row_a = const("row_a", [P, D])
    row_b = const("row_b", [P, D])
    conv_cols = const("conv_cols", [P, NF, 2, 4])
    norm_cols = const("norm_cols", [P, 2, KD])
    mod_cols = const("mod_cols", [P, 4, KD])
    stat_a = const("stat_a", [P, 2 * NT])
    stat_b = const("stat_b", [P, 2 * NT])
    stat_c = const("stat_c", [P, 2 * NT])
    sink_row = const("sink_row", [P, Q_HEADS])
    ones_row = const("ones_row", [1, P])
    dskip_cols = const("dskip_cols", [GC, GROUPS])
    c_cols = const("c_cols", [P, KD])
    log_dt_rows = const("log_dt_rows", [GROUPS, 2])

    x_rows = place("x_rows", [P, NT, D], GR)
    junk = place("junk", [P, D], GR + 32 * KB)
    junk2 = place("junk2", [P, P], GR + 39 * KB + 512)
    c_plain = place("c_plain", [P, 2, PAIRS, GC], GR + 36 * KB)
    ada_w = [place(f"ada_w{i}", [P, KD, HALF], XR + 16 * KB * i) for i in range(2)]
    c_bcast = place("c_bcast", [P, KD, P], RR + 40 * KB)
    ada_b = [place(f"ada_b{i}", [1, HALF], XR + 56 * KB + 2 * KB * i) for i in range(2)]
    vec_rows = [place(f"vec_rows{i}", [P, P], RR + 512 * i) for i in range(2)]
    lam_rows = place("lam_rows", [GROUPS, 3, P], RR + KB)
    dskip_rows = place("dskip_rows", [GROUPS, GC], RR + 2 * KB + 512)
    b_raw = place("b_raw", [P, 2, 2, PAIRS, GC], RR + 28 * KB)
    c_rows = place("c_rows", [P, 2, 3, 2, STATE], RR + 31 * KB)
    w_tmp = place("w_tmp", [P, 2, 4, PAIRS, GC], RR + 34 * KB)
    e_tmp = place("e_tmp", [P, 4, PAIRS, GC], RR + 4 * KB)
    c_pad = place("c_pad", [P, 2, PAIRS, 2, GC], XR + 60 * KB)
    lam_b = place("lam_b", [P, 2, 2, PAIRS, CH, GC], XR + 32 * KB)
    k_sum = place("k_sum", [P, 2, GROUPS * GC], RR + 7 * KB)
    k_shift = place("k_shift", [P, GROUPS * GC], RR + 10 * KB)
    prm = place("prm", [P, 26, 2 * PAIRS], RR + 12 * KB)
    prm_int = place("prm_int", [P, 2 * PAIRS], RR + 15 * KB + 896, I32)
    pw = place("pw", [P, 2, 7, 2 * PAIRS], RR + 14 * KB + 512)
    toep = place("toep", [P, CH, GROUPS * GC], RR + 16 * KB)
    carry_out = place("carry_out", [P, 2, 2, PAIRS, CH, GC], GR + 40 * KB)
    state_in = place("state_in", [P, 2, 2, PAIRS, P], GR + 64 * KB)
    h_t = place("h_t", [P, KD, SEQ], XR)
    win_raw = [place(f"win_raw{i}", [P, KD, P], RR + 4 * KB * i) for i in range(3)]
    u_t = place("u_t", [P, 3, SEQ], GR)
    f_t = place("f_t", [P, 2, SEQ], GR + 12 * KB)
    q_t = place("q_t", [P, 3, SEQ], GR + 20 * KB)
    k_t = place("k_t", [P, SEQ], GR + 32 * KB)
    v_t = place("v_t", [P, SEQ], GR + 36 * KB)
    toep_dram = nc.dram_tensor("toep_dram", (2 * CH - 1, GC, GROUPS * GC), F32).ap()

    ident_in, small_in, x_in, bc_in, ssm_in = (sem(n) for n in ("ident_in", "small_in", "x_in", "bc_in", "ssm_in"))
    vec_in = sem("vec_in")
    ada_in = [sem(f"ada_in{i}") for i in range(2)]
    c_spread, dt_spread, ada_mm, ada_used = (sem(n) for n in ("c_spread", "dt_spread", "ada_mm", "ada_used"))
    rows_turned, vec_used = sem("rows_turned"), sem("vec_used")
    lam_turned, c_turned, c_ready = sem("lam_turned"), sem("c_turned"), sem("c_ready")
    prm_angle, prm_trig, prm_lam = (sem(n) for n in ("prm_angle", "prm_trig", "prm_lam"))
    lam_b_ready, win_turned, win_ready, k_mm, k_ready = (sem(n) for n in ("lam_b_ready", "win_turned", "win_ready", "k_mm", "k_ready"))
    carry_ready, k_shift_in, k_low, k_in_dram, toep_in = (sem(n) for n in ("carry_ready", "k_shift_in", "k_low", "k_in_dram", "toep_in"))
    x_sq, x_var, x_std, x_scaled, x_turned, h_ready = (sem(n) for n in ("x_sq", "x_var", "x_std", "x_scaled", "x_turned", "h_ready"))
    win_in = [sem(f"win_in{i}") for i in range(3)]
    win_mm, z_ready = sem("win_mm"), sem("z_ready")
    dve_steps, pool_steps, act_steps = sem("dve_steps"), sem("pool_steps"), sem("act_steps")
    mod_ready = sem("mod_ready")

    f0, q0, k0 = SSM_W, SSM_W + FFT_W, SSM_W + FFT_W + ATT_W
    v0 = k0 + P
    win_units = [([(f0 + P * i, P)], f_t[:, i, :]) for i in range(2)]
    win_units += [([(P * i, P)], u_t[:, i, :]) for i in range(3)]
    win_units += [([(q0 + HEAD * j, HEAD), (q0 + HEAD * (j + 3), HEAD)], q_t[:, j, :]) for j in range(3)]
    win_units += [([(k0, P)], k_t[:, :]), ([(v0, P)], v_t[:, :])]
    win_counts, landed = [], [0, 0, 0]
    for n, (cols, _) in enumerate(win_units):
        landed[n % 3] += 16 * len(cols)
        win_counts.append(landed[n % 3])

    fw_rows = place("fw_rows", [P, 2, P], RR + 40 * KB)
    dft_d = place("dft_d", [P, 2, P], RR + 41 * KB)
    fw = place("fw", [P, 2, 2, P], RR + 42 * KB)
    f_mixed = place("f_mixed", [P, NT, 2, 2, P], XR + 32 * KB)
    dft_w = [place(f"dft_w{i}", [P, SEQ], XR + 48 * KB + 4 * KB * i) for i in range(4)]
    u_rows = place("u_rows", [P, GROUPS, CH, GC], RR)
    turn = place("turn", [P, 2, PAIRS, NCH], RR)
    u_chunk = place("u_chunk", [P, GROUPS, NCH], RR + 28 * KB)
    carry = place("carry", [P, 2, 2, PAIRS, NCH + 1], XR + 32 * KB)
    rot = [place(f"rot{i}", [P, 3, NCH], XR + 56 * KB + 512 + 1536 * i) for i in range(4)]
    rot.append(place("rot4", [P, 3, NCH], GR + 17 * KB + 512))
    y_rows = place("y_rows", [P, CH, GROUPS * GC], GR + 64 * KB)
    w_glu = place("w_glu", [P, 3, SSM_W], GR + 76 * KB)
    glu_tmp = [place(f"glu_tmp{i}", [P, HALF], GR + 82 * KB + 2 * KB * i) for i in range(2)]
    y_act = place("y_act", [P, 3, NCH, CH], RR + 12 * KB)
    yc_t = place("yc_t", [P, KD, SEQ], XR)
    att_bias = place("att_bias", [P, Q_HEADS, SPAN], GR)
    v_rows = place("v_rows", [P, NT, P], GR + 9 * KB + 4608)
    probs = [place(f"probs{i}", [P, SPAN], GR + 9 * KB + 1536 * i) for i in range(3)]
    probs_t = [place(f"probs_t{i}", [P, SPAN], RR + 40 * KB + 1536 * i) for i in range(2)]
    att_max = place("att_max", [P, NT * Q_HEADS], RR + 43 * KB)
    att_sum = place("att_sum", [P, NT * Q_HEADS], RR + 43 * KB + 192)
    att_sink = place("att_sink", [P, NT * Q_HEADS], RR + 43 * KB + 384)

    fw_zero, fw_in, fw_mm, fw_ready = (sem(n) for n in ("fw_zero", "fw_in", "fw_mm", "fw_ready"))
    fm_mm, fm_ready, dft_mm, yf_mm, yf_ready = (sem(n) for n in ("fm_mm", "fm_ready", "dft_mm", "yf_mm", "yf_ready"))
    dft_in = [sem(f"dft_in{i}") for i in range(4)]
    u_turned, u_rows_ready, uc_turned, uc_ready = (sem(n) for n in ("u_turned", "u_rows_ready", "uc_turned", "uc_ready"))
    v_turned, v_ready, bias_in, glu_in = (sem(n) for n in ("v_turned", "v_ready", "bias_in", "glu_in"))
    states_mm, states_used, carry_done = (sem(n) for n in ("states_mm", "states_used", "carry_done"))
    scores_mm, max_ready, exp_ready, sink_ready, probs_ready = (sem(n) for n in ("scores_mm", "max_ready", "exp_ready", "sink_ready", "probs_ready"))
    probs_turned, probs_t_ready, att_mm, att_ready = (sem(n) for n in ("probs_turned", "probs_t_ready", "att_mm", "att_ready"))
    y_mm, y_rows_ready, y_turned, y_act_ready, glu_mm, glu_sig, glu_ready = (
        sem(n) for n in ("y_mm", "y_rows_ready", "y_turned", "y_act_ready", "glu_mm", "glu_sig", "glu_ready"))

    Z_F, Z_U, Z_Q, Z_ALL = 2, 5, 8, 10
    ITEMS = NT * Q_HEADS

    def item(i):
        n, h = i // Q_HEADS, i % Q_HEADS
        return n, h, h // 3, h % 3, range(max(n - 1, 0), min(n + 2, NT))

    def mix_sync(sp):
        sp.wait_ge(fw_zero, 1)
        for h in range(4):
            rows = slice(HEAD * (h % 2), HEAD * (h % 2 + 1))
            sp.dma_start(fw_rows[rows, h // 2, rows], a["w_fft"][0, h]).then_inc(fw_in, 16)
        sp.dma_start(dft_d[:], a["dft_d"]).then_inc(fw_in, 16)
        sp.wait_ge(win_turned, 12)
        for i in range(2 * NT):
            if i >= 4:
                sp.wait_ge(dft_mm, i - 3)
            sp.dma_start(dft_w[i % 4][:], a["dft"][P * (i // 2):P * (i // 2 + 1), i % 2, :]).then_inc(dft_in[i % 4], 16)
        sp.wait_ge(u_turned, 6)
        sp.dma_start(att_bias[:], a["att_bias"]).then_inc(bias_in, 16)
        sp.wait_ge(states_mm, NT)
        sp.dma_start(w_glu[:], a["w_glu"][0].rearrange("(k p) n -> p k n", p=P)).then_inc(glu_in, 16)
        blocks_sync(sp)

    def mix_tensor(pe, t):
        pe.wait_ge(fw_in, 16 * 5)
        pe.wait_ge(z_ready, Z_ALL)
        for pair in range(2):
            for cs in range(2):
                ins = t.matmul(bank(2, P, P * (2 * pair + cs)), dft_d[:, cs, :], fw_rows[:, pair, :], start=True, stop=True)
        ins.then_inc(fw_mm, 1)
        pe.wait_ge(fw_ready, 1)
        for n in range(NT):
            if n >= 2:
                pe.wait_ge(fm_ready, n - 1)
            for pair in range(2):
                ins = t.matmul(bank(4 + n % 2, 2 * P, 2 * P * pair), f_t[:, pair, P * n:P * (n + 1)],
                               fw[:, pair].rearrange("p c e -> p (c e)"), start=True, stop=True)
            ins.then_inc(fm_mm, 1)
        for i in range(6):
            b, sq = i // 2, i % 2
            if i >= 2:
                pe.wait_ge(u_rows_ready, i - 1)
            for s in range(4):
                ins = t.transpose(bank(6 + i % 2, P, P * s), u_t[:, b].rearrange("p (j s) -> p s j", s=CH)[:, 4 * sq + s, :], ident[:])
            ins.then_inc(u_turned, 1)
        pe.wait_ge(fm_ready, NT)
        for i in range(2 * NT):
            n, cs = i // 2, i % 2
            pe.wait_ge(dft_in[i % 4], 16 * (i // 4 + 1))
            for pair in range(2):
                for half in range(2):
                    ins = t.matmul(bank(2 * pair + half), f_mixed[:, n, pair, cs, :], dft_w[i % 4][:, HALF * half:HALF * (half + 1)],
                                   start=(i == 0), stop=(i == 2 * NT - 1))
            ins.then_inc(dft_mm, 1)
        pe.wait_ge(u_rows_ready, 6)
        for i in range(6):
            if i >= 2:
                pe.wait_ge(uc_ready, i - 1)
            for g in range(4):
                ins = t.transpose(bank(6 + i % 2, P, P * g), u_rows[:, 4 * i + g].rearrange("p s c -> p (s c)"), ident[:])
            ins.then_inc(uc_turned, 1)
        for i in range(2):
            for n in range(4):
                ins = t.transpose(bank(4 + i, P, P * n), v_t[:, P * (4 * i + n):P * (4 * i + n + 1)], ident[:])
            ins.then_inc(v_turned, 1)
        pe.wait_ge(yf_ready, 4)
        pe.wait_ge(v_ready, 2)
        pe.wait_ge(uc_ready, 6)

        def states(c):
            d, q3 = c // 4, 3 * (c % 4)
            if c >= 1:
                pe.wait_ge(states_used, c)
            for q in range(3):
                for ri in range(2):
                    for e in range(2):
                        half = slice(STATE * e, STATE * (e + 1))
                        ins = t.matmul(bank(5 + ri, NCH, NCH * q)[half], state_in[:, ri, d, q3 + q, half],
                                       u_chunk[:, 2 * (q3 + q) + e, :], start=True, stop=True)
            ins.then_inc(states_mm, 1)

        def scores(i):
            n, h, e, j, keys = item(i)
            if i >= 2:
                pe.wait_ge(max_ready, i - 1)
            rows = slice(HEAD * e, HEAD * (e + 1))
            t.matmul(bank(i % 2, P * len(keys)), q_t[rows, j, P * n:P * (n + 1)], k_t[rows, P * keys[0]:P * (keys[-1] + 1)],
                     start=True, stop=True).then_inc(scores_mm, 1)

        def turn_probs(i):
            n, h, e, j, keys = item(i)
            pe.wait_ge(probs_ready, i + 1)
            if i >= 2:
                pe.wait_ge(probs_t_ready, i - 1)
            for b in range(len(keys)):
                ins = t.transpose(bank(2 + i % 2, P, P * b), probs[i % 3][:, P * b:P * (b + 1)], ident[:])
            ins.then_inc(probs_turned, 1)

        def values(i):
            n, h, e, j, keys = item(i)
            pe.wait_ge(probs_t_ready, i + 1)
            if h == 0 and n:
                pe.wait_ge(att_ready, n)
            rows = slice(HEAD * (h % 2), HEAD * (h % 2 + 1))
            for b, key in enumerate(keys):
                ins = t.matmul(bank(4, P, P * (h // 2))[rows], v_rows[:, key, HEAD * e:HEAD * (e + 1)],
                               probs_t[i % 2][:, P * b:P * (b + 1)], start=(b == 0), stop=(b == len(keys) - 1))
            ins.then_inc(att_mm, 1)

        for i in range(ITEMS + 3):
            if i < ITEMS:
                if i % Q_HEADS == 0:
                    states(i // Q_HEADS)
                scores(i)
            if 2 <= i < ITEMS + 2:
                turn_probs(i - 2)
            if i >= 3:
                values(i - 3)
        pe.wait_ge(carry_done, NT)
        pe.wait_ge(toep_in, 16 * CH)
        for i in range(3):
            for e in range(2):
                b = 5 + e if i % 2 == 0 else (7 if e == 0 else 0)
                half = slice(STATE * e, STATE * (e + 1))
                if i == 2:
                    pe.wait_ge(y_rows_ready, e + 1)
                for q in range(4):
                    pair = 4 * i + q
                    g = 2 * pair + e
                    dst = bank(b, P, P * q)
                    t.matmul(dst, u_chunk[:, g, :], toep[:, :, GC * g:GC * (g + 1)], start=True, stop=False)
                    for d in range(2):
                        for ri in range(2):
                            ins = t.matmul(dst, carry[half, d, ri, pair, d:d + NCH],
                                           carry_out[half, d, ri, pair].rearrange("p t c -> p (t c)"),
                                           start=False, stop=(d == 1 and ri == 1))
                ins.then_inc(y_mm, 1)
        pe.wait_ge(y_rows_ready, 6)
        for i in range(6):
            tq, b = i // 3, i % 3
            if i >= 2:
                pe.wait_ge(y_act_ready, i - 1)
            for n in range(4):
                ins = t.transpose(bank(1 + i % 2, P, P * n), y_rows[:, 4 * tq + n, P * b:P * (b + 1)], ident[:])
            ins.then_inc(y_turned, 1)
        pe.wait_ge(y_act_ready, 6)
        pe.wait_ge(glu_in, 16)
        for i in range(6):
            b, half = i // 2, i % 2
            if i >= 2:
                pe.wait_ge(glu_sig, i - 1)
            for k in range(3):
                ins = t.matmul(bank(3 + i % 2), w_glu[:, k, P * b:P * (b + 1)],
                               y_act[:, k].rearrange("p j s -> p (j s)")[:, HALF * half:HALF * (half + 1)],
                               start=(k == 0), stop=(k == 2))
            ins.then_inc(glu_mm, 1)
        blocks_tensor(pe, t)

    def mix_scalar(act, steps):
        s = nc.scalar
        act.wait_ge(fw_mm, 1)
        s.copy(fw[:].rearrange("p a c e -> p (a c e)"), bank(2)).then_inc(fw_ready, 1)
        for n in range(NT):
            act.wait_ge(fm_mm, n + 1)
            s.copy(f_mixed[:, n].rearrange("p a c e -> p (a c e)"), bank(4 + n % 2)).then_inc(fm_ready, 1)
        for i in range(6):
            act.wait_ge(uc_turned, i + 1)
            s.copy(u_chunk[:, 4 * i:4 * i + 4, :], bank(6 + i % 2).rearrange("p (g j) -> p g j", g=4)).then_inc(uc_ready, 1)
        for i in range(2):
            act.wait_ge(v_turned, i + 1)
            s.copy(v_rows[:, 4 * i:4 * i + 4, :], bank(4 + i).rearrange("p (n c) -> p n c", n=4)).then_inc(v_ready, 1)
        act.wait_ge(dft_mm, 2 * NT)
        for i in range(4):
            s.copy(yc_t[:, 3 + i // 2, HALF * (i % 2):HALF * (i % 2 + 1)], bank(i)).then_inc(yf_ready, 1)

        def exponentials(i):
            n, h, e, j, keys = item(i)
            act.wait_ge(max_ready, i + 1)
            p = probs[i % 3][:, 0:P * len(keys)]
            s.activation(p, p, ACT.Exp, bias=att_max[:, i:i + 1], accum_out=att_sum[:, i:i + 1]).then_inc(exp_ready, 1)
            s.activation(att_sink[:, i:i + 1], sink_row[:, h:h + 1], ACT.Exp, bias=att_max[:, i:i + 1]).then_inc(sink_ready, 1)

        def copy_probs(i):
            n, h, e, j, keys = item(i)
            act.wait_ge(probs_turned, i + 1)
            if i >= 2:
                act.wait_ge(att_mm, i - 1)
            s.copy(probs_t[i % 2][:, 0:P * len(keys)], bank(2 + i % 2, P * len(keys))).then_inc(probs_t_ready, 1)
            if h == Q_HEADS - 1:
                pass

        for i in range(ITEMS + 4):
            if i < ITEMS:
                exponentials(i)
            if 2 <= i < ITEMS + 2:
                copy_probs(i - 2)
            if i >= 4 and (i - 4) % Q_HEADS == Q_HEADS - 1:
                n = (i - 4) // Q_HEADS
                act.wait_ge(att_mm, Q_HEADS * (n + 1))
                s.copy(yc_t[:, 5:8, P * n:P * (n + 1)], bank(4, 3 * P).rearrange("p (c q) -> p c q", c=3)).then_inc(att_ready, 1)
        for i in range(3):
            for e in range(2):
                b = 5 + e if i % 2 == 0 else (7 if e == 0 else 0)
                act.wait_ge(y_mm, 2 * i + e + 1)
                dst = y_rows[:].rearrange("p t (q e c) -> p q e t c", e=2, c=GC)
                for q in range(4):
                    ins = s.copy(dst[:, 4 * i + q, e], bank(b, P, P * q).rearrange("p (t c) -> p t c", t=CH))
                ins.then_inc(y_rows_ready, 1)
        for i in range(6):
            tq, b = i // 3, i % 3
            act.wait_ge(y_turned, i + 1)
            s.activation(y_act[:, b].rearrange("p j s -> p s j")[:, 4 * tq:4 * tq + 4, :],
                         bank(1 + i % 2).rearrange("p (s j) -> p s j", s=4), ACT.Gelu_apprx_tanh).then_inc(y_act_ready, 1)
        for i in range(6):
            act.wait_ge(glu_mm, i + 1)
            if i >= 2:
                act.wait_ge(glu_ready, i - 1)
            s.activation(glu_tmp[i % 2][:], bank(3 + i % 2), ACT.Sigmoid).then_inc(glu_sig, 1)
        blocks_scalar(act, steps)

    def mix_vector(dve, v, steps):
        steps.add(v.memset(fw_rows[:], 0.0))
        steps.settle()
        dve.sem_inc(fw_zero, 1)
        for i in range(6):
            b, sq = i // 2, i % 2
            dve.wait_ge(u_turned, i + 1)
            v.tensor_copy(u_rows[:, 8 * b:8 * b + 8, 4 * sq:4 * sq + 4, :].rearrange("p g s c -> p s g c"),
                          bank(6 + i % 2).rearrange("p (s g c) -> p s g c", s=4, g=8)).then_inc(u_rows_ready, 1)

        def turns(d):
            tr, ti = turn[:, 0], turn[:, 1]
            steps.add(v.memset(tr[:, :, 0:1], 1.0))
            steps.add(v.memset(ti[:, :, 0:1], 0.0))
            steps.settle()
            for m in range(7):
                w = 1 << m
                pr, pi = (pw[:, x, m, PAIRS * d:PAIRS * (d + 1)].unsqueeze(2).to_broadcast([P, PAIRS, w]) for x in range(2))
                halves = [r[:].rearrange("p a b -> p (a b)")[:, 0:0 + 3 * NCH] for r in rot]
                done = 0
                step = min(PAIRS, 3 * NCH // w)
                for q in range(0, PAIRS, step):
                    qs = slice(q, q + step)
                    tmp = [x[:, 0:step * w].rearrange("p (a b) -> p a b", a=step) for x in halves[:4]]
                    br, bi = pr[:, qs], pi[:, qs]
                    steps.add(v.tensor_tensor(tmp[0], tr[:, qs, 0:w], br, ALU.mult))
                    steps.add(v.tensor_tensor(tmp[1], ti[:, qs, 0:w], bi, ALU.mult))
                    steps.add(v.tensor_tensor(tmp[2], tr[:, qs, 0:w], bi, ALU.mult))
                    steps.add(v.tensor_tensor(tmp[3], ti[:, qs, 0:w], br, ALU.mult))
                    steps.settle()
                    steps.add(v.tensor_tensor(tr[:, qs, w:2 * w], tmp[0], tmp[1], ALU.subtract))
                    steps.add(v.tensor_tensor(ti[:, qs, w:2 * w], tmp[2], tmp[3], ALU.add))
                    steps.settle()

        def scan(c):
            d, q3 = c // 4, 3 * (c % 4)
            sr, si = (bank(5 + x, 3 * NCH).rearrange("p (q j) -> p q j", q=3) for x in range(2))
            tr, ti = turn[:, 0, q3:q3 + 3], turn[:, 1, q3:q3 + 3]
            back, forth = (ALU.add, ALU.subtract) if d == 0 else (ALU.subtract, ALU.add)
            dve.wait_ge(states_mm, c + 1)
            steps.add(v.tensor_tensor(rot[0][:], sr, tr, ALU.mult))
            steps.add(v.tensor_tensor(rot[1][:], si, ti, ALU.mult))
            steps.add(v.tensor_tensor(rot[2][:], si, tr, ALU.mult))
            steps.add(v.tensor_tensor(rot[3][:], sr, ti, ALU.mult))
            steps.settle()
            dve.sem_inc(states_used, 1)
            steps.add(v.tensor_tensor(rot[0][:], rot[0][:], rot[1][:], back))
            steps.add(v.tensor_tensor(rot[2][:], rot[2][:], rot[3][:], forth))
            steps.settle()
            for q in range(3):
                decay = prm[:, 9, PAIRS * d + q3 + q:PAIRS * d + q3 + q + 1].to_broadcast([P, NCH])
                for x in (0, 2):
                    src, dst = rot[x][:, q, :], rot[x + 1][:, q, :]
                    if d:
                        src, dst = src[:, ::-1], dst[:, ::-1]
                    steps.add(v.tensor_tensor_scan(dst, decay, src, 0.0, ALU.mult, ALU.add))
            steps.settle()
            steps.add(v.tensor_tensor(rot[0][:], rot[1][:], tr, ALU.mult))
            steps.add(v.tensor_tensor(rot[2][:], rot[1][:], ti, ALU.mult))
            steps.add(v.tensor_tensor(rot[4][:], rot[3][:], ti, ALU.mult))
            steps.settle()
            steps.add(v.tensor_tensor(rot[1][:], rot[3][:], tr, ALU.mult))
            dst = [carry[:, d, x, q3:q3 + 3, 1 - d:1 - d + NCH] for x in range(2)]
            steps.add(v.tensor_tensor(dst[0], rot[0][:], rot[4][:], forth))
            steps.settle()
            steps.add(v.tensor_tensor(dst[1], rot[1][:], rot[2][:], back))
            steps.settle()
            dve.sem_inc(carry_done, 1)

        def maximum(i):
            n, h, e, j, keys = item(i)
            dve.wait_ge(scores_mm, i + 1)
            if i >= 3:
                dve.wait_ge(probs_turned, i - 2)
            w = P * len(keys)
            at = P if n == 0 else 0
            steps.add(v.tensor_tensor_reduce(probs[i % 3][:, 0:w], bank(i % 2, w), att_bias[:, h, at:at + w], 1.0 / 8, NEG,
                                             ALU.add, ALU.max, att_max[:, i:i + 1]))
            steps.settle()
            v.tensor_scalar(att_max[:, i:i + 1], att_max[:, i:i + 1], sink_row[:, h:h + 1], -1.0, ALU.max, ALU.mult).then_inc(max_ready, 1)

        def normalise(i):
            n, h, e, j, keys = item(i)
            dve.wait_ge(exp_ready, i + 1)
            dve.wait_ge(sink_ready, i + 1)
            one = slice(i, i + 1)
            steps.add(v.tensor_tensor(att_sum[:, one], att_sum[:, one], att_sink[:, one], ALU.add))
            steps.settle()
            steps.add(v.reciprocal(att_sum[:, one], att_sum[:, one]))
            steps.settle()
            p = probs[i % 3][:, 0:P * len(keys)]
            v.tensor_scalar(p, p, att_sum[:, one], None, ALU.mult).then_inc(probs_ready, 1)

        dve.wait_ge(uc_turned, 6)
        dve.wait_ge(yf_ready, 4)
        steps.add(v.memset(carry[:, 0, :, :, 0:1], 0.0))
        steps.add(v.memset(carry[:, 1, :, :, NCH:NCH + 1], 0.0))
        turns(0)
        dve.wait_ge(bias_in, 16)
        for i in range(ITEMS + 1):
            if i < ITEMS:
                maximum(i)
            if i:
                normalise(i - 1)
            if i % Q_HEADS == Q_HEADS - 1:
                if i // Q_HEADS == 4:
                    turns(1)
                scan(i // Q_HEADS)
        for i in range(6):
            b, half = i // 2, i % 2
            dve.wait_ge(glu_sig, i + 1)
            v.tensor_tensor(yc_t[:, b, HALF * half:HALF * (half + 1)],
                            y_act[:, b].rearrange("p j s -> p (j s)")[:, HALF * half:HALF * (half + 1)],
                            glu_tmp[i % 2][:], ALU.mult).then_inc(glu_ready, 1)
        blocks_vector(dve, v, steps)

    def mix_gpsimd(pool, steps):
        blocks_gpsimd(pool, steps)

    x_hi = place("x_hi", [P, KD, SEQ], XR, F32R)
    x_lo = place("x_lo", [P, KD, SEQ], XR + 32 * KB, F32R)
    raw = [place(f"raw{i}", [P, SEQ], RR + 4 * KB * i) for i in range(2)]
    split_hi = [place(f"split_hi{i}", [P, SEQ], RR + 8 * KB + 8 * KB * i, F32R) for i in range(2)]
    split_lo = [place(f"split_lo{i}", [P, SEQ], RR + 12 * KB + 8 * KB * i, F32R) for i in range(2)]
    src_hi = [place(f"src_hi{i}", [P, HALF], RR + 24 * KB + 4 * KB * i, F32R) for i in range(2)]
    src_lo = [place(f"src_lo{i}", [P, HALF], RR + 26 * KB + 4 * KB * i, F32R) for i in range(2)]
    gate = [place(f"gate{i}", [P, SEQ], RR + 28 * KB + 4 * KB * i) for i in range(4)]
    split_tmp = [place(f"split_tmp{i}", [P, HALF], RR + 32 * KB + 2 * KB * i) for i in range(2)]
    sq_junk = place("sq_junk", [P, 2, HALF], RR + 36 * KB)
    y_left = place("y_left", [P, 4, 2, HALF], XR + 48 * KB)
    hidden = place("hidden", [P, NF, SEQ], GR)
    conv_now = const("conv_now", [P, 2, 2, 4])
    moments = const("moments", [P, NT, 2, 6])
    mean_var = const("mean_var", [P, NT, 2])
    res_dram = [nc.dram_tensor(f"res_dram{i}", (SEQ, D), F32).ap() for i in range(4)]
    ALPHA = 2 ** 0.25
    HN = NT // 2
    STEP = 3 * 2 * HN

    def res(n):
        return hidden[:, 2 * n:2 * n + 2, 0:HALF]

    def res_block(n, k):
        c = P * (k % 4)
        return hidden[:, 2 * n + k // 4, c:c + P]

    def y_row(n):
        return y_left[:, n] if n < HN else hidden[:, 2 * (n - HN):2 * (n - HN) + 2, HALF:SEQ]

    def y_banks(n):
        return psum[:, SEQ * (n % HN):SEQ * (n % HN + 1)].rearrange("p (c d) -> p c d", c=2)

    def scaled_row(n):
        if n < HN:
            return hidden[:, 8 + 2 * n:10 + 2 * n, HALF:SEQ]
        return hidden[:, 12 + n, :].rearrange("p (c d) -> p c d", c=2)

    def scaled_block(n, k):
        return scaled_row(n)[:, k // 4, P * (k % 4):P * (k % 4 + 1)]

    def wide(row):
        return row[:].rearrange("p (c d) -> p c d", c=2)

    MIX_STEPS = [3, 4, 5, 6, 7, 0, 1, 2]
    row_view = lambda ap: ap.rearrange("(n p) (c d) -> n p c d", p=P, c=2)
    tiles = lambda ap: ap.rearrange("(k p) (f c) -> f p k c", p=P, c=P)

    w_in = [sem(f"w_in{i}") for i in range(2)]
    w_hi, w_lo, w_mm = sem("w_hi"), sem("w_lo"), sem("w_mm")
    evac_act, evac_dve, y_used = sem("evac_act"), sem("evac_dve"), sem("y_used")
    up_act, up_prod, up_coef, up_shift = sem("up_act"), sem("up_prod"), sem("up_coef"), sem("up_shift")
    before = {"units": 0, "evac": 0, "pairs": 0, "act": 0}

    class Down:
        def __init__(self, e, kt, src, w):
            self.e, self.kt, self.src = e, kt, src
            self.w = w.rearrange("(k p) n -> k p n", p=P)
            self.order = MIX_STEPS if kt == KD else range(kt)
            self.base, self.evacs = before["units"], before["evac"]
            self.half_end, self.end = self.base + kt, self.base + 2 * kt
            before["units"] = self.end
            before["evac"] += 4 if e < 2 else 2

    class Up:
        def __init__(self, w_gate, w_val, conv):
            self.w, self.conv = (w_gate, w_val), conv
            self.base, self.pairs, self.acts = before["units"], before["pairs"], before["act"]
            self.end, self.pairs_end = self.base + 2 * NF, self.pairs + NF
            before["units"], before["pairs"] = self.end, self.pairs_end
            before["act"] += (3 if conv else 1) * NF

    down_mix = Down(0, KD, yc_t, a["w_out"][0])
    up_conv = Up(tiles(a["w_up"][0][:, 0:D_FF]), tiles(a["w_up"][0][:, D_FF:2 * D_FF]), True)
    down_conv = Down(1, NF, hidden, a["w_down"][0])
    up_1 = Up(tiles(a["ffn1_w1_2"][0]), tiles(a["ffn1_w3_2"][0]), False)
    down_1 = Down(2, NF, hidden, a["ffn1_w2_2"][0])
    down_mix2 = Down(3, KD, yc_t, a["w_out_2"][0])
    up_2 = Up(tiles(a["ffn2_w1_2"][0]), tiles(a["ffn2_w3_2"][0]), False)
    down_2 = Down(4, NF, hidden, a["ffn2_w2_2"][0])

    res_in, sq_done, var_ready, std_ready, row_ready = (sem(n) for n in ("res_in", "sq_done", "var_ready", "std_ready", "row_ready"))
    row_scaled, cols_turned, cols_tmp, cols_hi, cols_ready = (sem(n) for n in ("row_scaled", "cols_turned", "cols_tmp", "cols_hi", "cols_ready"))
    res_out, gain_in, row_centred = (sem(n) for n in ("res_out", "gain_in", "row_centred"))
    factors_ready = sem("factors_ready")
    PIECES, LATE = 8, 4


    def down_half(st, engine, step, half, skip=0):
        base = st.base + half * st.kt
        head = KD if st.kt == KD else PIECES + LATE if half else 2
        for k in range(skip, head):
            step(half, k, st.order[k], base + k, k % 2)
        if st.kt > head:
            with engine.Fori(0, (st.kt - head) // 2) as i:
                for u in range(2):
                    step(half, None, 2 * i + head + u, base + 2 * i + head + u, u)

    def down_sync(sp, st):
        def step(half, k, kk, j, slot):
            if k is None or j >= 2:
                sp.wait_ge(w_lo, j - 1)
            sp.dma_start(raw[slot][:], st.w[kk]).then_inc(w_in[slot], 16)
            if k is None or half != (st.kt > KD):
                return
            n = k - 1 if half else k
            if k == 0 and st.e:
                sp.wait_ge(res_out, 16 * NT * st.e)
            if half and k == 1:
                sp.wait_ge(w_mm, st.half_end)
            if 0 <= n < NT:
                src = row_view(a["x"][0] if st.e == 0 else res_dram[st.e - 1])
                sp.dma_start(res(n), src[n]).then_inc(res_in, 16)
        for half in range(2):
            down_half(st, sp, step, half)

    def down_scalar(act, st, skip=0):
        s = nc.scalar

        def step(half, k, kk, j, slot):
            down_split(act, st, half, k, kk, j, slot)
            if half and k is not None:
                if k == 0:
                    act.wait_ge(w_mm, st.half_end)
                    for n in range(0, HN, 2):
                        s.copy(y_row(n), y_banks(n)).then_inc(evac_act, 1)
                end_piece_scalar(act, st, k - (LATE if st.kt > KD else 0))
        for half in range(2):
            down_half(st, act, step, half, 0 if half else skip)

    def down_split(act, st, half, k, kk, j, slot):
        s = nc.scalar
        if k is None or j >= 2:
            act.wait_ge(w_mm, j - 1)
        s.copy(src_hi[slot][:], st.src[:, kk, HALF * half:HALF * (half + 1)])
        act.wait_ge(w_in[slot], (j - slot) * 8 + 16)
        s.copy(split_hi[slot][:], raw[slot][:]).then_inc(w_hi, 1)

    def down_rest(dve, st, half, k, kk, j, slot):
        v = nc.vector
        dve.wait_ge(w_hi, j + 1)
        v.tensor_tensor(src_lo[slot][:], st.src[:, kk, HALF * half:HALF * (half + 1)], src_hi[slot][:], ALU.subtract)
        v.tensor_tensor(split_lo[slot][:], raw[slot][:], split_hi[slot][:], ALU.subtract).then_inc(w_lo, 1)

    def down_vector(dve, st, steps, skip=0):
        v = nc.vector

        def step(half, k, kk, j, slot):
            down_rest(dve, st, half, k, kk, j, slot)
            if half and k is not None:
                if k == 0:
                    dve.wait_ge(w_mm, st.half_end)
                    for n in range(1, HN, 2):
                        v.tensor_copy(y_row(n), y_banks(n)).then_inc(evac_dve, 1)
                end_piece_vector(dve, v, steps, st, k - (LATE if st.kt > KD else 0))
        for half in range(2):
            down_half(st, dve, step, half, 0 if half else skip)

    def down_tensor(pe, st, up=None):
        t = nc.tensor

        def step(half, kk, j, slot, first, last):
            pe.wait_ge(w_lo, j + 1)
            for n in range(HN):
                if first and half:
                    pe.wait_ge((evac_act, evac_dve)[n % 2], st.evacs + n // 2 + 1)
                elif first and up and n % 2 == 0:
                    freed, done = up_freed(up)
                    pe.wait_ge(freed, done(NF - 1 + n // 2))
                rows = slice(P * n, P * (n + 1))
                for m, (l, r) in enumerate(((src_hi, split_hi), (src_hi, split_lo), (src_lo, split_hi))):
                    for c in range(2):
                        ins = t.matmul(bank(2 * n + c), l[slot][:, rows], r[slot][:, HALF * c:HALF * (c + 1)],
                                       start=(first and m == 0), stop=(last and m == 2))
            ins.then_inc(w_mm, 1)

        for half in range(2):
            base = st.base + half * st.kt
            step(half, st.order[0], base, 0, True, False)
            if st.kt == KD:
                for k in range(1, KD - 1):
                    step(half, st.order[k], base + k, k % 2, False, False)
            else:
                with pe.Fori(0, (st.kt - 2) // 2) as i:
                    for u in range(2):
                        step(half, None, base + 2 * i + 1 + u, 1 - u, False, False)
            step(half, None, base + st.kt - 1, 1, False, True)


    def up_freed(st):
        if st.conv:
            return up_shift, lambda p: 4 * p
        return up_prod, lambda p: st.pairs + p

    def up_pairs(engine, pair):
        with engine.Fori(0, (NF - 2) // 2) as i:
            pair(2 * i + 1, 1)
            pair(2 * i + 2, 0)
        pair(NF - 1, 1)

    def up_sync(sp, st):
        def pair(p, par):
            for u in range(2):
                sp.wait_ge(w_lo, st.base + 2 * p + u - 1)
                sp.dma_start(raw[u][:].rearrange("p (k c) -> p k c", c=P), st.w[u][p]).then_inc(w_in[u], 16)
        up_pairs(sp, pair)

    def up_first(sp, st):
        for u in range(2):
            sp.wait_ge(w_lo, st.base + u - 1)
            sp.dma_start(raw[u][:].rearrange("p (k c) -> p k c", c=P), st.w[u][0]).then_inc(w_in[u], 16)

    def up_split(act, st, p, u):
        act.wait_ge(w_mm, st.base + 2 * p + u - 1)
        act.wait_ge(w_in[u], 8 * st.base + 16 * p + 16)
        nc.scalar.copy(split_hi[u][:], raw[u][:]).then_inc(w_hi, 1)

    def up_rest(dve, st, p, u):
        dve.wait_ge(w_hi, st.base + 2 * p + u + 1)
        nc.vector.tensor_tensor(split_lo[u][:], raw[u][:], split_hi[u][:], ALU.subtract).then_inc(w_lo, 1)

    def up_taps(dve, st, p, par):
        nc.vector.tensor_copy(conv_now[:, par], conv_cols[:, p]).then_inc(up_coef, 1)

    def up_scalar(act, st, down):
        s = nc.scalar

        def finish(p, par):
            banks = 4 * (1 - par)
            act.wait_ge(w_mm, st.base + 2 * p - 1)
            if not st.conv:
                s.activation(gate[1 - par][:], psum[:, HALF * banks:HALF * (banks + 2)], ACT.Silu).then_inc(up_act, 1)
                return
            act.wait_ge(up_coef, p)
            for u in range(2):
                if u:
                    act.wait_ge(w_mm, st.base + 2 * p)
                w = conv_now[:, 1 - par, u]
                s.activation(gate[2 * (1 - par) + u][:], psum[:, HALF * (banks + 2 * u):HALF * (banks + 2 * u + 2)],
                             ACT.Identity, scale=w[:, 1:2], bias=w[:, 3:4]).then_inc(up_act, 1)

        def activate(p, par):
            act.wait_ge(up_shift, 4 * p - 2)
            s.activation(gate[2 * (1 - par)][:], gate[2 * (1 - par)][:], ACT.Gelu_apprx_tanh).then_inc(up_act, 1)

        def pair(p, par):
            up_split(act, st, p, 0)
            finish(p, par)
            up_split(act, st, p, 1)
            if st.conv:
                activate(p, par)

        up_pairs(act, pair)
        act.wait_ge(up_prod, st.pairs_end - 2)
        down_split(act, down, 0, 0, down.order[0], down.base, 0)
        finish(NF, 0)
        if st.conv:
            activate(NF, 0)
        act.wait_ge(up_prod, st.pairs_end)

    def up_vector(dve, st, down):
        v = nc.vector

        def shifts(p, par):
            for u in range(2):
                dve.wait_ge(up_act, 3 * p - 2 + u)
                b = HALF * (4 * (1 - par) + 2 * u)
                g, w = gate[2 * (1 - par) + u], conv_now[:, 1 - par, u]
                v.scalar_tensor_tensor(g[:, 1:SEQ], psum[:, b:b + SEQ - 1], w[:, 0:1], g[:, 1:SEQ], ALU.mult, ALU.add).then_inc(up_shift, 1)
                dve.wait_ge(up_shift, 4 * p - 3 + 2 * u)
                v.scalar_tensor_tensor(g[:, 0:SEQ - 1], psum[:, b + 1:b + SEQ], w[:, 2:3], g[:, 0:SEQ - 1], ALU.mult, ALU.add).then_inc(up_shift, 1)

        def product(p, par):
            b = HALF * (4 * (1 - par) + 2)
            if st.conv:
                dve.wait_ge(up_act, 3 * p)
                dve.wait_ge(up_shift, 4 * p)
                left, right = gate[2 * (1 - par)][:], gate[2 * (1 - par) + 1][:]
            else:
                dve.wait_ge(up_act, st.acts + p)
                dve.wait_ge(w_mm, st.base + 2 * p)
                left, right = gate[1 - par][:], psum[:, b:b + SEQ]
            v.tensor_tensor(hidden[:, p - 1, :], left, right, ALU.mult).then_inc(up_prod, 1)

        def pair(p, par):
            up_rest(dve, st, p, 0)
            if st.conv:
                up_taps(dve, st, p, par)
                shifts(p, par)
            else:
                product(p, par)
            up_rest(dve, st, p, 1)
            if st.conv:
                product(p, par)

        up_pairs(dve, pair)
        down_rest(dve, down, 0, 0, down.order[0], down.base, 0)
        if st.conv:
            shifts(NF, 0)
        product(NF, 0)

    def up_unit(st, p, par, u, halves):
        t = nc.tensor
        for k in range(KD):
            cols = slice(P * k, P * (k + 1))
            for m, (l, r) in enumerate(((split_hi, x_hi), (split_hi, x_lo), (split_lo, x_hi))):
                for half in halves:
                    ins = t.matmul(bank(4 * par + 2 * u + half), l[u][:, cols], r[:, k, HALF * half:HALF * (half + 1)],
                                   start=(k == 0 and m == 0), stop=(k == KD - 1 and m == 2))
        return ins

    def up_tensor(pe, st):
        freed, done = up_freed(st)

        def pair(p, par):
            for u in range(2):
                pe.wait_ge(w_lo, st.base + 2 * p + u + 1)
                up_unit(st, p, par, u, range(2)).then_inc(w_mm, 1)

        pair(1, 1)
        with pe.Fori(0, (NF - 2) // 2) as i:
            for u in range(2):
                pe.wait_ge(freed, done(2 * i + u + 1))
                pair(2 * i + 2 + u, u)


    Y_SCALE = {2: 0.5 / ALPHA, 3: 1.0 / ALPHA, 4: 0.5 / ALPHA}
    roots = {"act": 0, "dve": 0}

    def take_root(act, cols=slice(0, NT)):
        roots["act"] += 1
        act.wait_ge(var_ready, roots["act"])
        nc.scalar.activation(stat_b[:, cols], stat_a[:, NT + cols.start:NT + cols.stop], ACT.Sqrt).then_inc(std_ready, 1)

    def end_root(dve, v, steps, cols=slice(0, NT)):
        roots["dve"] += 1
        dve.sem_inc(var_ready, 1)
        dve.wait_ge(std_ready, roots["dve"])
        inverse_root(v, steps, stat_a[:, NT + cols.start:NT + cols.stop], cols)

    def norm_factors(dve, v, steps, sums, cols):
        steps.add(v.tensor_scalar(stat_a[:, NT + cols.start:NT + cols.stop], sums, 1.0 / D, RMS_EPS, ALU.mult, ALU.add))
        steps.settle()
        end_root(dve, v, steps, cols)

    def layer_factors(dve, v, steps, cols):
        steps.add(v.tensor_scalar(stat_a[:, NT + cols.start:NT + cols.stop], mean_var[:, cols, 1], LN_EPS / ALPHA ** 2, None, ALU.add))
        steps.settle()
        end_root(dve, v, steps, cols)
        steps.add(v.scalar_tensor_tensor(stat_c[:, cols], mean_var[:, cols, 0], -1.0, stat_b[:, NT + cols.start:NT + cols.stop],
                                         ALU.mult, ALU.mult))
        steps.settle()

    def rows_of(half):
        return range(HN * half, HN * (half + 1))

    def cols_of(half):
        return slice(HN * half, HN * (half + 1))

    def rstd(n):
        return stat_b[:, NT + n:NT + n + 1]

    def end_store(sp, e, half):
        dst = row_view(res_dram[e] if e < 4 else out[0])
        for n in rows_of(half):
            sp.wait_ge(row_ready, NT * e + n + 1)
            sp.dma_start(dst[n], res(n)).then_inc(res_out, 16)

    def load_gains(sp, g_name, b_name):
        sp.dma_start(row_a[:], a[g_name].to_broadcast([P, D])).then_inc(gain_in, 16)
        sp.dma_start(row_b[:], a[b_name].to_broadcast([P, D])).then_inc(gain_in, 16)

    GAINS_IN = {2: 32, 3: 96, 4: 128}
    SQUARES = {0: 0, 1: 2 * NT}

    def square_row(act, e, n, again):
        m = SQUARES[e] + (2 * HN * (n // HN) + n % HN + (HN if again else 0) if e == 0 else n)
        if again:
            act.wait_ge(row_ready, n + 1)
        if m:
            act.wait_ge(sq_done, m)
        src, dst = (res(n), stat_c[:, n:n + 1]) if again else (y_row(n), stat_a[:, n:n + 1])
        nc.scalar.activation(sq_junk[:], src, ACT.Square, accum_out=dst).then_inc(sq_done, 1)

    def end_piece_scalar(act, st, i):
        e = st.e
        if e < 2:
            if i == 0:
                act.wait_ge(evac_act, st.evacs + 2)
                act.wait_ge(evac_dve, st.evacs + 2)
                for n in (0, 1):
                    square_row(act, e, n, False)
            elif i == 1:
                for n in (2, 3):
                    square_row(act, e, n, False)
                take_root(act, cols_of(0))
            elif e == 0 and 3 <= i < 7:
                square_row(act, e, i - 3, True)
                if i == 6:
                    take_root(act, cols_of(0))
        elif i == 4:
            take_root(act, cols_of(0))
        elif i in (5, 6):
            centre(act, e, range(2 * i - 10, 2 * i - 8))

    def centre(act, e, rows):
        for n in rows:
            if n % HN == 0:
                act.wait_ge(factors_ready, 2 * (e - 2) + n // HN + 1)
            nc.scalar.activation(res(n), res(n), ACT.Identity, scale=rstd(n), bias=stat_c[:, n:n + 1]).then_inc(row_centred, 1)

    def end_piece_vector(dve, v, steps, st, i):
        e = st.e
        if e < 2:
            if i == 1:
                dve.wait_ge(sq_done, SQUARES[e] + HN)
                norm_factors(dve, v, steps, stat_a[:, cols_of(0)], cols_of(0))
            elif 2 <= i < 6:
                add_branch(dve, v, steps, e, i - 2)
            elif e == 0 and i == 6:
                dve.wait_ge(sq_done, 2 * HN)
                norm_factors(dve, v, steps, stat_c[:, cols_of(0)], cols_of(0))
            elif e == 0 and i == 7:
                scale_rows(v, 0)
        elif 0 <= i < 4:
            dve.wait_ge(res_in, 16 * (NT * e + i + 1))
            if i == 0:
                dve.wait_ge(evac_act, st.evacs + 2)
                dve.wait_ge(evac_dve, st.evacs + 2)
            steps.add(v.scalar_tensor_tensor(res(i), y_row(i), Y_SCALE[e], res(i), ALU.mult, ALU.add))
            steps.settle()
            row_moments(v, steps, i)
        elif i == 4:
            layer_factors(dve, v, steps, cols_of(0))
            dve.sem_inc(factors_ready, 1)
        elif i in (6, 7):
            gain_rows(dve, v, steps, e, range(2 * i - 12, 2 * i - 10))

    def add_branch(dve, v, steps, e, n):
        row = wide(row_a if e == 0 else row_b)
        for c in range(2):
            steps.add(v.scalar_tensor_tensor(y_row(n)[:, c], y_row(n)[:, c], rstd(n), row[:, c], ALU.mult, ALU.mult))
        steps.settle()
        dve.wait_ge(res_in, 16 * (NT * e + n + 1))
        v.tensor_tensor(res(n), res(n), y_row(n), ALU.add).then_inc(row_ready, 1)

    def scale_rows(v, half):
        for n in rows_of(half):
            v.tensor_scalar(scaled_row(n), res(n), rstd(n), None, ALU.mult).then_inc(row_scaled, 1)

    def row_moments(v, steps, n):
        for c in range(2):
            steps.add(v.bn_stats(moments[:, n, c, :], res(n)[:, c]))
        steps.settle()
        steps.add(v.bn_aggr(mean_var[:, n, :], moments[:, n].rearrange("p a b -> p (a b)")))
        steps.settle()

    def gain_rows(dve, v, steps, e, rows):
        dve.wait_ge(gain_in, GAINS_IN[e])
        for n in rows:
            dve.wait_ge(row_centred, NT * (e - 2) + n + 1)
            steps.add(v.tensor_tensor(res(n), res(n), wide(row_a), ALU.mult))
        steps.settle()
        for n in rows:
            v.tensor_tensor(res(n), res(n), wide(row_b), ALU.add).then_inc(row_ready, 1)

    def end_scalar(act, st, begin):
        s, e = nc.scalar, st.e
        if e < 2:
            act.wait_ge(w_mm, st.end)
            for n in range(HN, NT, 2):
                s.copy(y_row(n), y_banks(n)).then_inc(evac_act, 1)
        if begin:
            begin()
            upper_columns(act, e, 0)
        if e < 2:
            act.wait_ge(evac_act, st.evacs + 4)
            act.wait_ge(evac_dve, st.evacs + 4)
            for n in rows_of(1):
                square_row(act, e, n, False)
            take_root(act, cols_of(1))
            if e == 0:
                for n in rows_of(1):
                    square_row(act, e, n, True)
                take_root(act, cols_of(1))
        else:
            take_root(act, cols_of(1))
            centre(act, e, rows_of(1))
        if begin:
            upper_columns(act, e, 1)

    def end_vector(dve, v, steps, st, begin):
        e = st.e
        dve.wait_ge(w_mm, st.end)
        if e < 2:
            for n in range(HN + 1, NT, 2):
                v.tensor_copy(y_row(n), y_banks(n)).then_inc(evac_dve, 1)
        else:
            dve.wait_ge(res_in, 16 * NT * (e + 1))
            for n in rows_of(1):
                v.scalar_tensor_tensor(res(n), y_banks(n), Y_SCALE[e], res(n), ALU.mult, ALU.add).then_inc(y_used, 1)
        if begin:
            begin()
            split_columns(dve, v, e, 0)
        if e < 2:
            dve.wait_ge(evac_act, st.evacs + 4)
            dve.wait_ge(evac_dve, st.evacs + 4)
            dve.wait_ge(sq_done, SQUARES[e] + (3 * HN if e == 0 else NT))
            norm_factors(dve, v, steps, stat_a[:, cols_of(1)], cols_of(1))
            for n in rows_of(1):
                add_branch(dve, v, steps, e, n)
            if e == 0:
                dve.wait_ge(sq_done, 2 * NT)
                norm_factors(dve, v, steps, stat_c[:, cols_of(1)], cols_of(1))
                scale_rows(v, 1)
        else:
            dve.wait_ge(y_used, NT // 2 * (e - 1))
            for n in rows_of(1):
                row_moments(v, steps, n)
            layer_factors(dve, v, steps, cols_of(1))
            dve.sem_inc(factors_ready, 1)
            gain_rows(dve, v, steps, e, rows_of(1))
        if begin:
            split_columns(dve, v, e, 1)

    def column_bank(half, k):
        return bank(4 * half + k % 4)

    def upper_columns(act, e, half):
        for k in range(KD):
            i = 2 * KD * e + KD * half + k
            dst = x_hi[:, k, HALF * half:HALF * (half + 1)]
            if e == 0:
                act.wait_ge(cols_tmp, i + 1)
                nc.scalar.copy(dst, split_tmp[i % 2][:]).then_inc(cols_hi, 1)
            else:
                act.wait_ge(cols_turned, i + 1)
                nc.scalar.copy(dst, column_bank(half, k)).then_inc(cols_hi, 1)

    def split_columns(dve, v, e, half):
        dst = slice(HALF * half, HALF * (half + 1))

        def rest(k):
            i = 2 * KD * e + KD * half + k
            dve.wait_ge(cols_hi, i + 1)
            src = split_tmp[i % 2][:] if e == 0 else column_bank(half, k)
            v.tensor_tensor(x_lo[:, k, dst], src, x_hi[:, k, dst], ALU.subtract).then_inc(cols_ready, 1)
        for k in range(KD):
            if e == 0:
                i = KD * half + k
                dve.wait_ge(cols_turned, i + 1)
                if i >= 2:
                    dve.wait_ge(cols_ready, i - 1)
                v.tensor_scalar(split_tmp[i % 2][:], column_bank(half, k), mod_cols[:, 3, k:k + 1], mod_cols[:, 2, k:k + 1],
                                ALU.mult, ALU.add).then_inc(cols_tmp, 1)
                if k:
                    rest(k - 1)
            else:
                rest(k)
        if e == 0:
            rest(KD - 1)

    def end_tensor(pe, st, wait_unit, unit, unit_done):
        t, e = nc.tensor, st.e
        for half in range(2):
            if e == 0:
                pe.wait_ge(row_scaled, HN * (half + 1))
            else:
                pe.wait_ge(row_ready, NT * e + HN * (half + 1))
            for k in range(KD):
                i = 2 * KD * e + KD * half + k
                if k >= 4:
                    pe.wait_ge(cols_ready, i - 3)
                elif k % 2 == 0:
                    n = 2 * half + k // 2
                    if e < 2:
                        pe.wait_ge((evac_act, evac_dve)[n % 2], st.evacs + 3 + n // 2)
                    else:
                        pe.wait_ge(y_used, HN * (e - 2) + n + 1)
                for n in range(HN):
                    row = scaled_block(HN * half + n, k) if e == 0 else res_block(HN * half + n, k)
                    ins = t.transpose(column_bank(half, k)[:, P * n:P * (n + 1)], row, ident[:])
                ins.then_inc(cols_turned, 1)
            pe.wait_ge(cols_ready, 2 * KD * e + KD * (half + 1))
            for u in range(2):
                if half == 0:
                    wait_unit(u)
                ins = unit(u, [half])
                if half:
                    unit_done(ins)

    def end_tensor_up(pe, st, up):
        end_tensor(pe, st, lambda u: pe.wait_ge(w_lo, up.base + u + 1), lambda u, halves: up_unit(up, 0, 0, u, halves),
                   lambda ins: ins.then_inc(w_mm, 1))

    def up_begin_scalar(act, st):
        for u in range(2):
            up_split(act, st, 0, u)

    def up_begin_vector(dve, st):
        for u in range(2):
            up_rest(dve, st, 0, u)
        if st.conv:
            up_taps(dve, st, 0, 0)

    def feed_sync(sp, st, up):
        down_sync(sp, st)
        up_first(sp, up)
        for half in range(2):
            end_store(sp, st.e, half)

    def blocks_sync(sp):
        sp.wait_ge(y_mm, 6)
        feed_sync(sp, down_mix, up_conv)
        up_sync(sp, up_conv)
        feed_sync(sp, down_conv, up_1)
        load_gains(sp, "ln1_g_2", "ln1_b_2")
        up_sync(sp, up_1)
        down_sync(sp, down_1)
        mix2_first(sp)
        for half in range(2):
            end_store(sp, 2, half)
        mix2_sync(sp)
        feed_sync(sp, down_mix2, up_2)
        load_gains(sp, "ln3_g_2", "ln3_b_2")
        up_sync(sp, up_2)
        down_sync(sp, down_2)
        for half in range(2):
            end_store(sp, 4, half)
        sp.wait_ge(res_out, 16 * NT * 5)

    def blocks_scalar(act, steps):
        act.wait_ge(glu_ready, 6)
        down_scalar(act, down_mix)
        end_scalar(act, down_mix, lambda: up_begin_scalar(act, up_conv))
        up_scalar(act, up_conv, down_conv)
        down_scalar(act, down_conv, 1)
        end_scalar(act, down_conv, lambda: up_begin_scalar(act, up_1))
        up_scalar(act, up_1, down_1)
        down_scalar(act, down_1, 1)
        end_scalar(act, down_1, lambda: mix2_begin_scalar(act))
        mix2_scalar(act, steps)
        down_scalar(act, down_mix2)
        end_scalar(act, down_mix2, lambda: up_begin_scalar(act, up_2))
        up_scalar(act, up_2, down_2)
        down_scalar(act, down_2, 1)
        end_scalar(act, down_2, None)

    def blocks_vector(dve, v, steps):
        down_vector(dve, down_mix, steps)
        end_vector(dve, v, steps, down_mix, lambda: up_begin_vector(dve, up_conv))
        dve.wait_ge(res_out, 16 * NT)
        up_vector(dve, up_conv, down_conv)
        down_vector(dve, down_conv, steps, 1)
        end_vector(dve, v, steps, down_conv, lambda: up_begin_vector(dve, up_1))
        dve.wait_ge(res_out, 16 * NT * 2)
        up_vector(dve, up_1, down_1)
        down_vector(dve, down_1, steps, 1)
        end_vector(dve, v, steps, down_1, lambda: None)
        mix2_vector(dve, v, steps)
        down_vector(dve, down_mix2, steps)
        end_vector(dve, v, steps, down_mix2, lambda: up_begin_vector(dve, up_2))
        dve.wait_ge(res_out, 16 * NT * 4)
        up_vector(dve, up_2, down_2)
        down_vector(dve, down_2, steps, 1)
        end_vector(dve, v, steps, down_2, None)

    def blocks_gpsimd(pool, steps):
        mix2_gpsimd(pool, steps)

    def blocks_tensor(pe, t):
        down_tensor(pe, down_mix)
        end_tensor_up(pe, down_mix, up_conv)
        up_tensor(pe, up_conv)
        down_tensor(pe, down_conv, up_conv)
        end_tensor_up(pe, down_conv, up_1)
        up_tensor(pe, up_1)
        down_tensor(pe, down_1, up_1)
        mix2_begin_tensor(pe, t)
        mix2_tensor(pe, t)
        down_tensor(pe, down_mix2)
        end_tensor_up(pe, down_mix2, up_2)
        up_tensor(pe, up_2)
        down_tensor(pe, down_2, up_2)

    TOP = 256
    A_HEADS, I_HEADS = 8, 4
    LAT = 128
    MLP = 512
    q2, c2 = 0, A_HEADS * HEAD
    qi2 = c2 + LAT
    ki2 = qi2 + I_HEADS * HEAD
    wi2 = ki2 + HEAD
    u2 = wi2 + I_HEADS
    v2 = u2 + MLP
    qi_t = place("qi_t", [P, 2, SEQ], GR + 32 * KB)
    ki_t = place("ki_t", [P, SEQ], GR + 40 * KB)
    wi_t = place("wi_t", [I_HEADS, SEQ], GR + 44 * KB)
    lat_t = place("lat_t", [P, SEQ], GR + 48 * KB)
    q2_t = place("q2_t", [P, 4, SEQ], GR + 52 * KB)
    mlp_v_t = place("mlp_v_t", [P, 4, SEQ], GR)
    mlp_u_t = place("mlp_u_t", [P, 4, SEQ], GR + 16 * KB)
    mlp_v = place("mlp_v", [P, NT, MLP], GR + 32 * KB)
    q_abs = [place(f"q_abs{i}", [P, 4, SEQ], GR + 32 * KB * i) for i in range(2)]
    sel_at = [P * b * (b + 1) // 2 for b in range(NT + 1)]
    select = place("select", [P, sel_at[NT]], GR + 68 * KB)
    count_junk = [place(f"count_junk{i}", [P, SEQ], GR + 48 * KB + 2 * KB * i, mybir.dt.bfloat16) for i in range(2)]
    sq_two = place("sq_two", [P, D], RR + 28 * KB)
    relu_tmp = [place(f"relu_tmp{i}", [P, SEQ], RR + 28 * KB + 4 * KB * i) for i in range(2)]
    equal, ranks = (place(n, [P, SEQ], RR + 28 * KB + 4 * KB * i) for i, n in enumerate(("equal", "ranks")))
    lat = place("lat", [P, NT, LAT], RR + 24 * KB)
    lat_n_t = place("lat_n_t", [P, SEQ], RR + 40 * KB)
    kv_gain = place("kv_gain", [P, LAT], RR + 38 * KB)
    causal = place("causal", [P, P], RR + 38 * KB + 512)
    wi_rows = place("wi_rows", [P, NT, I_HEADS], RR + 39 * KB)
    limit = place("limit", [P, 6], RR + 39 * KB + 128, I32)
    trial = place("trial", [P, 6], RR + 39 * KB + 160, I32)
    keep = place("keep", [P, 6], RR + 39 * KB + 192, I32)
    bit = place("bit", [P, 2], RR + 39 * KB + 224, I32)
    counts = place("counts", [P, 6], RR + 39 * KB + 256)
    wanted = place("wanted", [P, 6], RR + 39 * KB + 288)
    one_col = place("one_col", [P, 1], RR + 39 * KB + 320)
    v_sum = place("v_sum", [P, NT], RR + 39 * KB + 352)
    v_mean_neg = place("v_mean_neg", [P, NT], RR + 39 * KB + 384)
    row_max = place("row_max", [P, NT * A_HEADS], RR + 39 * KB + 416)
    row_sum = place("row_sum", [P, NT * A_HEADS], RR + 39 * KB + 672)
    uk_raw = place("uk_raw", [P, A_HEADS, HEAD], RR)
    w_uv = place("w_uv", [P, A_HEADS, HEAD], RR + 2 * KB)
    ws_raw = place("ws_raw", [P, 8, P], RR + 4 * KB)
    ws_t = place("ws_t", [P, 8, P], RR + 8 * KB)
    bs_rows = place("bs_rows", [P, 4, P], RR + 12 * KB)
    upper = place("upper", [P, P], RR + 14 * KB)
    gm_tmp = [place(f"gm_tmp{i}", [P, 4, P], RR + 16 * KB + 2 * KB * i) for i in range(2)]
    uk_t = place("uk_t", [P, 4, LAT], RR + 36 * KB)
    p2 = [place(f"p2_{i}", [P, SEQ], XR + 32 * KB + 4 * KB * i) for i in range(3)]
    p2_t = place("p2_t", [P, NT, 4, P], XR + 44 * KB)
    o_lat = [place(f"o_lat{i}", [P, 4, P], XR + 60 * KB + 2 * KB * i) for i in range(2)]

    a_hi, a_lo, a_mm, a_evac = (sem(n) for n in ("a_hi", "a_lo", "a_mm", "a_evac"))
    a_in = [sem(f"a_in{i}") for i in range(2)]
    small2_in, lat_turned, lat_sq, lat_ready, lat_back = (sem(n) for n in ("small2_in", "lat_turned", "lat_sq", "lat_ready", "lat_back"))
    logit_mm, relu_done, score_added, bits_done, chosen, mask_ready = (
        sem(n) for n in ("logit_mm", "relu_done", "score_added", "bits_done", "chosen", "mask_ready"))
    mix2_in, mix2_turned, ws_copied, ws_ready = (sem(n) for n in ("mix2_in", "mix2_turned", "ws_copied", "ws_ready"))
    mv_turned, mv_copied, mv_mean, mv_sq, mv_scaled, mv_ready = (
        sem(n) for n in ("mv_turned", "mv_copied", "mv_mean", "mv_sq", "mv_scaled", "mv_ready"))
    sv_mm, sv_copied, gm_ready, qa_mm, qa_ready = (sem(n) for n in ("sv_mm", "sv_copied", "gm_ready", "qa_mm", "qa_ready"))
    bs_in = sem("bs_in")
    ol_mm, ol_ready, sum_ready = sem("ol_mm"), sem("ol_ready"), sem("sum_ready")

    GELU = ACT.Gelu_apprx_tanh
    a_units = [([(qi2 + P * i, P)], qi_t[:, i, :], None) for i in range(2)]
    a_units += [([(ki2, HEAD), (ki2, HEAD)], ki_t[:, :], None), ([(wi2, I_HEADS)], wi_t[:, :], None),
                ([(c2, LAT)], lat_t[:, :], None)]
    a_units += [([(q2 + P * i, P)], q2_t[:, i, :], None) for i in range(4)]
    a_units += [([(v2 + P * i, P)], mlp_v_t[:, i, :], GELU) for i in range(4)]
    a_units += [([(u2 + P * i, P)], mlp_u_t[:, i, :], GELU) for i in range(4)]
    A_UNITS = len(a_units)
    A_V = 9
    a_counts, a_landed = [], [0, 0]
    for n, (cols, _, _) in enumerate(a_units):
        a_landed[n % 2] += 16 * len(cols)
        a_counts.append(a_landed[n % 2])
    LOGITS = [(h, b) for h in range(I_HEADS) for b in range(2, NT)]
    BITS_FIRST = 20
    SEARCHED = range(2, NT)

    def width(b):
        return P * (b + 1)

    def sel(b):
        return select[:, sel_at[b]:sel_at[b + 1]]

    def a_load(sp, n):
        at_col = 0
        for c, m in a_units[n][0]:
            sp.dma_start(tile_of(raw[n % 2], P)[:, :, at_col:at_col + m],
                         a["w_in_2"][0].rearrange("(k p) n -> p k n", p=P)[:, :, c:c + m]).then_inc(a_in[n % 2], 16)
            at_col += m

    def a_width(n):
        return sum(m for _, m in a_units[n][0])

    def tile_of(buf, m):
        return buf[:].rearrange("p (k c) -> p k c", c=P)[:, :, 0:m]

    def mix2_first(sp):
        for n in range(2):
            sp.wait_ge(w_lo, down_1.end - 1 + n)
            a_load(sp, n)

    def mix2_sync(sp):
        sp.dma_start(kv_gain[:], a["kv_norm_g_2"].to_broadcast([P, LAT])).then_inc(small2_in, 16)
        sp.dma_start(causal[:], a["causal"]).then_inc(small2_in, 16)
        sp.dma_start(row_a[:, 0:MLP], a["gmlp_ln_g_2"].to_broadcast([P, MLP])).then_inc(gain_in, 16)
        sp.dma_start(row_b[:, 0:MLP], a["gmlp_ln_b_2"].to_broadcast([P, MLP])).then_inc(gain_in, 16)
        for n in range(2, A_UNITS):
            sp.wait_ge(a_lo, n - 1)
            a_load(sp, n)
        sp.wait_ge(a_lo, A_UNITS)
        sp.dma_start(uk_raw[:], a["w_uk_2"][0].rearrange("h c d -> c h d")).then_inc(mix2_in, 16)
        sp.dma_start(w_uv[:], a["w_uv_2"][0].rearrange("h c d -> c h d")).then_inc(mix2_in, 16)
        sp.dma_start(ws_raw[:], a["gmlp_ws_2"][0].rearrange("g t s -> t g s")).then_inc(mix2_in, 16)
        sp.wait_ge(a_mm, A_UNITS)
        sp.dma_start(upper[:], a["upper"]).then_inc(bs_in, 16)
        for g in range(8):
            sp.dma_start(bs_rows[HEAD * (g % 2):HEAD * (g % 2 + 1), g // 2, :],
                         a["gmlp_bs_2"][0, g:g + 1, :].to_broadcast([HEAD, P])).then_inc(bs_in, 16)
        sp.wait_ge(mv_ready, NT)
        load_gains(sp, "ln2_g_2", "ln2_b_2")
        sp.wait_ge(att_ready, 2 * NT)
        sp.wait_ge(gm_ready, NT)

    def a_unit(n, halves):
        t, m, slot = nc.tensor, a_width(n), n % 2
        for k in range(KD):
            for i, (l, r) in enumerate(((split_hi, x_hi), (split_hi, x_lo), (split_lo, x_hi))):
                for half in halves:
                    ins = t.matmul(bank(2 * slot + half)[0:m], l[slot][:, P * k:P * k + m], r[:, k, HALF * half:HALF * (half + 1)],
                                   start=(k == 0 and i == 0), stop=(k == KD - 1 and i == 2))
        return ins

    def a_split(act, n):
        m, slot = a_width(n), n % 2
        if n >= 2:
            act.wait_ge(a_mm, n - 1)
        else:
            act.wait_ge(w_mm, down_1.end)
        act.wait_ge(a_in[slot], a_counts[n])
        nc.scalar.copy(tile_of(split_hi[slot], m), tile_of(raw[slot], m)).then_inc(a_hi, 1)

    def mix2_begin_scalar(act):
        for n in range(2):
            a_split(act, n)

    def mix2_begin_tensor(pe, t):
        end_tensor(pe, down_1, lambda n: pe.wait_ge(a_lo, n + 1), a_unit, lambda ins: ins.then_inc(a_mm, 1))

    def mix2_tensor(pe, t):
        def unit(n):
            pe.wait_ge(a_lo, n + 1)
            if n >= 2:
                pe.wait_ge(a_evac, n - 1)
            a_unit(n, range(2)).then_inc(a_mm, 1)

        def turn_values(n):
            if n >= 4:
                pe.wait_ge(mv_copied, n - 3)
            for i in range(4):
                ins = t.transpose(bank(4 + n % 4, P, P * i), mlp_v_t[:, i, P * n:P * (n + 1)], ident[:])
            ins.then_inc(mv_turned, 1)

        for n in range(2, 5):
            unit(n)
        pe.wait_ge(a_evac, 4)
        for b in range(NT):
            ins = t.transpose(bank(6, I_HEADS, I_HEADS * b), wi_t[:, P * b:P * (b + 1)], ident[0:I_HEADS, 0:I_HEADS])
        ins.then_inc(lat_turned, 1)
        pe.wait_ge(a_evac, 5)
        for b in range(NT):
            ins = t.transpose(bank(4 + b // 4, P, P * (b % 4)), lat_t[:, P * b:P * (b + 1)], ident[:])
        ins.then_inc(lat_turned, 1)
        unit(5)
        pe.wait_ge(lat_ready, NT + 1)
        for i, (h, b) in enumerate(LOGITS):
            if i >= 2:
                pe.wait_ge(relu_done, i - 1)
            rows = slice(HEAD * (h % 2), HEAD * (h % 2 + 1))
            for s0 in range(0, width(b), HALF):
                n = min(HALF, width(b) - s0)
                ins = t.matmul(bank(4 + 2 * (i % 2) + s0 // HALF, n), qi_t[rows, h // 2, P * b:P * (b + 1)], ki_t[rows, s0:s0 + n],
                               start=True, stop=True)
            ins.then_inc(logit_mm, 1)
        unit(6)
        pe.wait_ge(relu_done, len(LOGITS))
        for b in range(NT):
            ins = t.transpose(bank(4 + b // 4, P, P * (b % 4)), lat[:, b, :], ident[:])
        ins.then_inc(lat_turned, 1)
        for n in range(7, A_UNITS):
            unit(n)
            if n == 13:
                pe.wait_ge(lat_back, 2)
                pe.wait_ge(a_evac, 13)
                for b in range(4):
                    turn_values(b)
            elif n == 14:
                for b in range(4, NT):
                    turn_values(b)
        pe.wait_ge(mix2_in, 16 * 3)
        pe.wait_ge(mv_copied, NT)
        for i in range(4):
            ins = t.transpose(bank(6, P, P * i), uk_raw[:, 2 * i:2 * i + 2, :].rearrange("c h d -> c (h d)"), ident[:])
        ins.then_inc(mix2_turned, 1)
        for g in range(8):
            ins = t.transpose(bank(4 + g // 4, P, P * (g % 4)), ws_raw[:, g, :], ident[:])
        ins.then_inc(mix2_turned, 1)
        pe.wait_ge(a_evac, A_UNITS)
        pe.wait_ge(ws_copied, 2)

        def queries(h):
            rows = slice(HEAD * (h % 2), HEAD * (h % 2 + 1))
            for half in range(2):
                i = 2 * h + half
                if i >= 4:
                    pe.wait_ge(qa_ready, i - 3)
                t.matmul(bank(i % 4), uk_t[rows, h // 2, :], q2_t[rows, h // 2, HALF * half:HALF * (half + 1)],
                         start=True, stop=True).then_inc(qa_mm, 1)

        for h in range(4):
            queries(h)
        pe.wait_ge(ws_ready, 1)
        for n in range(NT):
            pe.wait_ge(mv_ready, n + 1)
            if n >= 4:
                pe.wait_ge(sv_copied, n - 3)
            for g in range(8):
                ins = t.matmul(bank(4 + n % 4, P, P * (g // 2))[HEAD * (g % 2):HEAD * (g % 2 + 1)],
                               mlp_v[:, n, HEAD * g:HEAD * (g + 1)], ws_t[:, g, :], start=True, stop=True)
            ins.then_inc(sv_mm, 1)
        for h in range(4, A_HEADS):
            queries(h)

        def scores(i):
            b, h = i // A_HEADS, i % A_HEADS
            if i >= 2:
                pe.wait_ge(max_ready, ITEMS + i - 1)
            for s0 in range(0, width(b), HALF):
                n = min(HALF, width(b) - s0)
                ins = t.matmul(bank(2 * (i % 2) + s0 // HALF, n), q_abs[h // 4][:, h % 4, P * b:P * (b + 1)], lat_n_t[:, s0:s0 + n],
                               start=True, stop=True)
            ins.then_inc(scores_mm, 1)

        def turn_probs(i):
            b = i // A_HEADS
            pe.wait_ge(probs_ready, ITEMS + i + 1)
            if i:
                pe.wait_ge(probs_t_ready, ITEMS + i)
            for k in range(b + 1):
                ins = t.transpose(bank(4 + k // 4, P, P * (k % 4)), p2[i % 3][:, P * k:P * (k + 1)], ident[:])
            ins.then_inc(probs_turned, 1)

        def values(i):
            b, half = i // 2, i % 2
            pe.wait_ge(probs_t_ready, ITEMS + 4 * i + 4)
            if i:
                pe.wait_ge(ol_ready, i)
            for k in range(b + 1):
                ins = t.matmul(bank(6), lat[:, k, :], p2_t[:, k].rearrange("p h q -> p (h q)"), start=(k == 0), stop=(k == b))
            ins.then_inc(ol_mm, 1)

        def outputs(i):
            b, half = i // 2, i % 2
            pe.wait_ge(ol_ready, i + 1)
            if b and half == 0:
                pe.wait_ge(att_ready, NT + b)
            for h in range(4 * half, 4 * half + 4):
                ins = t.matmul(bank(7, P, P * (h // 2))[HEAD * (h % 2):HEAD * (h % 2 + 1)], w_uv[:, h, :], o_lat[half][:, h % 4, :],
                               start=True, stop=True)
            ins.then_inc(att_mm, 1)

        pe.wait_ge(qa_ready, 2 * A_HEADS)
        pe.wait_ge(sv_copied, NT)
        for i in range(ITEMS2 + 4):
            if i < ITEMS2:
                scores(i)
            if 2 <= i < ITEMS2 + 2:
                turn_probs(i - 2)
            if i >= 6 and (i - 6) % 4 == 0:
                values((i - 6) // 4)
            if i >= 7 and (i - 7) % 4 == 0:
                outputs((i - 7) // 4)

    ITEMS2 = NT * A_HEADS

    def mix2_scalar(act, steps):
        s = nc.scalar

        def store(n):
            m, slot = a_width(n), n % 2
            act.wait_ge(a_mm, n + 1)
            if n == 0:
                act.wait_ge(res_out, 16 * NT * 3)
            src = psum[0:m, 2 * HALF * slot:2 * HALF * (slot + 1)]
            if a_units[n][2] is None:
                s.copy(a_units[n][1], src).then_inc(a_evac, 1)
            else:
                s.activation(a_units[n][1], src, a_units[n][2]).then_inc(a_evac, 1)

        for n in range(A_UNITS):
            if n >= 2:
                a_split(act, n)
            if n:
                store(n - 1)
            if n == 5:
                act.wait_ge(lat_turned, 2)
                for b in range(NT):
                    s.activation(relu_tmp[0][:, P * b:P * (b + 1)], bank(4 + b // 4, P, P * (b % 4)), ACT.Square,
                                 accum_out=stat_a[:, b:b + 1]).then_inc(lat_sq, 1)
                take_root(act)
            elif n == 6:
                act.wait_ge(lat_sq, NT)
                for i, (h, b) in enumerate(LOGITS):
                    act.wait_ge(logit_mm, i + 1)
                    if i >= 2:
                        act.wait_ge(score_added, i - 1)
                    src = psum[:, HALF * (4 + 2 * (i % 2)):HALF * (4 + 2 * (i % 2)) + width(b)]
                    s.activation(relu_tmp[i % 2][:, 0:width(b)], src, ACT.Relu, scale=HEAD ** -0.5).then_inc(relu_done, 1)
            elif n == 7:
                act.wait_ge(lat_turned, 3)
                for i in range(2):
                    s.copy(lat_n_t[:, HALF * i:HALF * (i + 1)], bank(4 + i)).then_inc(lat_back, 1)
            elif n in (14, 15):
                for b in range(4 * (n - 14), 4 * (n - 13)):
                    act.wait_ge(mv_turned, b + 1)
                    s.activation(mlp_v[:, b, :], bank(4 + b % 4), ACT.Copy, accum_out=v_sum[:, b:b + 1]).then_inc(mv_copied, 1)
                if n == 15:
                    act.wait_ge(mv_mean, 1)
                    act.wait_ge(score_added, len(LOGITS))
                    for b in range(NT):
                        if b >= 2:
                            act.wait_ge(mv_sq, b - 1)
                        s.activation(sq_two[:, MLP * (b % 2):MLP * (b % 2 + 1)], mlp_v[:, b, :], ACT.Square,
                                     bias=v_mean_neg[:, b:b + 1], accum_out=stat_a[:, b:b + 1]).then_inc(mv_sq, 1)
        store(A_UNITS - 1)
        act.wait_ge(mix2_turned, 1)
        s.copy(uk_t[:].rearrange("p a c -> p (a c)"), bank(6)).then_inc(ws_copied, 2)
        act.wait_ge(mix2_turned, 2)
        s.copy(ws_t[:].rearrange("p g t -> p (g t)"), psum[:, 4 * HALF:6 * HALF]).then_inc(ws_copied, 1)

        def queries(h):
            for half in range(2):
                i = 2 * h + half
                act.wait_ge(qa_mm, i + 1)
                s.mul(q_abs[h // 4][:, h % 4, HALF * half:HALF * (half + 1)], bank(i % 4), HEAD ** -0.5).then_inc(qa_ready, 1)

        for h in range(4):
            queries(h)
        take_root(act)
        act.wait_ge(mv_scaled, 1)
        for n in range(NT):
            s.activation(mlp_v[:, n, :], mlp_v[:, n, :], ACT.Identity, scale=stat_b[:, NT + n:NT + n + 1],
                         bias=stat_c[:, n:n + 1]).then_inc(mv_scaled, 1)
        for n in range(NT):
            act.wait_ge(sv_mm, n + 1)
            if n >= 2:
                act.wait_ge(gm_ready, n - 1)
            s.copy(gm_tmp[n % 2][:].rearrange("p a t -> p (a t)"), bank(4 + n % 4)).then_inc(sv_copied, 1)
        for h in range(4, A_HEADS):
            queries(h)

        def exponentials(i):
            w = width(i // A_HEADS)
            act.wait_ge(max_ready, ITEMS + i + 1)
            p = p2[i % 3][:, 0:w]
            s.activation(p, p, ACT.Exp, bias=row_max[:, i:i + 1], accum_out=row_sum[:, i:i + 1]).then_inc(exp_ready, 1)

        def copy_probs(i):
            b, h = i // A_HEADS, i % A_HEADS
            act.wait_ge(probs_turned, ITEMS + i + 1)
            if h % 4 == 0 and i:
                act.wait_ge(ol_mm, i // 4)
            s.copy(p2_t[:, 0:b + 1, h % 4, :], psum[:, 4 * HALF:4 * HALF + width(b)].rearrange("p (k q) -> p k q", q=P)).then_inc(probs_t_ready, 1)

        def finish(i):
            b, half = i // 2, i % 2
            act.wait_ge(ol_mm, i + 1)
            if i >= 2:
                act.wait_ge(att_mm, ITEMS + i - 1)
            s.copy(o_lat[half][:].rearrange("p h q -> p (h q)"), bank(6)).then_inc(ol_ready, 1)
            if i % 2 == 0 and i:
                last(b - 1)

        def last(b):
            act.wait_ge(att_mm, ITEMS + 2 * b + 2)
            s.copy(yc_t[:, 0:4, P * b:P * (b + 1)], bank(7).rearrange("p (k q) -> p k q", q=P)).then_inc(att_ready, 1)

        for i in range(ITEMS2 + 4):
            if i < ITEMS2:
                exponentials(i)
            if 2 <= i < ITEMS2 + 2:
                copy_probs(i - 2)
            if i >= 6 and (i - 6) % 4 == 0:
                finish((i - 6) // 4)
        last(NT - 1)
        act.wait_ge(gm_ready, NT)
        act.wait_ge(att_ready, 2 * NT)

    def mix2_vector(dve, v, steps):
        one = steps.add
        dve.wait_ge(lat_turned, 1)
        one(v.tensor_scalar(wi_rows[:].rearrange("p n h -> p (n h)"), bank(6, NT * I_HEADS), I_HEADS ** -0.5, None, ALU.mult))
        one(v.memset(one_col[:], 1.0))
        dve.wait_ge(lat_sq, NT)
        one(v.tensor_scalar(stat_a[:, NT:2 * NT], stat_a[:, 0:NT], 1.0 / LAT, LN_EPS, ALU.mult, ALU.add))
        steps.settle()
        dve.sem_inc(lat_ready, 1)
        end_root(dve, v, steps)
        dve.wait_ge(small2_in, 32)
        for b in range(NT):
            v.scalar_tensor_tensor(lat[:, b, :], bank(4 + b // 4, P, P * (b % 4)), stat_b[:, NT + b:NT + b + 1], kv_gain[:],
                                   ALU.mult, ALU.mult).then_inc(lat_ready, 1)
        n_b = len(SEARCHED)
        for i, (h, b) in enumerate(LOGITS):
            dve.wait_ge(relu_done, i + 1)
            r, w = relu_tmp[i % 2][:, 0:width(b)], wi_rows[:, b, h:h + 1]
            if h == 0:
                v.tensor_scalar(sel(b), r, w, None, ALU.mult).then_inc(score_added, 1)
            else:
                dve.wait_ge(score_added, i - n_b + 1)
                v.scalar_tensor_tensor(sel(b), r, w, sel(b), ALU.mult, ALU.add).then_inc(score_added, 1)
        dve.wait_ge(score_added, len(LOGITS))
        for b in SEARCHED:
            diagonal = select[:, sel_at[b + 1] - P:sel_at[b + 1]]
            one(v.tensor_tensor(diagonal, diagonal, causal[:], ALU.add))
        steps.settle()
        limits = limit[:].bitcast(F32)

        def count_all(op, against):
            for j, b in enumerate(SEARCHED):
                if j >= 2:
                    dve.wait_ge(dve_steps, steps.n - 1)
                one(v.tensor_scalar(count_junk[j % 2][:, 0:width(b)], sel(b), against[j], 0.0, op, ALU.add, counts[:, j:j + 1]))

        count_all(ALU.is_ge, [0.0] * n_b)
        one(v.memset(bit[:, 0:1], 1 << 30))
        steps.settle()
        one(v.tensor_scalar(limit[:], counts[:], float(TOP), -1.0, ALU.is_lt, ALU.mult))
        steps.settle()
        per = n_b + 4

        def next_bit(i):
            done = per * i
            v.tensor_tensor(trial[:], limit[:], bit[:, 0:1].to_broadcast([P, n_b]), ALU.bitwise_xor).then_inc(bits_done, 1)
            dve.wait_ge(bits_done, done + 1)
            for j, b in enumerate(SEARCHED):
                if j >= 2:
                    dve.wait_ge(bits_done, done + j)
                v.tensor_scalar(count_junk[j % 2][:, 0:width(b)], sel(b), trial[:, j:j + 1].bitcast(F32), 0.0, ALU.is_ge, ALU.add,
                                counts[:, j:j + 1]).then_inc(bits_done, 1)
            dve.wait_ge(bits_done, done + n_b + 1)
            v.tensor_scalar(keep[:], counts[:], float(TOP), -1.0, ALU.is_ge, ALU.mult).then_inc(bits_done, 1)
            dve.wait_ge(bits_done, done + n_b + 2)
            v.tensor_tensor(keep[:], keep[:], bit[:, 0:1].to_broadcast([P, n_b]), ALU.bitwise_and).then_inc(bits_done, 1)
            dve.wait_ge(bits_done, done + n_b + 3)
            v.tensor_tensor(limit[:], limit[:], keep[:], ALU.bitwise_xor)
            v.tensor_scalar(bit[:, 0:1], bit[:, 0:1], 1, None, ALU.logical_shift_right).then_inc(bits_done, 1)
            dve.wait_ge(bits_done, done + n_b + 4)

        with dve.Fori(0, BITS_FIRST) as i:
            next_bit(i)
        dve.wait_ge(mv_sq, NT)
        one(v.tensor_scalar(stat_a[:, NT:2 * NT], stat_a[:, 0:NT], 1.0 / MLP, LN_EPS, ALU.mult, ALU.add))
        steps.settle()
        end_root(dve, v, steps)
        one(v.tensor_tensor(stat_c[:, 0:NT], v_mean_neg[:], stat_b[:, NT:2 * NT], ALU.mult))
        steps.settle()
        dve.sem_inc(mv_scaled, 1)
        with dve.Fori(BITS_FIRST, 31) as i:
            next_bit(i)
        count_all(ALU.is_gt, [limits[:, j:j + 1] for j in range(n_b)])
        steps.settle()
        one(v.tensor_scalar(wanted[:], counts[:], -1.0, float(TOP), ALU.mult, ALU.add))
        steps.settle()
        for j, b in enumerate(SEARCHED):
            eq, rank, lim = equal[:, 0:width(b)], ranks[:, 0:width(b)], limits[:, j:j + 1]
            one(v.tensor_scalar(eq, sel(b), lim, None, ALU.is_equal))
            steps.settle()
            one(v.tensor_tensor_scan(rank, one_col[:].to_broadcast([P, width(b)]), eq, 0.0, ALU.mult, ALU.add))
            steps.settle()
            one(v.scalar_tensor_tensor(eq, rank, wanted[:, j:j + 1], eq, ALU.is_le, ALU.mult))
            steps.settle()
            v.scalar_tensor_tensor(sel(b), sel(b), lim, eq, ALU.is_gt, ALU.add).then_inc(chosen, 1)
            dve.wait_ge(chosen, j + 1)

        def maximum(i):
            b = i // A_HEADS
            w = width(b)
            dve.wait_ge(scores_mm, ITEMS + i + 1)
            if i >= 3:
                dve.wait_ge(probs_turned, ITEMS + i - 2)
            if i % A_HEADS == 0:
                dve.wait_ge(mask_ready, max(b - 1, 0) + 1)
            one(v.tensor_tensor_reduce(p2[i % 3][:, 0:w], psum[:, 2 * HALF * (i % 2):2 * HALF * (i % 2) + w], sel(b), 1.0, NEG,
                                       ALU.add, ALU.max, row_max[:, i:i + 1]))
            steps.settle()
            v.tensor_scalar(row_max[:, i:i + 1], row_max[:, i:i + 1], -1.0, None, ALU.mult).then_inc(max_ready, 1)

        def reciprocal(i):
            dve.wait_ge(exp_ready, ITEMS + i + 1)
            v.reciprocal(row_sum[:, i:i + 1], row_sum[:, i:i + 1]).then_inc(sum_ready, 1)

        for i in range(ITEMS2 + 1):
            if i < ITEMS2:
                maximum(i)
            if i:
                reciprocal(i - 1)

    def mix2_gpsimd(pool, steps):
        g = nc.gpsimd
        for n in range(A_UNITS):
            m, slot = a_width(n), n % 2
            pool.wait_ge(a_hi, n + 1)
            g.tensor_tensor(tile_of(split_lo[slot], m), tile_of(raw[slot], m), tile_of(split_hi[slot], m), ALU.subtract).then_inc(a_lo, 1)
            if n == 1:
                pool.wait_ge(small2_in, 32)
                steps.add(g.memset(select[:, sel_at[1]:sel_at[1] + P], 0.0))
                steps.add(g.tensor_copy(select[:, 0:P], causal[:]))
                steps.add(g.tensor_copy(select[:, sel_at[1] + P:sel_at[2]], causal[:]))
                steps.settle()
                pool.sem_inc(mask_ready, 1)
            elif n == 15:
                pool.wait_ge(mv_copied, NT)
                g.tensor_scalar(v_mean_neg[:], v_sum[:], -1.0 / MLP, 1.0, ALU.mult, ALU.mult).then_inc(mv_mean, 1)
        pool.wait_ge(ws_copied, 3)
        pool.wait_ge(bs_in, 16 * 9)
        g.tensor_tensor(ws_t[:], ws_t[:], upper[:].unsqueeze(1).to_broadcast([P, 8, P]), ALU.mult).then_inc(ws_ready, 1)
        pool.wait_ge(gain_in, 64)
        for n in range(NT):
            pool.wait_ge(mv_scaled, n + 2)
            steps.add(g.tensor_tensor(mlp_v[:, n, :], mlp_v[:, n, :], row_a[:, 0:MLP], ALU.mult))
            steps.settle()
            g.tensor_tensor(mlp_v[:, n, :], mlp_v[:, n, :], row_b[:, 0:MLP], ALU.add).then_inc(mv_ready, 1)
        for n in range(NT):
            pool.wait_ge(sv_copied, n + 1)
            tmp = gm_tmp[n % 2]
            steps.add(g.tensor_tensor(tmp[:], tmp[:], bs_rows[:], ALU.add))
            steps.settle()
            g.tensor_tensor(yc_t[:, 4:8, P * n:P * (n + 1)], tmp[:], mlp_u_t[:, :, P * n:P * (n + 1)], ALU.mult).then_inc(gm_ready, 1)
        for j, b in enumerate(SEARCHED):
            pool.wait_ge(chosen, j + 1)
            g.tensor_scalar(sel(b), sel(b), -NEG, NEG, ALU.mult, ALU.add).then_inc(mask_ready, 1)
        for i in range(ITEMS2):
            w = width(i // A_HEADS)
            pool.wait_ge(sum_ready, i + 1)
            p = p2[i % 3][:, 0:w]
            g.tensor_scalar(p, p, row_sum[:, i:i + 1], 1.0, ALU.mult, ALU.mult).then_inc(probs_ready, 1)

    block = ctx.enter_context(nc.Block())

    N_ADA = 6 * D // HALF

    @block.sync
    def _(sp):
        sp.dma_start(c_cols[:], a["c"].rearrange("o (p k) -> (o p) k", k=KD)).then_inc(small_in, 16)
        sp.dma_start(ident[:], a["ident"]).then_inc(ident_in, 16)
        w_ada = a["w_ada"][0].rearrange("(p k) n -> p k n", k=KD)
        for j in range(N_ADA):
            if j >= 2:
                sp.wait_ge(ada_mm, j - 1)
            cols = slice(HALF * j, HALF * (j + 1))
            sp.dma_start(ada_w[j % 2][:], w_ada[:, :, cols]).then_inc(ada_in[j % 2], 16)
            sp.dma_start(ada_b[j % 2][:], a["b_ada"][:, cols]).then_inc(ada_in[j % 2], 16)
        taps = GROUPS * GC
        sp.wait_ge(k_ready, 1)
        sp.dma_start(k_shift[7 * GC:8 * GC, :], k_sum[0:GC, 1, :]).then_inc(k_shift_in, 16)
        sp.wait_ge(k_ready, 2)
        for s in range(CH):
            sp.dma_start(toep_dram[14 - s], k_sum[GC * s:GC * (s + 1), 0, :]).then_inc(k_in_dram, 16)
            if s:
                sp.dma_start(toep_dram[7 - s], k_sum[GC * s:GC * (s + 1), 1, :]).then_inc(k_in_dram, 16)
        sp.wait_ge(k_in_dram, 16 * 15)
        for s in range(CH):
            sp.dma_start(toep[GC * s:GC * (s + 1), :, :],
                         toep_dram[7 - s:15 - s].rearrange("t c n -> c t n")).then_inc(toep_in, 16)
        w_in = a["w_in"][0].rearrange("(k p) n -> p k n", p=P)
        for n, (cols, _) in enumerate(win_units):
            if n >= 3:
                sp.wait_ge(win_mm, n - 2)
            elif n == 0:
                sp.wait_ge(vec_used, 1)
            elif n == 1:
                sp.wait_ge(carry_ready, 2)
            at_col = 0
            for c, m in cols:
                sp.dma_start(win_raw[n % 3][:, :, at_col:at_col + m], w_in[:, :, c:c + m]).then_inc(win_in[n % 3], 16)
                at_col += m
        mix_sync(sp)

    @block.scalar
    def _(act):
        steps = Steps(act, act_steps)
        lam = lam_rows
        act.dma_start(lam[:, 0, :], a["lam_re"][0].rearrange("d (q e) p -> (d q) (e p)", e=2)).then_inc(ssm_in, 16)
        act.dma_start(lam[:, 1, :], a["lam_im"][0].rearrange("d (q e) p -> (d q) (e p)", e=2)).then_inc(ssm_in, 16)
        act.dma_start(log_dt_rows[:], a["log_dt"][0].rearrange("d (q e) -> (d q) e", e=2)).then_inc(ssm_in, 16)
        for i, name in enumerate(("b_re", "b_im")):
            for d in range(2):
                act.dma_start(b_raw[:, i, d, :, :],
                              a[name][0, d].rearrange("(q e) p c -> (e p) q c", e=2)).then_inc(ssm_in, 16)
        for i, name in enumerate(("c_re", "c_im")):
            for twice in range(2):
                act.dma_start(c_rows[:, i, :, twice, :],
                              a[name][0].rearrange("(b g) c p -> (g c) b p", b=3)).then_inc(ssm_in, 16)
        act.dma_start(dskip_rows[:], a["d_skip"][0].rearrange("(g c) -> g c", c=GC)).then_inc(ssm_in, 16)
        wide = 2 * D_FF // P
        for i, src in enumerate((a["conv_w"][0, 0], a["conv_w"][0, 1])):
            act.dma_start(vec_rows[0][wide * i:wide * (i + 1), :], src.rearrange("(f p) -> f p", p=P)).then_inc(vec_in, 16)
        for i, src in enumerate((a["conv_w"][0, 2], a["conv_b"][0])):
            act.dma_start(vec_rows[1][wide * i:wide * (i + 1), :], src.rearrange("(f p) -> f p", p=P)).then_inc(vec_in, 16)
        for i, name in enumerate(("g_pre_mix", "g_pre_ffn")):
            at_row = 2 * wide + KD * i
            act.dma_start(vec_rows[0][at_row:at_row + KD, :], a[name][0].rearrange("(k p) -> k p", p=P)).then_inc(vec_in, 16)
        x = a["x"][0].rearrange("(n p) d -> p n d", p=P)
        for n in range(NT):
            act.dma_start(x_rows[:, n, :], x[:, n, :]).then_inc(x_in, 16)
        act.dma_start(row_a[:], a["g_post_mix"].to_broadcast([P, D])).then_inc(bc_in, 16)
        act.dma_start(row_b[:], a["g_post_ffn"].to_broadcast([P, D])).then_inc(bc_in, 16)
        act.dma_start(sink_row[:], a["sink"].to_broadcast([P, Q_HEADS])).then_inc(bc_in, 16)

        act.wait_ge(prm_angle, 1)
        nc.scalar.activation(prm[:, 10, :], prm[:, 7, :], ACT.Sin).then_inc(prm_trig, 1)
        nc.scalar.activation(prm[:, 11, :], prm[:, 7, :], ACT.Sin, scale=0.5).then_inc(prm_trig, 1)

        act.wait_ge(x_in, 16 * NT)
        for n in range(NT):
            if n:
                act.wait_ge(x_sq, n)
            nc.scalar.activation(junk[:], x_rows[:, n, :], ACT.Square, accum_out=stat_a[:, n:n + 1]).then_inc(x_sq, 1)
        for i in range(12):
            act.wait_ge(win_turned, i + 1)
            ri, d, q = i // 6, i // 3 % 2, 4 * (i % 3)
            nc.scalar.copy(state_in[:, ri, d, q:q + 4, :], bank(4 + i % 2).rearrange("p (q m) -> p q m", q=4)).then_inc(win_ready, 1)
        act.wait_ge(x_var, 1)
        nc.scalar.activation(stat_b[:, 0:NT], stat_a[:, NT:2 * NT], ACT.Sqrt).then_inc(x_std, 1)
        act.wait_ge(mod_ready, 1)
        for i in range(2 * KD):
            k, half = i // 2, i % 2
            act.wait_ge(x_turned, i + 1)
            nc.scalar.activation(h_t[:, k, HALF * half:HALF * (half + 1)], bank(i % 2), ACT.Identity,
                                 scale=mod_cols[:, 1, k:k + 1], bias=mod_cols[:, 0, k:k + 1]).then_inc(h_ready, 1)
        for n, (_, dst) in enumerate(win_units):
            act.wait_ge(win_mm, n + 1)
            nc.scalar.copy(dst, psum[:, 2 * HALF * (1 + n % 3):2 * HALF * (2 + n % 3)]).then_inc(z_ready, 1)
        mix_scalar(act, steps)

    def inverse_root(v, steps, var, cols=slice(0, NT)):
        root, y = stat_b[:, cols], stat_b[:, NT + cols.start:NT + cols.stop]
        steps.add(v.reciprocal(y, root))
        steps.settle()
        steps.add(v.tensor_tensor(root, y, y, ALU.mult))
        steps.settle()
        steps.add(v.tensor_tensor(root, root, var, ALU.mult))
        steps.settle()
        steps.add(v.tensor_scalar(root, root, -0.5, 1.5, ALU.mult, ALU.add))
        steps.settle()
        steps.add(v.tensor_tensor(y, y, root, ALU.mult))
        steps.settle()

    def x_norm(dve, v, steps):
        dve.wait_ge(x_sq, NT)
        steps.add(v.tensor_scalar(stat_a[:, NT:2 * NT], stat_a[:, 0:NT], 1.0 / D, RMS_EPS, ALU.mult, ALU.add))
        steps.settle()
        dve.sem_inc(x_var, 1)
        dve.wait_ge(x_std, 1)
        inverse_root(v, steps, stat_a[:, NT:2 * NT])
        for n in range(NT):
            v.tensor_scalar(x_rows[:, n, :], x_rows[:, n, :], stat_b[:, NT + n:NT + n + 1], None, ALU.mult).then_inc(x_scaled, 1)


    @block.vector
    def _(dve):
        steps = Steps(dve, dve_steps)
        v = nc.vector
        v.memset(ones_row[:], 1.0).then_inc(c_spread, 1)
        dve.wait_ge(small_in, 16)
        v.tensor_copy(c_bcast[:], c_cols[:].unsqueeze(2).to_broadcast([P, KD, P])).then_inc(c_spread, 1)
        dve.wait_ge(ssm_in, 16 * 12)
        v.tensor_copy(lam_rows[:, 2, :].rearrange("r (e p) -> r e p", e=2),
                      log_dt_rows[:].unsqueeze(2).to_broadcast([GROUPS, 2, STATE])).then_inc(dt_spread, 1)
        dve.wait_ge(rows_turned, 1)
        wide = 2 * D_FF // P
        for i in range(4):
            src = bank(2 + i // 2, wide, wide * (i % 2)).rearrange("p (g f) -> p f g", g=2)
            steps.add(v.tensor_copy(conv_cols[:, :, :, i], src))
        steps.add(v.tensor_copy(norm_cols[:].rearrange("p a k -> p (a k)"), bank(2, 2 * KD, 2 * wide)))
        steps.settle()
        dve.sem_inc(vec_used, 1)
        dve.wait_ge(c_turned, 2)
        steps.add(v.memset(c_pad[:], 0.0))
        steps.settle()
        for e in range(2):
            half = slice(STATE * e, STATE * (e + 1))
            for i, sign in enumerate((1.0, -1.0)):
                src = bank(4 + i, GROUPS * GC)[half].rearrange("p (q e c) -> p q e c", e=2, c=GC)[:, :, e, :]
                steps.add(v.tensor_scalar(c_plain[half, i], src, sign, None, ALU.mult))
                steps.add(v.tensor_scalar(c_pad[half, i, :, e, :], src, sign, None, ALU.mult))
        steps.settle()
        dve.sem_inc(c_ready, 2)
        dve.wait_ge(lam_turned, 1)
        steps.add(v.tensor_copy(dskip_cols[:], bank(7, GROUPS, 96)[0:GC]))
        steps.add(v.tensor_copy(prm[:, 0:3, :], bank(7, 96).rearrange("p (a c) -> p a c", a=3)[:, :, 0:2 * PAIRS]))
        steps.settle()
        col = lambda i: prm[:, i, :]

        def exponential(dst, src, t0, t1, t_int):
            one = steps.add
            one(v.tensor_scalar(t0, src, -87.0, 88.0, ALU.max, ALU.min))
            steps.settle()
            one(v.tensor_scalar(t1, t0, 1 / math.log(2), ROUND, ALU.mult, ALU.add))
            steps.settle()
            one(v.tensor_scalar(t1, t1, -ROUND, None, ALU.add))
            steps.settle()
            one(v.scalar_tensor_tensor(t0, t1, -LN2_HI, t0, ALU.mult, ALU.add))
            one(v.tensor_scalar(t_int, t1, 127.0, None, ALU.add))
            steps.settle()
            one(v.scalar_tensor_tensor(t0, t1, -LN2_LO, t0, ALU.mult, ALU.add))
            one(v.tensor_scalar(t_int, t_int, 23, None, ALU.logical_shift_left))
            steps.settle()
            one(v.tensor_scalar(dst, t0, 1 / math.factorial(8), 1 / math.factorial(7), ALU.mult, ALU.add))
            for n in range(6, -1, -1):
                steps.settle()
                one(v.tensor_tensor(dst, dst, t0, ALU.mult))
                steps.settle()
                one(v.tensor_scalar(dst, dst, 1 / math.factorial(n), None, ALU.add))
            steps.settle()
            one(v.tensor_tensor(dst, dst, t_int.bitcast(F32), ALU.mult))
            steps.settle()

        exponential(col(3), col(2), col(22), col(23), prm_int[:])
        steps.add(v.tensor_tensor(col(4), col(0), col(3), ALU.mult))
        steps.add(v.tensor_tensor(col(5), col(1), col(3), ALU.mult))
        steps.settle()
        steps.add(v.tensor_scalar(col(6), col(5), 1 / (2 * math.pi), ROUND, ALU.mult, ALU.add))
        steps.settle()
        steps.add(v.tensor_scalar(col(6), col(6), -ROUND, None, ALU.add))
        steps.settle()
        steps.add(v.scalar_tensor_tensor(col(7), col(6), -TWO_PI_HI, col(5), ALU.mult, ALU.add))
        steps.settle()
        steps.add(v.scalar_tensor_tensor(col(7), col(6), -TWO_PI_LO, col(7), ALU.mult, ALU.add))
        steps.settle()
        v.tensor_scalar(col(7), col(7), PI_DOWN, -PI_DOWN, ALU.min, ALU.max).then_inc(prm_angle, 1)
        exponential(col(8), col(4), col(22), col(23), prm_int[:])
        steps.add(v.tensor_tensor(col(9), col(8), col(8), ALU.mult))
        for _ in range(2):
            steps.settle()
            steps.add(v.tensor_tensor(col(9), col(9), col(9), ALU.mult))
        dve.wait_ge(prm_trig, 2)
        steps.add(v.tensor_tensor(col(12), col(11), col(11), ALU.mult))
        steps.settle()
        steps.add(v.tensor_scalar(col(12), col(12), -2.0, 1.0, ALU.mult, ALU.add))
        steps.add(v.tensor_tensor(col(14), col(8), col(10), ALU.mult))
        steps.settle()
        steps.add(v.tensor_tensor(col(13), col(8), col(12), ALU.mult))
        steps.settle()
        dve.sem_inc(prm_lam, 1)
        steps.add(v.tensor_tensor(col(15), col(0), col(0), ALU.mult))
        steps.add(v.tensor_tensor(col(16), col(1), col(1), ALU.mult))
        steps.add(v.tensor_scalar(col(17), col(13), -1.0, None, ALU.add))
        steps.settle()
        steps.add(v.tensor_tensor(col(15), col(15), col(16), ALU.add))
        steps.add(v.tensor_tensor(col(18), col(17), col(0), ALU.mult))
        steps.add(v.tensor_tensor(col(19), col(14), col(1), ALU.mult))
        steps.add(v.tensor_tensor(col(20), col(14), col(0), ALU.mult))
        steps.add(v.tensor_tensor(col(21), col(17), col(1), ALU.mult))
        steps.settle()
        steps.add(v.reciprocal(col(15), col(15)))
        steps.add(v.tensor_tensor(col(18), col(18), col(19), ALU.add))
        steps.add(v.tensor_tensor(col(20), col(20), col(21), ALU.subtract))
        steps.settle()
        steps.add(v.tensor_tensor(col(18), col(18), col(15), ALU.mult))
        steps.add(v.tensor_tensor(col(20), col(20), col(15), ALU.mult))
        steps.settle()

        def spread(i, d):
            return prm[:, i, PAIRS * d:PAIRS * (d + 1)].unsqueeze(2).to_broadcast([P, PAIRS, GC])

        def complex_step(dst, src, re, im):
            for d in range(2):
                t = w_tmp[:, d]
                sr, si = src[d]
                steps.add(v.tensor_tensor(t[:, 0], sr, spread(re, d), ALU.mult))
                steps.add(v.tensor_tensor(t[:, 1], si, spread(im, d), ALU.mult))
                steps.add(v.tensor_tensor(t[:, 2], sr, spread(im, d), ALU.mult))
                steps.add(v.tensor_tensor(t[:, 3], si, spread(re, d), ALU.mult))
            steps.settle()
            for d in range(2):
                t = w_tmp[:, d]
                dr, di = dst[d]
                steps.add(v.tensor_tensor(dr, t[:, 0], t[:, 1], ALU.subtract))
                steps.add(v.tensor_tensor(di, t[:, 2], t[:, 3], ALU.add))
            steps.settle()

        def modulation_used(j):
            dve.wait_ge(ada_mm, j + 1)
            part, half = j // 2, j % 2
            ps = bank(j % 2)
            if part in (2, 5):
                row = row_a if part == 2 else row_b
                cols = slice(HALF * half, HALF * (half + 1))
                v.tensor_tensor(row[:, cols], row[:, cols], ps, ALU.mult).then_inc(ada_used, 1)
                return
            kind = {0: 0, 1: 1, 3: 2, 4: 3}[part]
            for k in range(4):
                kk = 4 * half + k
                dst = stat_c[:, kk:kk + 1] if kind % 2 else mod_cols[:, kind, kk:kk + 1]
                ins = v.tensor_tensor_reduce(junk2[:], ps[:, P * k:P * (k + 1)], ident[:], 1.0, 0.0, ALU.mult, ALU.add, dst)
                if k < 3:
                    steps.add(ins)
                    steps.settle()
            ins.then_inc(ada_used, 1)
            dve.wait_ge(ada_used, j + 1)
            if kind % 2 and half == 1:
                steps.add(v.scalar_tensor_tensor(mod_cols[:, kind, :], stat_c[:, 0:KD], 1.0,
                                                 norm_cols[:, kind // 2, :], ALU.add, ALU.mult))
                steps.settle()

        dve.wait_ge(bc_in, 48)
        def lam_b_at(k):
            return [(lam_b[:, 0, d, :, s, :], lam_b[:, 1, d, :, s, :]) for d, s in ((0, CH - 1 - k), (1, k))]

        complex_step(lam_b_at(0), [(b_raw[:, 0, d], b_raw[:, 1, d]) for d in range(2)], 18, 20)
        for k in range(1, CH):
            modulation_used(k - 1)
            complex_step(lam_b_at(k), lam_b_at(k - 1), 13, 14)
        modulation_used(CH - 1)
        dve.sem_inc(lam_b_ready, 1)
        def square(dr, di, sr, si):
            steps.add(v.tensor_tensor(col(22), sr, sr, ALU.mult))
            steps.add(v.tensor_tensor(col(23), si, si, ALU.mult))
            steps.add(v.scalar_tensor_tensor(col(24), sr, 2.0, si, ALU.mult, ALU.mult))
            steps.settle()
            steps.add(v.tensor_tensor(dr, col(22), col(23), ALU.subtract))
            steps.add(v.tensor_copy(di, col(24)))
            steps.settle()

        square(pw[:, 0, 1], pw[:, 1, 1], col(12), col(10))
        square(pw[:, 0, 2], pw[:, 1, 2], pw[:, 0, 1], pw[:, 1, 1])
        square(pw[:, 0, 0], pw[:, 1, 0], pw[:, 0, 2], pw[:, 1, 2])
        for m in range(6):
            square(pw[:, 0, m + 1], pw[:, 1, m + 1], pw[:, 0, m], pw[:, 1, m])
        x_norm(dve, v, steps)
        dve.wait_ge(k_mm, 1)
        taps = GROUPS * GC
        steps.add(v.memset(k_shift[:], 0.0))
        dsk = k_sum[0:GC, 0, :].rearrange("c (g o) -> c g o", g=GROUPS)
        steps.add(v.tensor_tensor(dsk, ident[0:GC, 0:GC].unsqueeze(1).to_broadcast([GC, GROUPS, GC]),
                                  dskip_cols[:].unsqueeze(2).to_broadcast([GC, GROUPS, GC]), ALU.mult))
        steps.add(v.tensor_copy(k_sum[:, 1, :], bank(7, taps)))
        steps.settle()
        steps.add(v.tensor_tensor(k_sum[0:GC, 1, :], k_sum[0:GC, 1, :], k_sum[0:GC, 0, :], ALU.add))
        steps.settle()
        dve.sem_inc(k_ready, 1)
        dve.wait_ge(k_shift_in, 16)
        v.tensor_tensor(k_sum[:, 0, :], bank(6, taps), k_shift[:], ALU.add).then_inc(k_ready, 1)

        for j in range(CH, N_ADA):
            modulation_used(j)
        dve.wait_ge(ada_used, N_ADA)
        dve.sem_inc(mod_ready, 1)
        mix_vector(dve, v, steps)

    @block.gpsimd
    def _(pool):
        steps = Steps(pool, pool_steps)
        g = nc.gpsimd
        pool.wait_ge(prm_lam, 1)
        pool.wait_ge(c_ready, 2)
        for d in range(2):
            re = prm[:, 13, PAIRS * d:PAIRS * (d + 1)].unsqueeze(2).to_broadcast([P, PAIRS, GC])
            im = prm[:, 14, PAIRS * d:PAIRS * (d + 1)].unsqueeze(2).to_broadcast([P, PAIRS, GC])
            src_r, src_n = c_plain[:, 0], c_plain[:, 1]
            for k in range(1, CH + 1):
                t = k - 1 if d == 0 else CH - k
                dst_r, dst_n = carry_out[:, d, 0, :, t, :], carry_out[:, d, 1, :, t, :]
                steps.add(g.tensor_tensor(e_tmp[:, 0], src_r, re, ALU.mult))
                steps.add(g.tensor_tensor(e_tmp[:, 1], src_n, im, ALU.mult))
                steps.add(g.tensor_tensor(e_tmp[:, 2], src_n, re, ALU.mult))
                steps.add(g.tensor_tensor(e_tmp[:, 3], src_r, im, ALU.mult))
                steps.settle()
                steps.add(g.tensor_tensor(dst_r, e_tmp[:, 0], e_tmp[:, 1], ALU.add))
                steps.add(g.tensor_tensor(dst_n, e_tmp[:, 2], e_tmp[:, 3], ALU.subtract))
                steps.settle()
                src_r, src_n = dst_r, dst_n
            pool.sem_inc(carry_ready, 1)
        mix_gpsimd(pool, steps)

    @block.tensor
    def _(pe):
        t = nc.tensor
        pe.wait_ge(ident_in, 16)
        pe.wait_ge(vec_in, 16 * 6)
        wide = 2 * D_FF // P
        t.transpose(bank(2, 2 * wide + 2 * KD), vec_rows[0][0:2 * wide + 2 * KD, :], ident[0:2 * wide + 2 * KD, 0:2 * wide + 2 * KD])
        t.transpose(bank(3, 2 * wide), vec_rows[1][0:2 * wide, :], ident[0:2 * wide, 0:2 * wide]).then_inc(rows_turned, 1)
        pe.wait_ge(ssm_in, 16 * 12)
        pe.wait_ge(dt_spread, 1)
        for i in range(3):
            t.transpose(bank(7, GROUPS, 32 * i), lam_rows[:, i, :], ident[0:GROUPS, 0:GROUPS])
        ins = t.transpose(bank(7, GROUPS, 96)[0:GC], dskip_rows[:], ident[0:GROUPS, 0:GROUPS])
        ins.then_inc(lam_turned, 1)
        for i in range(2):
            for b in range(3):
                ins = t.transpose(bank(4 + i, P, P * b), c_rows[:, i, b].rearrange("r t p -> r (t p)"), ident[:])
            ins.then_inc(c_turned, 1)

        def modulation(j):
            pe.wait_ge(ada_in[j % 2], 32 * (j // 2 + 1))
            if j >= 2:
                pe.wait_ge(ada_used, j - 1)
            for k in range(KD):
                t.matmul(bank(j % 2), c_bcast[:, k, :], ada_w[j % 2][:, k, :], start=(k == 0), stop=False)
            t.matmul(bank(j % 2), ones_row[:], ada_b[j % 2][:], start=False, stop=True).then_inc(ada_mm, 1)

        pe.wait_ge(c_spread, 2)
        for j in range(CH):
            modulation(j)
        pe.wait_ge(lam_b_ready, 1)
        pe.wait_ge(c_ready, 2)
        for d in range(2):
            for q in range(PAIRS):
                for ri in range(2):
                    ins = t.matmul(bank(6 + d, 2 * GC, 2 * GC * q), lam_b[:, ri, d, q].rearrange("p s c -> p (s c)"),
                                   c_pad[:, ri, q].rearrange("p e c -> p (e c)"), start=(ri == 0), stop=(ri == 1))
        ins.then_inc(k_mm, 1)
        for i in range(12):
            ri, d, q = i // 6, i // 3 % 2, 4 * (i % 3)
            if i >= 2:
                pe.wait_ge(win_ready, i - 1)
            for n in range(4):
                ins = t.transpose(bank(4 + i % 2, P, P * n), lam_b[:, ri, d, q + n].rearrange("p s c -> p (s c)"), ident[:])
            ins.then_inc(win_turned, 1)
        for j in range(CH, N_ADA):
            modulation(j)
        pe.wait_ge(ada_used, N_ADA)
        for i in range(2 * KD):
            k, half = i // 2, i % 2
            pe.wait_ge(x_scaled, 4 * (half + 1))
            if i >= 2:
                pe.wait_ge(h_ready, i - 1)
            for n in range(4):
                ins = t.transpose(bank(i % 2, P, P * n), x_rows[:, 4 * half + n, P * k:P * (k + 1)], ident[:])
            ins.then_inc(x_turned, 1)
        pe.wait_ge(h_ready, 2 * KD)
        pe.wait_ge(k_ready, 2)
        pe.wait_ge(win_ready, 12)
        for n in range(len(win_units)):
            pe.wait_ge(win_in[n % 3], win_counts[n])
            if n >= 3:
                pe.wait_ge(z_ready, n - 2)
            for k in range(KD):
                for half in range(2):
                    ins = t.matmul(bank(2 + 2 * (n % 3) + half), win_raw[n % 3][:, k, :], h_t[:, k, HALF * half:HALF * (half + 1)],
                                   start=(k == 0), stop=(k == KD - 1))
            ins.then_inc(win_mm, 1)
        mix_tensor(pe, t)


def constants():
    n = np.arange(SEQ, dtype=np.int64)
    turn = 2 * np.pi / SEQ * ((n[:, None] * n[None, :]) % SEQ)
    m = np.arange(HEAD, dtype=np.int64)
    turn_d = 2 * np.pi / HEAD * ((m[:, None] * m[None, :]) % HEAD)
    dft = np.stack([np.cos(turn), np.sin(turn)], 1) / 32.0
    eye2 = np.eye(2)
    dft_d = np.stack([np.kron(eye2, np.cos(turn_d)), np.kron(eye2, -np.sin(turn_d))], 1) / 8.0
    dist = np.abs(np.arange(P)[:, None] + P - np.arange(SPAN)[None, :])
    slopes = np.exp2(np.float32(-8.0) * np.arange(1, Q_HEADS + 1, dtype=np.float32) / np.float32(Q_HEADS)).astype(np.float32)
    bias = -slopes[None, :, None] * dist[:, None, :].astype(np.float32)
    bias = np.where(dist[:, None, :] <= P, bias * np.float32(8.0), np.float32(8 * NEG))
    row, col = np.arange(P)[:, None], np.arange(P)[None, :]
    return {
        "ident": np.eye(P, dtype=np.float32),
        "dft": dft.astype(np.float32),
        "dft_d": dft_d.astype(np.float32),
        "att_bias": bias.astype(np.float32),
        "causal": np.where(col <= row, 0.0, NEG).astype(np.float32),
        "upper": (row <= col).astype(np.float32),
    }


_INS = ["x", "c", "w_ada", "b_ada", "g_pre_mix", "g_post_mix", "g_pre_ffn", "g_post_ffn", "w_in", "lam_re", "lam_im",
        "log_dt", "b_re", "b_im", "c_re", "c_im", "d_skip", "w_glu", "w_fft", "sink", "w_out", "w_up", "conv_w", "conv_b",
        "w_down", "ffn1_w1_2", "ffn1_w3_2", "ffn1_w2_2", "ln1_g_2", "ln1_b_2", "w_in_2", "kv_norm_g_2", "w_uk_2",
        "w_uv_2", "gmlp_ln_g_2", "gmlp_ln_b_2", "gmlp_ws_2", "gmlp_bs_2", "w_out_2", "ln2_g_2", "ln2_b_2",
        "ffn2_w1_2", "ffn2_w3_2", "ffn2_w2_2", "ln3_g_2", "ln3_b_2"]


def kernel(**inputs):
    import concourse.bacc as bacc
    from concourse.bass_utils import run_bass_kernel_spmd

    nc = bacc.Bacc("TRN2", target_bir_lowering=False, num_devices=1)
    arrays = {name: np.ascontiguousarray(inputs[name]) for name in _INS}
    arrays.update(constants())
    arrays = {f"in_{name}": array for name, array in arrays.items()}
    a = {name[3:]: nc.dram_tensor(name, array.shape, mybir.dt.from_np(array.dtype), kind="ExternalInput").ap()
         for name, array in arrays.items()}
    out = nc.dram_tensor("out", (1, SEQ, D), F32, kind="ExternalOutput").ap()
    build(nc, a, out)
    got = run_bass_kernel_spmd(nc, [arrays], core_ids=[0])
    return got.results[0]["out"]
```

```python
from contextlib import ExitStack
import math

import numpy as np

import concourse.bass as bass
from concourse import mybir

F32 = mybir.dt.float32
F32R = mybir.dt.float32r
ACT = mybir.ActivationFunctionType
ALU = mybir.AluOpType
AX_X = mybir.AxisListType.X

P = 128
SEQ = 1024
D = 1024
KD = D // P
NT = SEQ // P
HALF = 512
D_FF = 2816
NF = D_FF // P
SSM_W, FFT_W, ATT_W = 384, 256, 384
HEAD = 64
GROUPS, STATE, GC = 24, 64, 16
PAIRS = GROUPS // 2
CH = 8
NCH = SEQ // CH
Q_HEADS, KV_HEADS = 6, 2
SPAN = 3 * P
RMS_EPS, LN_EPS = 1e-6, 1e-5
NEG = -1e30
TWO_PI_HI = 6.28125
TWO_PI_LO = 2 * math.pi - TWO_PI_HI
ROUND = 1.5 * 2 ** 23
PI_DOWN = 3.1415925
LN2_HI = 0.693359375
LN2_LO = math.log(2) - LN2_HI
I32 = mybir.dt.int32


class Steps:

    def __init__(self, engine, sem):
        self.engine, self.sem, self.n = engine, sem, 0

    def add(self, ins):
        ins.then_inc(self.sem, 1)
        self.n += 1

    def settle(self):
        self.engine.wait_ge(self.sem, self.n)


def build(nc, a, out):
    with ExitStack() as ctx:
        body(ctx, nc, a, out)


def body(ctx, nc, a, out):
    sems = {}

    def sem(name):
        if name not in sems:
            sems[name] = ctx.enter_context(nc.semaphore(name))
        return sems[name]

    KB = 1024
    CONST = (nc.sbuf_base + 63) // 64 * 64
    XR = CONST + 12096
    GR = XR + 64 * KB
    RR = GR + 88 * KB
    at = {"next": CONST}

    def place(name, shape, offset, dt=F32):
        return nc.alloc_sbuf_tensor_at(name, shape, dt, offset=offset)

    def const(name, shape):
        n = 4 * int(np.prod(shape[1:]))
        t = place(name, shape, at["next"])
        at["next"] += (n + 31) // 32 * 32
        assert at["next"] <= XR
        return t

    psum = ctx.enter_context(nc.psum_tensor("psum", [P, 8 * HALF], F32))

    def bank(b, n=HALF, at=0):
        return psum[:, b * HALF + at:b * HALF + at + n]

    ident = const("ident", [P, P])
    row_a = const("row_a", [P, D])
    row_b = const("row_b", [P, D])
    conv_cols = const("conv_cols", [P, NF, 2, 4])
    norm_cols = const("norm_cols", [P, 2, KD])
    mod_cols = const("mod_cols", [P, 4, KD])
    stat_a = const("stat_a", [P, 2 * NT])
    stat_b = const("stat_b", [P, 2 * NT])
    stat_c = const("stat_c", [P, 2 * NT])
    sink_row = const("sink_row", [P, Q_HEADS])
    ones_row = const("ones_row", [1, P])
    dskip_cols = const("dskip_cols", [GC, GROUPS])
    c_cols = const("c_cols", [P, KD])
    log_dt_rows = const("log_dt_rows", [GROUPS, 2])

    x_rows = place("x_rows", [P, NT, D], GR)
    junk = place("junk", [P, D], GR + 32 * KB)
    junk2 = place("junk2", [P, P], GR + 39 * KB + 512)
    c_plain = place("c_plain", [P, 2, PAIRS, GC], GR + 36 * KB)
    ada_w = [place(f"ada_w{i}", [P, KD, HALF], at) for i, at in enumerate((XR, XR + 16 * KB, GR + 64 * KB))]
    c_bcast = place("c_bcast", [P, KD, P], RR + 40 * KB)
    ada_b = [place(f"ada_b{i}", [1, HALF], at) for i, at in enumerate((XR + 56 * KB, XR + 58 * KB, GR + 80 * KB))]
    vec_rows = [place(f"vec_rows{i}", [P, P], RR + 512 * i) for i in range(2)]
    lam_rows = place("lam_rows", [GROUPS, 3, P], RR + KB)
    dskip_rows = place("dskip_rows", [GROUPS, GC], RR + 2 * KB + 512)
    b_raw = place("b_raw", [P, 2, 2, PAIRS, GC], RR + 28 * KB)
    c_rows = place("c_rows", [P, 2, 3, 2, STATE], RR + 31 * KB)
    w_tmp = place("w_tmp", [P, 2, 4, PAIRS, GC], RR + 34 * KB)
    e_tmp = place("e_tmp", [P, 4, PAIRS, GC], RR + 4 * KB)
    c_pad = place("c_pad", [P, 2, PAIRS, 2, GC], XR + 60 * KB)
    lam_b = place("lam_b", [P, 2, 2, PAIRS, CH, GC], XR + 32 * KB)
    k_sum = place("k_sum", [P, 2, GROUPS * GC], RR + 28 * KB)
    k_shift = place("k_shift", [P, GROUPS * GC], RR + 8 * KB)
    prm = place("prm", [P, 26, 2 * PAIRS], RR + 12 * KB)
    prm_int = place("prm_int", [P, 2 * PAIRS], RR + 15 * KB + 896, I32)
    pw = place("pw", [P, 2, 7, 2 * PAIRS], RR + 14 * KB + 512)
    toep = place("toep", [P, CH, GROUPS * GC], RR + 16 * KB)
    carry_out = place("carry_out", [P, 2, 2, PAIRS, CH, GC], GR + 40 * KB)
    state_in = place("state_in", [P, 2, 2, PAIRS, P], GR + 64 * KB)
    x_hi = place("x_hi", [P, KD, SEQ], XR, F32R)
    x_lo = place("x_lo", [P, KD, SEQ], XR + 32 * KB, F32R)
    h_tmp = [place(f"h_tmp{i}", [P, HALF], RR + 8 * KB + 2 * KB * i) for i in range(2)]
    win_raw = [place(f"win_raw{i}", [P, KD * P], RR + 4 * KB * i) for i in range(2)]
    win_upper = [place(f"win_upper{i}", [P, KD * P], at, F32R) for i, at in enumerate((GR + 32 * KB, RR + 31 * KB))]
    win_lower = [place(f"win_lower{i}", [P, KD * P], at, F32R) for i, at in enumerate((GR + 36 * KB, RR + 35 * KB))]
    u_t = place("u_t", [P, 3, SEQ], GR)
    f_t = place("f_t", [P, 2, SEQ], GR + 12 * KB)
    q_t = place("q_t", [P, 3, SEQ], GR + 20 * KB)
    k_t = place("k_t", [P, SEQ], GR + 32 * KB)
    v_t = place("v_t", [P, SEQ], GR + 36 * KB)
    toep_dram = nc.dram_tensor("toep_dram", (2 * CH - 1, GC, GROUPS * GC), F32).ap()

    ident_in, small_in, x_in, bc_in, ssm_in = (sem(n) for n in ("ident_in", "small_in", "x_in", "bc_in", "ssm_in"))
    vec_in = sem("vec_in")
    ada_in = [sem(f"ada_in{i}") for i in range(3)]
    c_spread, dt_spread, ada_mm, ada_used = (sem(n) for n in ("c_spread", "dt_spread", "ada_mm", "ada_used"))
    rows_turned, vec_used = sem("rows_turned"), sem("vec_used")
    lam_turned, c_turned, c_ready = sem("lam_turned"), sem("c_turned"), sem("c_ready")
    prm_angle, prm_trig, prm_lam = (sem(n) for n in ("prm_angle", "prm_trig", "prm_lam"))
    lam_b_ready, win_turned, win_ready, k_mm, k_ready = (sem(n) for n in ("lam_b_ready", "win_turned", "win_ready", "k_mm", "k_ready"))
    carry_ready, k_shift_in, k_low, k_in_dram, toep_in = (sem(n) for n in ("carry_ready", "k_shift_in", "k_low", "k_in_dram", "toep_in"))
    x_sq, x_var, x_std, x_scaled, x_turned, h_ready = (sem(n) for n in ("x_sq", "x_var", "x_std", "x_scaled", "x_turned", "h_ready"))
    win_in = [sem(f"win_in{i}") for i in range(2)]
    win_hi, win_lo, h_made = sem("win_hi"), sem("win_lo"), sem("h_made")
    win_mm, z_ready = sem("win_mm"), sem("z_ready")
    dve_steps, pool_steps, act_steps = sem("dve_steps"), sem("pool_steps"), sem("act_steps")
    mod_ready = sem("mod_ready")

    f0, q0, k0 = SSM_W, SSM_W + FFT_W, SSM_W + FFT_W + ATT_W
    v0 = k0 + P
    win_units = [([(f0 + P * i, P)], f_t[:, i, :]) for i in range(2)]
    win_units += [([(P * i, P)], u_t[:, i, :]) for i in range(3)]
    win_units += [([(q0 + HEAD * j, HEAD), (q0 + HEAD * (j + 3), HEAD)], q_t[:, j, :]) for j in range(3)]
    win_units += [([(k0, P)], k_t[:, :]), ([(v0, P)], v_t[:, :])]
    win_counts, landed = [], [0, 0]
    for n, (cols, _) in enumerate(win_units):
        landed[n % 2] += 16 * len(cols)
        win_counts.append(landed[n % 2])

    fw_rows = place("fw_rows", [P, 2, P], RR + 40 * KB)
    dft_d = place("dft_d", [P, 2, P], RR + 41 * KB)
    fw = place("fw", [P, 2, 2, P], RR + 42 * KB)
    f_mixed = place("f_mixed", [P, NT, 2, 2, P], XR + 32 * KB)
    dft_w = [place(f"dft_w{i}", [P, SEQ], XR + 4 * KB * i) for i in range(4)]
    u_rows = place("u_rows", [P, GROUPS, CH, GC], RR)
    u_chunk = place("u_chunk", [P, GROUPS, NCH], RR + 28 * KB)
    carry = [place(f"carry{d}", [P, 2, PAIRS, NCH + 1], XR + 32 * KB + 16 * KB * d) for d in range(2)]
    turn = [place("turn", [P, 2, PAIRS, NCH], RR)[:], carry[1][:, :, :, 0:NCH]]
    rot = [place(f"rot{i}", [P, 3, NCH], XR + (44 + 16 * (i // 2)) * KB + 256 + 1536 * (i % 2)) for i in range(4)]
    rot.append(place("rot4", [P, 3, NCH], GR + 17 * KB + 512))
    y_rows = place("y_rows", [P, CH, GROUPS * GC], GR + 64 * KB)
    w_glu = place("w_glu", [P, 3, SSM_W], GR + 76 * KB)
    glu_tmp = [place(f"glu_tmp{i}", [P, HALF], GR + 82 * KB + 2 * KB * i) for i in range(2)]
    y_act = place("y_act", [P, 3, NCH, CH], RR + 12 * KB)
    yc_t = place("yc_t", [P, KD, SEQ], XR)
    att_bias = place("att_bias", [P, Q_HEADS, SPAN], GR)
    v_rows = place("v_rows", [P, NT, P], GR + 9 * KB + 4608)
    probs_at = [XR + 1536 * i for i in range(8)] + [GR + 9 * KB + 1536 * i for i in range(3)] + [GR + 36 * KB]
    SLOTS = len(probs_at)
    probs = [place(f"probs{i}", [P, SPAN], at) for i, at in enumerate(probs_at)]
    turn_tmp = [place(f"turn_tmp{i}", [P, 3, NCH], XR + 20 * KB + 1536 * i) for i in range(4)]
    probs_t = [place(f"probs_t{i}", [P, SPAN], RR + 40 * KB + 1536 * i) for i in range(2)]
    att_max = place("att_max", [P, NT * Q_HEADS], RR + 43 * KB)
    att_sum = place("att_sum", [P, NT * Q_HEADS], RR + 43 * KB + 192)
    att_sink = place("att_sink", [P, NT * Q_HEADS], RR + 43 * KB + 384)
    sink_neg = place("sink_neg", [P, Q_HEADS], RR + 43 * KB + 576)

    fw_zero, fw_in, fw_mm, fw_ready = (sem(n) for n in ("fw_zero", "fw_in", "fw_mm", "fw_ready"))
    fm_mm, fm_ready, dft_mm, yf_mm, yf_ready = (sem(n) for n in ("fm_mm", "fm_ready", "dft_mm", "yf_mm", "yf_ready"))
    dft_in = [sem(f"dft_in{i}") for i in range(4)]
    u_turned, u_rows_ready, uc_turned, uc_ready = (sem(n) for n in ("u_turned", "u_rows_ready", "uc_turned", "uc_ready"))
    v_turned, v_ready, bias_in, glu_in = (sem(n) for n in ("v_turned", "v_ready", "bias_in", "glu_in"))
    states_mm, states_used, carry_done = (sem(n) for n in ("states_mm", "states_used", "carry_done"))
    scores_mm, max_ready, exp_ready, sink_ready, probs_ready = (sem(n) for n in ("scores_mm", "max_ready", "exp_ready", "sink_ready", "probs_ready"))
    probs_turned, probs_t_ready, att_mm, att_ready = (sem(n) for n in ("probs_turned", "probs_t_ready", "att_mm", "att_ready"))
    y_mm, y_rows_ready, y_turned, y_act_ready, glu_mm, glu_sig, glu_ready = (
        sem(n) for n in ("y_mm", "y_rows_ready", "y_turned", "y_act_ready", "glu_mm", "glu_sig", "glu_ready"))

    Z_F, Z_U, Z_Q, Z_ALL = 2, 5, 8, 10
    ITEMS = NT * Q_HEADS
    DELAY = 9
    scores_used, sums_ready = sem("scores_used"), sem("sums_ready")

    def item(i):
        n, h = i // Q_HEADS, i % Q_HEADS
        return n, h, h // 3, h % 3, range(max(n - 1, 0), min(n + 2, NT))

    def mix_sync(sp):
        sp.wait_ge(fw_zero, 1)
        for h in range(4):
            rows = slice(HEAD * (h % 2), HEAD * (h % 2 + 1))
            sp.dma_start(fw_rows[rows, h // 2, rows], a["w_fft"][0, h]).then_inc(fw_in, 16)
        sp.dma_start(dft_d[:], a["dft_d"]).then_inc(fw_in, 16)
        sp.wait_ge(win_mm, Z_ALL)
        for i in range(2 * NT):
            if i >= 4:
                sp.wait_ge(dft_mm, i - 3)
            sp.dma_start(dft_w[i % 4][:], a["dft"][P * (i // 2):P * (i // 2 + 1), i % 2, :]).then_inc(dft_in[i % 4], 16)
        sp.wait_ge(u_turned, 6)
        sp.dma_start(att_bias[:], a["att_bias"]).then_inc(bias_in, 16)
        sp.wait_ge(states_mm, NT)
        sp.dma_start(w_glu[:], a["w_glu"][0].rearrange("(k p) n -> p k n", p=P)).then_inc(glu_in, 16)
        blocks_sync(sp)

    def mix_tensor(pe, t):
        pe.wait_ge(fw_in, 16 * 5)
        pe.wait_ge(z_ready, Z_ALL)
        for pair in range(2):
            for cs in range(2):
                ins = t.matmul(bank(2, P, P * (2 * pair + cs)), dft_d[:, cs, :], fw_rows[:, pair, :], start=True, stop=True)
        ins.then_inc(fw_mm, 1)
        pe.wait_ge(fw_ready, 1)
        for n in range(NT):
            if n >= 2:
                pe.wait_ge(fm_ready, n - 1)
            for pair in range(2):
                ins = t.matmul(bank(4 + n % 2, 2 * P, 2 * P * pair), f_t[:, pair, P * n:P * (n + 1)],
                               fw[:, pair].rearrange("p c e -> p (c e)"), start=True, stop=True)
            ins.then_inc(fm_mm, 1)
        for i in range(6):
            b, sq = i // 2, i % 2
            if i >= 2:
                pe.wait_ge(u_rows_ready, i - 1)
            for s in range(4):
                ins = t.transpose(bank(6 + i % 2, P, P * s), u_t[:, b].rearrange("p (j s) -> p s j", s=CH)[:, 4 * sq + s, :], ident[:])
            ins.then_inc(u_turned, 1)
        pe.wait_ge(u_rows_ready, 6)
        for i in range(6):
            if i >= 2:
                pe.wait_ge(uc_ready, i - 1)
            for g in range(4):
                ins = t.transpose(bank(6 + i % 2, P, P * g), u_rows[:, 4 * i + g].rearrange("p s c -> p (s c)"), ident[:])
            ins.then_inc(uc_turned, 1)
        pe.wait_ge(fm_ready, NT)
        for i in range(2):
            for n in range(4):
                ins = t.transpose(bank(4 + i, P, P * n), v_t[:, P * (4 * i + n):P * (4 * i + n + 1)], ident[:])
            ins.then_inc(v_turned, 1)
        pe.wait_ge(fm_ready, NT)
        for i in range(2 * NT):
            n, cs = i // 2, i % 2
            pe.wait_ge(dft_in[i % 4], 16 * (i // 4 + 1))
            for pair in range(2):
                for half in range(2):
                    ins = t.matmul(bank(2 * pair + half), f_mixed[:, n, pair, cs, :], dft_w[i % 4][:, HALF * half:HALF * (half + 1)],
                                   start=(i == 0), stop=(i == 2 * NT - 1))
            ins.then_inc(dft_mm, 1)
        pe.wait_ge(yf_ready, 4)
        pe.wait_ge(v_ready, 2)
        pe.wait_ge(uc_ready, 6)

        def states(c):
            d, q3 = c // 4, 3 * (c % 4)
            if c >= 1:
                pe.wait_ge(states_used, c)
            for q in range(3):
                for ri in range(2):
                    for e in range(2):
                        half = slice(STATE * e, STATE * (e + 1))
                        ins = t.matmul(bank(5 + ri, NCH, NCH * q)[half], state_in[:, ri, d, q3 + q, half],
                                       u_chunk[:, 2 * (q3 + q) + e, :], start=True, stop=True)
            ins.then_inc(states_mm, 1)

        def scores(i):
            n, h, e, j, keys = item(i)
            if i >= 2:
                pe.wait_ge(scores_used, i - 1)
            rows = slice(HEAD * e, HEAD * (e + 1))
            t.matmul(bank(i % 2, P * len(keys)), q_t[rows, j, P * n:P * (n + 1)], k_t[rows, P * keys[0]:P * (keys[-1] + 1)],
                     start=True, stop=True).then_inc(scores_mm, 1)

        def turn_probs(i):
            n, h, e, j, keys = item(i)
            pe.wait_ge(probs_ready, i + 1)
            if i >= 2:
                pe.wait_ge(probs_t_ready, i - 1)
            for b in range(len(keys)):
                ins = t.transpose(bank(2 + i % 2, P, P * b), probs[i % SLOTS][:, P * b:P * (b + 1)], ident[:])
            ins.then_inc(probs_turned, 1)

        def values(i):
            n, h, e, j, keys = item(i)
            pe.wait_ge(probs_t_ready, i + 1)
            if h == 0 and n:
                pe.wait_ge(att_ready, n)
            rows = slice(HEAD * (h % 2), HEAD * (h % 2 + 1))
            for b, key in enumerate(keys):
                ins = t.matmul(bank(4, P, P * (h // 2))[rows], v_rows[:, key, HEAD * e:HEAD * (e + 1)],
                               probs_t[i % 2][:, P * b:P * (b + 1)], start=(b == 0), stop=(b == len(keys) - 1))
            ins.then_inc(att_mm, 1)

        for i in range(ITEMS + DELAY + 1):
            if i < ITEMS:
                if i % Q_HEADS == 0:
                    states(i // Q_HEADS)
                scores(i)
            if DELAY <= i < ITEMS + DELAY:
                turn_probs(i - DELAY)
            if i > DELAY:
                values(i - DELAY - 1)
        pe.wait_ge(carry_done, NT)
        pe.wait_ge(toep_in, 16 * CH)
        for i in range(3):
            for e in range(2):
                b = 5 + e if i % 2 == 0 else (7 if e == 0 else 0)
                half = slice(STATE * e, STATE * (e + 1))
                if i == 2:
                    pe.wait_ge(y_rows_ready, e + 1)
                for q in range(4):
                    pair = 4 * i + q
                    g = 2 * pair + e
                    dst = bank(b, P, P * q)
                    t.matmul(dst, u_chunk[:, g, :], toep[:, :, GC * g:GC * (g + 1)], start=True, stop=False)
                    for d in range(2):
                        for ri in range(2):
                            ins = t.matmul(dst, carry[d][half, ri, pair, d:d + NCH],
                                           carry_out[half, d, ri, pair].rearrange("p t c -> p (t c)"),
                                           start=False, stop=(d == 1 and ri == 1))
                ins.then_inc(y_mm, 1)
        pe.wait_ge(y_rows_ready, 6)
        for i in range(6):
            tq, b = i // 3, i % 3
            if i >= 2:
                pe.wait_ge(y_act_ready, i - 1)
            for n in range(4):
                ins = t.transpose(bank(1 + i % 2, P, P * n), y_rows[:, 4 * tq + n, P * b:P * (b + 1)], ident[:])
            ins.then_inc(y_turned, 1)
        pe.wait_ge(y_act_ready, 6)
        pe.wait_ge(glu_in, 16)
        for i in range(6):
            b, half = i // 2, i % 2
            if i >= 2:
                pe.wait_ge(glu_sig, i - 1)
            for k in range(3):
                ins = t.matmul(bank(3 + i % 2), w_glu[:, k, P * b:P * (b + 1)],
                               y_act[:, k].rearrange("p j s -> p (j s)")[:, HALF * half:HALF * (half + 1)],
                               start=(k == 0), stop=(k == 2))
            ins.then_inc(glu_mm, 1)
        blocks_tensor(pe, t)

    def mix_scalar(act, steps):
        s = nc.scalar
        act.wait_ge(fw_mm, 1)
        s.copy(fw[:].rearrange("p a c e -> p (a c e)"), bank(2)).then_inc(fw_ready, 1)
        for n in range(NT):
            act.wait_ge(fm_mm, n + 1)
            s.copy(f_mixed[:, n].rearrange("p a c e -> p (a c e)"), bank(4 + n % 2)).then_inc(fm_ready, 1)
        for i in range(6):
            act.wait_ge(uc_turned, i + 1)
            s.copy(u_chunk[:, 4 * i:4 * i + 4, :], bank(6 + i % 2).rearrange("p (g j) -> p g j", g=4)).then_inc(uc_ready, 1)
        for i in range(2):
            act.wait_ge(v_turned, i + 1)
            s.copy(v_rows[:, 4 * i:4 * i + 4, :], bank(4 + i).rearrange("p (n c) -> p n c", n=4)).then_inc(v_ready, 1)
        act.wait_ge(dft_mm, 2 * NT)
        for i in range(4):
            s.copy(yc_t[:, 3 + i // 2, HALF * (i % 2):HALF * (i % 2 + 1)], bank(i)).then_inc(yf_ready, 1)

        def exponentials(n):
            act.wait_ge(max_ready, n + 1)
            for h in range(Q_HEADS):
                i = Q_HEADS * n + h
                p = probs[i % SLOTS][:, 0:P * len(item(i)[4])]
                s.activation(p, p, ACT.Exp, bias=att_max[:, i:i + 1], accum_out=att_sum[:, i:i + 1]).then_inc(exp_ready, 1)
            one = att_sink[:, Q_HEADS * n:Q_HEADS * (n + 1)]
            s.activation(one, one, ACT.Exp).then_inc(sink_ready, 1)

        def copy_probs(i):
            n, h, e, j, keys = item(i)
            act.wait_ge(probs_turned, i + 1)
            if i >= 2:
                act.wait_ge(att_mm, i - 1)
            s.copy(probs_t[i % 2][:, 0:P * len(keys)], bank(2 + i % 2, P * len(keys))).then_inc(probs_t_ready, 1)

        for i in range(ITEMS + DELAY + 2):
            if i < ITEMS and i % Q_HEADS == Q_HEADS - 1:
                exponentials(i // Q_HEADS)
            if DELAY <= i < ITEMS + DELAY:
                copy_probs(i - DELAY)
            if i >= DELAY + 2 and (i - DELAY - 2) % Q_HEADS == Q_HEADS - 1:
                n = (i - DELAY - 2) // Q_HEADS
                act.wait_ge(att_mm, Q_HEADS * (n + 1))
                s.copy(yc_t[:, 5:8, P * n:P * (n + 1)], bank(4, 3 * P).rearrange("p (c q) -> p c q", c=3)).then_inc(att_ready, 1)
        for i in range(3):
            for e in range(2):
                b = 5 + e if i % 2 == 0 else (7 if e == 0 else 0)
                act.wait_ge(y_mm, 2 * i + e + 1)
                dst = y_rows[:].rearrange("p t (q e c) -> p q e t c", e=2, c=GC)
                for q in range(4):
                    ins = s.copy(dst[:, 4 * i + q, e], bank(b, P, P * q).rearrange("p (t c) -> p t c", t=CH))
                ins.then_inc(y_rows_ready, 1)
        for i in range(6):
            tq, b = i // 3, i % 3
            act.wait_ge(y_turned, i + 1)
            s.activation(y_act[:, b].rearrange("p j s -> p s j")[:, 4 * tq:4 * tq + 4, :],
                         bank(1 + i % 2).rearrange("p (s j) -> p s j", s=4), ACT.Gelu_apprx_tanh).then_inc(y_act_ready, 1)
        for i in range(6):
            act.wait_ge(glu_mm, i + 1)
            if i >= 2:
                act.wait_ge(glu_ready, i - 1)
            s.activation(glu_tmp[i % 2][:], bank(3 + i % 2), ACT.Sigmoid).then_inc(glu_sig, 1)
        blocks_scalar(act, steps)

    def mix_vector(dve, v, steps):
        steps.add(v.memset(fw_rows[:], 0.0))
        steps.settle()
        dve.sem_inc(fw_zero, 1)
        for i in range(6):
            b, sq = i // 2, i % 2
            dve.wait_ge(u_turned, i + 1)
            v.tensor_copy(u_rows[:, 8 * b:8 * b + 8, 4 * sq:4 * sq + 4, :].rearrange("p g s c -> p s g c"),
                          bank(6 + i % 2).rearrange("p (s g c) -> p s g c", s=4, g=8)).then_inc(u_rows_ready, 1)

        def turns(d):
            tr, ti = turn[d][:, 0], turn[d][:, 1]
            steps.add(v.memset(tr[:, :, 0:1], 1.0))
            steps.add(v.memset(ti[:, :, 0:1], 0.0))
            steps.settle()
            for m in range(7):
                w = 1 << m
                pr, pi = (pw[:, x, m, PAIRS * d:PAIRS * (d + 1)].unsqueeze(2).to_broadcast([P, PAIRS, w]) for x in range(2))
                halves = [r[:].rearrange("p a b -> p (a b)")for r in turn_tmp]
                done = 0
                step = min(PAIRS, 3 * NCH // w)
                for q in range(0, PAIRS, step):
                    qs = slice(q, q + step)
                    tmp = [x[:, 0:step * w].rearrange("p (a b) -> p a b", a=step) for x in halves]
                    br, bi = pr[:, qs], pi[:, qs]
                    steps.add(v.tensor_tensor(tmp[0], tr[:, qs, 0:w], br, ALU.mult))
                    steps.add(v.tensor_tensor(tmp[1], ti[:, qs, 0:w], bi, ALU.mult))
                    steps.add(v.tensor_tensor(tmp[2], tr[:, qs, 0:w], bi, ALU.mult))
                    steps.add(v.tensor_tensor(tmp[3], ti[:, qs, 0:w], br, ALU.mult))
                    steps.settle()
                    steps.add(v.tensor_tensor(tr[:, qs, w:2 * w], tmp[0], tmp[1], ALU.subtract))
                    steps.add(v.tensor_tensor(ti[:, qs, w:2 * w], tmp[2], tmp[3], ALU.add))
                    steps.settle()

        def turn_states(c):
            d, q3 = c // 4, 3 * (c % 4)
            sr, si = (bank(5 + x, 3 * NCH).rearrange("p (q j) -> p q j", q=3) for x in range(2))
            tr, ti = turn[d][:, 0, q3:q3 + 3], turn[d][:, 1, q3:q3 + 3]
            back, forth = (ALU.add, ALU.subtract) if d == 0 else (ALU.subtract, ALU.add)
            dve.wait_ge(states_mm, c + 1)
            steps.add(v.tensor_tensor(rot[0][:], sr, tr, ALU.mult))
            steps.add(v.tensor_tensor(rot[1][:], si, ti, ALU.mult))
            steps.add(v.tensor_tensor(rot[2][:], si, tr, ALU.mult))
            steps.add(v.tensor_tensor(rot[3][:], sr, ti, ALU.mult))
            steps.settle()
            dve.sem_inc(states_used, 1)
            steps.add(v.tensor_tensor(rot[0][:], rot[0][:], rot[1][:], back))
            steps.add(v.tensor_tensor(rot[2][:], rot[2][:], rot[3][:], forth))
            steps.settle()

        def scan(c):
            d, q3 = c // 4, 3 * (c % 4)
            tr, ti = turn[d][:, 0, q3:q3 + 3], turn[d][:, 1, q3:q3 + 3]
            back, forth = (ALU.add, ALU.subtract) if d == 0 else (ALU.subtract, ALU.add)
            for q in range(3):
                decay = prm[:, 9, PAIRS * d + q3 + q:PAIRS * d + q3 + q + 1].to_broadcast([P, NCH])
                for x in (0, 2):
                    src, dst = rot[x][:, q, :], rot[x + 1][:, q, :]
                    if d:
                        src, dst = src[:, ::-1], dst[:, ::-1]
                    steps.add(v.tensor_tensor_scan(dst, decay, src, 0.0, ALU.mult, ALU.add))
            steps.settle()
            steps.add(v.tensor_tensor(rot[0][:], rot[1][:], tr, ALU.mult))
            steps.add(v.tensor_tensor(rot[2][:], rot[1][:], ti, ALU.mult))
            steps.add(v.tensor_tensor(rot[4][:], rot[3][:], ti, ALU.mult))
            steps.settle()
            steps.add(v.tensor_tensor(rot[1][:], rot[3][:], tr, ALU.mult))
            if d:
                steps.settle()
            dst = [carry[d][:, x, q3:q3 + 3, 1 - d:1 - d + NCH] for x in range(2)]
            steps.add(v.tensor_tensor(dst[0], rot[0][:], rot[4][:], forth))
            steps.settle()
            steps.add(v.tensor_tensor(dst[1], rot[1][:], rot[2][:], back))
            steps.settle()
            dve.sem_inc(carry_done, 1)

        def maximum(i):
            n, h, e, j, keys = item(i)
            dve.wait_ge(scores_mm, i + 1)
            if i >= SLOTS:
                dve.wait_ge(probs_turned, i - SLOTS + 1)
            w = P * len(keys)
            at = P if n == 0 else 0
            v.tensor_tensor_reduce(probs[i % SLOTS][:, 0:w], bank(i % 2, w), att_bias[:, h, at:at + w], 1.0 / 8, NEG,
                                   ALU.add, ALU.max, att_max[:, i:i + 1]).then_inc(scores_used, 1)

        def of_block(n):
            return slice(Q_HEADS * n, Q_HEADS * (n + 1))

        def shifts(n):
            dve.wait_ge(scores_used, Q_HEADS * (n + 1))
            steps.add(v.scalar_tensor_tensor(att_max[:, of_block(n)], att_max[:, of_block(n)], -1.0, sink_neg[:], ALU.mult, ALU.min))
            steps.settle()
            v.tensor_tensor(att_sink[:, of_block(n)], sink_row[:], att_max[:, of_block(n)], ALU.add).then_inc(max_ready, 1)

        def sums(n):
            dve.wait_ge(exp_ready, Q_HEADS * (n + 1))
            dve.wait_ge(sink_ready, n + 1)
            steps.add(v.tensor_tensor(att_sum[:, of_block(n)], att_sum[:, of_block(n)], att_sink[:, of_block(n)], ALU.add))
            steps.settle()
            v.reciprocal(att_sum[:, of_block(n)], att_sum[:, of_block(n)]).then_inc(sums_ready, 1)

        dve.wait_ge(uc_turned, 6)
        for d in range(2):
            turns(d)
        steps.add(v.tensor_scalar(sink_neg[:], sink_row[:], -1.0, None, ALU.mult))
        dve.wait_ge(yf_ready, 4)
        steps.add(v.memset(carry[0][:, :, :, 0:1], 0.0))
        steps.add(v.memset(carry[1][:, :, :, NCH:NCH + 1], 0.0))
        steps.settle()
        dve.wait_ge(bias_in, 16)
        for n in range(NT):
            for h in range(Q_HEADS):
                maximum(Q_HEADS * n + h)
            shifts(n)
            turn_states(n)
            sums(n)
            scan(n)
        for i in range(6):
            b, half = i // 2, i % 2
            dve.wait_ge(glu_sig, i + 1)
            v.tensor_tensor(yc_t[:, b, HALF * half:HALF * (half + 1)],
                            y_act[:, b].rearrange("p j s -> p (j s)")[:, HALF * half:HALF * (half + 1)],
                            glu_tmp[i % 2][:], ALU.mult).then_inc(glu_ready, 1)
        blocks_vector(dve, v, steps)

    def mix_gpsimd(pool, steps):
        for i in range(ITEMS):
            if i % Q_HEADS == 0:
                pool.wait_ge(sums_ready, i // Q_HEADS + 1)
            p = probs[i % SLOTS][:, 0:P * len(item(i)[4])]
            nc.gpsimd.tensor_scalar(p, p, att_sum[:, i:i + 1], 1.0, ALU.mult, ALU.mult).then_inc(probs_ready, 1)
        blocks_gpsimd(pool, steps)

    raw = [place(f"raw{i}", [P, SEQ], RR + 4 * KB * i) for i in range(2)]
    split_hi = [place(f"split_hi{i}", [P, SEQ], RR + 8 * KB + 8 * KB * i, F32R) for i in range(2)]
    split_lo = [place(f"split_lo{i}", [P, SEQ], RR + 12 * KB + 8 * KB * i, F32R) for i in range(2)]
    src_hi = [place(f"src_hi{i}", [P, HALF], RR + 24 * KB + 4 * KB * i, F32R) for i in range(2)]
    src_lo = [place(f"src_lo{i}", [P, HALF], RR + 26 * KB + 4 * KB * i, F32R) for i in range(2)]
    gate = [place(f"gate{i}", [P, SEQ], RR + 28 * KB + 4 * KB * i) for i in range(4)]
    split_tmp = [place(f"split_tmp{i}", [P, HALF], RR + 32 * KB + 2 * KB * i) for i in range(4)]
    sq_junk = place("sq_junk", [P, 2, HALF], RR + 36 * KB)
    y_left = place("y_left", [P, 4, 2, HALF], XR + 48 * KB)
    hidden = place("hidden", [P, NF, SEQ], GR)
    conv_now = const("conv_now", [P, 2, 2, 4])
    moments = const("moments", [P, NT, 2, 6])
    mean_var = const("mean_var", [P, NT, 2])
    res_dram = [nc.dram_tensor(f"res_dram{i}", (SEQ, D), F32).ap() for i in range(4)]
    ALPHA = 2 ** 0.25
    HN = NT // 2
    STEP = 3 * 2 * HN

    def res(n):
        return hidden[:, 2 * n:2 * n + 2, 0:HALF]

    def res_block(n, k):
        c = P * (k % 4)
        return hidden[:, 2 * n + k // 4, c:c + P]

    def y_row(n):
        return y_left[:, n] if n < HN else hidden[:, 2 * (n - HN):2 * (n - HN) + 2, HALF:SEQ]

    def y_banks(n):
        return psum[:, SEQ * (n % HN):SEQ * (n % HN + 1)].rearrange("p (c d) -> p c d", c=2)

    def scaled_row(n):
        if n < HN:
            return hidden[:, 8 + 2 * n:10 + 2 * n, HALF:SEQ]
        return hidden[:, 12 + n, :].rearrange("p (c d) -> p c d", c=2)

    def scaled_block(n, k):
        return scaled_row(n)[:, k // 4, P * (k % 4):P * (k % 4 + 1)]

    def wide(row):
        return row[:].rearrange("p (c d) -> p c d", c=2)

    MIX_STEPS = [3, 4, 5, 6, 7, 0, 1, 2]
    row_view = lambda ap: ap.rearrange("(n p) (c d) -> n p c d", p=P, c=2)
    tiles = lambda ap: ap.rearrange("(k p) (f c) -> f p k c", p=P, c=P)

    w_in = [sem(f"w_in{i}") for i in range(2)]
    w_hi, w_lo, w_mm = sem("w_hi"), sem("w_lo"), sem("w_mm")
    evac_act, evac_dve, y_used = sem("evac_act"), sem("evac_dve"), sem("y_used")
    up_act, up_prod, up_coef, up_shift = sem("up_act"), sem("up_prod"), sem("up_coef"), sem("up_shift")
    before = {"units": 0, "evac": 0, "pairs": 0, "act": 0}

    class Down:
        def __init__(self, e, kt, src, w):
            self.e, self.kt, self.src = e, kt, src
            self.w = w.rearrange("(k p) n -> k p n", p=P)
            self.order = MIX_STEPS if kt == KD else range(kt)
            self.base, self.evacs = before["units"], before["evac"]
            self.half_end, self.end = self.base + kt, self.base + 2 * kt
            before["units"] = self.end
            before["evac"] += 4 if e < 2 else 2

    class Up:
        def __init__(self, w_gate, w_val, conv):
            self.w, self.conv = (w_gate, w_val), conv
            self.base, self.pairs, self.acts = before["units"], before["pairs"], before["act"]
            self.end, self.pairs_end = self.base + 2 * NF, self.pairs + NF
            before["units"], before["pairs"] = self.end, self.pairs_end
            before["act"] += (3 if conv else 1) * NF

    down_mix = Down(0, KD, yc_t, a["w_out"][0])
    up_conv = Up(tiles(a["w_up"][0][:, 0:D_FF]), tiles(a["w_up"][0][:, D_FF:2 * D_FF]), True)
    down_conv = Down(1, NF, hidden, a["w_down"][0])
    up_1 = Up(tiles(a["ffn1_w1_2"][0]), tiles(a["ffn1_w3_2"][0]), False)
    down_1 = Down(2, NF, hidden, a["ffn1_w2_2"][0])
    down_mix2 = Down(3, KD, yc_t, a["w_out_2"][0])
    up_2 = Up(tiles(a["ffn2_w1_2"][0]), tiles(a["ffn2_w3_2"][0]), False)
    down_2 = Down(4, NF, hidden, a["ffn2_w2_2"][0])

    res_in, sq_done, var_ready, std_ready, row_ready = (sem(n) for n in ("res_in", "sq_done", "var_ready", "std_ready", "row_ready"))
    row_scaled, cols_turned, cols_tmp, cols_hi, cols_ready = (sem(n) for n in ("row_scaled", "cols_turned", "cols_tmp", "cols_hi", "cols_ready"))
    res_out, gain_in, row_centred = (sem(n) for n in ("res_out", "gain_in", "row_centred"))
    factors_ready = sem("factors_ready")
    PIECES, LATE = 8, 4


    def down_half(st, engine, step, half, skip=0):
        base = st.base + half * st.kt
        head = KD if st.kt == KD else PIECES + LATE if half else 2
        for k in range(skip, head):
            step(half, k, st.order[k], base + k, k % 2)
        if st.kt > head:
            with engine.Fori(0, (st.kt - head) // 2) as i:
                for u in range(2):
                    step(half, None, 2 * i + head + u, base + 2 * i + head + u, u)

    def down_first(sp, st):
        sp.dma_start(raw[0][:], st.w[st.order[0]]).then_inc(w_in[0], 16)

    def down_sync(sp, st, begun=False):
        def step(half, k, kk, j, slot):
            if half or k or not begun:
                if k is None or j >= 2:
                    sp.wait_ge(w_lo, j - 1)
                sp.dma_start(raw[slot][:], st.w[kk]).then_inc(w_in[slot], 16)
            if k is None or half != (st.kt > KD):
                return
            n = k - 1 if half else k
            if k == 0 and st.e:
                sp.wait_ge(res_out, 16 * NT * st.e)
            if half and k == 1:
                sp.wait_ge(w_mm, st.half_end)
            if 0 <= n < NT:
                src = row_view(a["x"][0] if st.e == 0 else res_dram[st.e - 1])
                sp.dma_start(res(n), src[n]).then_inc(res_in, 16)
        for half in range(2):
            down_half(st, sp, step, half)

    def down_scalar(act, st, skip=0):
        s = nc.scalar

        def step(half, k, kk, j, slot):
            down_split(act, st, half, k, kk, j, slot)
            if half and k is not None:
                if k == 0:
                    act.wait_ge(w_mm, st.half_end)
                    for n in range(0, HN, 2):
                        s.copy(y_row(n), y_banks(n)).then_inc(evac_act, 1)
                end_piece_scalar(act, st, k - (LATE if st.kt > KD else 0))
        for half in range(2):
            down_half(st, act, step, half, 0 if half else skip)

    def down_split(act, st, half, k, kk, j, slot):
        s = nc.scalar
        if k is None or j >= 2:
            act.wait_ge(w_mm, j - 1)
        s.copy(src_hi[slot][:], st.src[:, kk, HALF * half:HALF * (half + 1)])
        act.wait_ge(w_in[slot], (j - slot) * 8 + 16)
        s.copy(split_hi[slot][:], raw[slot][:]).then_inc(w_hi, 1)

    def down_rest(dve, st, half, k, kk, j, slot):
        v = nc.vector
        dve.wait_ge(w_hi, j + 1)
        v.tensor_tensor(src_lo[slot][:], st.src[:, kk, HALF * half:HALF * (half + 1)], src_hi[slot][:], ALU.subtract)
        v.tensor_tensor(split_lo[slot][:], raw[slot][:], split_hi[slot][:], ALU.subtract).then_inc(w_lo, 1)

    def down_vector(dve, st, steps, skip=0):
        v = nc.vector

        def step(half, k, kk, j, slot):
            down_rest(dve, st, half, k, kk, j, slot)
            if half and k is not None:
                if k == 0:
                    dve.wait_ge(w_mm, st.half_end)
                    for n in range(1, HN, 2):
                        v.tensor_copy(y_row(n), y_banks(n)).then_inc(evac_dve, 1)
                end_piece_vector(dve, v, steps, st, k - (LATE if st.kt > KD else 0))
        for half in range(2):
            down_half(st, dve, step, half, 0 if half else skip)

    def down_tensor(pe, st, up=None):
        t = nc.tensor

        def step(half, kk, j, slot, first, last):
            pe.wait_ge(w_lo, j + 1)
            for n in range(HN):
                if first and half:
                    pe.wait_ge((evac_act, evac_dve)[n % 2], st.evacs + n // 2 + 1)
                elif first and up and n % 2 == 0:
                    freed, done = up_freed(up)
                    pe.wait_ge(freed, done(NF - 1 + n // 2))
                rows = slice(P * n, P * (n + 1))
                for m, (l, r) in enumerate(((src_hi, split_hi), (src_hi, split_lo), (src_lo, split_hi))):
                    for c in range(2):
                        ins = t.matmul(bank(2 * n + c), l[slot][:, rows], r[slot][:, HALF * c:HALF * (c + 1)],
                                       start=(first and m == 0), stop=(last and m == 2))
            ins.then_inc(w_mm, 1)

        for half in range(2):
            base = st.base + half * st.kt
            step(half, st.order[0], base, 0, True, False)
            if st.kt == KD:
                for k in range(1, KD - 1):
                    step(half, st.order[k], base + k, k % 2, False, False)
            else:
                with pe.Fori(0, (st.kt - 2) // 2) as i:
                    for u in range(2):
                        step(half, None, base + 2 * i + 1 + u, 1 - u, False, False)
            step(half, None, base + st.kt - 1, 1, False, True)


    def up_freed(st):
        if st.conv:
            return up_shift, lambda p: 4 * p
        return up_prod, lambda p: st.pairs + p

    def up_pairs(engine, pair):
        with engine.Fori(0, (NF - 2) // 2) as i:
            pair(2 * i + 1, 1)
            pair(2 * i + 2, 0)
        pair(NF - 1, 1)

    def up_sync(sp, st):
        def pair(p, par):
            for u in range(2):
                sp.wait_ge(w_lo, st.base + 2 * p + u - 1)
                sp.dma_start(raw[u][:].rearrange("p (k c) -> p k c", c=P), st.w[u][p]).then_inc(w_in[u], 16)
        up_pairs(sp, pair)

    def up_first(sp, st):
        for u in range(2):
            sp.wait_ge(w_lo, st.base + u - 1)
            sp.dma_start(raw[u][:].rearrange("p (k c) -> p k c", c=P), st.w[u][0]).then_inc(w_in[u], 16)

    def up_split(act, st, p, u):
        act.wait_ge(w_mm, st.base + 2 * p + u - 1)
        act.wait_ge(w_in[u], 8 * st.base + 16 * p + 16)
        nc.scalar.copy(split_hi[u][:], raw[u][:]).then_inc(w_hi, 1)

    def up_rest(dve, st, p, u):
        dve.wait_ge(w_hi, st.base + 2 * p + u + 1)
        nc.vector.tensor_tensor(split_lo[u][:], raw[u][:], split_hi[u][:], ALU.subtract).then_inc(w_lo, 1)

    def up_taps(dve, st, p, par):
        nc.vector.tensor_copy(conv_now[:, par], conv_cols[:, p]).then_inc(up_coef, 1)

    def up_scalar(act, st, down):
        s = nc.scalar

        def finish(p, par):
            banks = 4 * (1 - par)
            act.wait_ge(w_mm, st.base + 2 * p - 1)
            if not st.conv:
                s.activation(gate[1 - par][:], psum[:, HALF * banks:HALF * (banks + 2)], ACT.Silu).then_inc(up_act, 1)
                return
            act.wait_ge(up_coef, p)
            for u in range(2):
                if u:
                    act.wait_ge(w_mm, st.base + 2 * p)
                w = conv_now[:, 1 - par, u]
                s.activation(gate[2 * (1 - par) + u][:], psum[:, HALF * (banks + 2 * u):HALF * (banks + 2 * u + 2)],
                             ACT.Identity, scale=w[:, 1:2], bias=w[:, 3:4]).then_inc(up_act, 1)

        def activate(p, par):
            act.wait_ge(up_shift, 4 * p - 2)
            s.activation(gate[2 * (1 - par)][:], gate[2 * (1 - par)][:], ACT.Gelu_apprx_tanh).then_inc(up_act, 1)

        def pair(p, par):
            up_split(act, st, p, 0)
            finish(p, par)
            up_split(act, st, p, 1)
            if st.conv:
                activate(p, par)

        up_pairs(act, pair)
        act.wait_ge(up_prod, st.pairs_end - 2)
        down_split(act, down, 0, 0, down.order[0], down.base, 0)
        finish(NF, 0)
        if st.conv:
            activate(NF, 0)
        act.wait_ge(up_prod, st.pairs_end)

    def up_vector(dve, st, down):
        v = nc.vector

        def shifts(p, par):
            for u in range(2):
                dve.wait_ge(up_act, 3 * p - 2 + u)
                b = HALF * (4 * (1 - par) + 2 * u)
                g, w = gate[2 * (1 - par) + u], conv_now[:, 1 - par, u]
                v.scalar_tensor_tensor(g[:, 1:SEQ], psum[:, b:b + SEQ - 1], w[:, 0:1], g[:, 1:SEQ], ALU.mult, ALU.add).then_inc(up_shift, 1)
                dve.wait_ge(up_shift, 4 * p - 3 + 2 * u)
                v.scalar_tensor_tensor(g[:, 0:SEQ - 1], psum[:, b + 1:b + SEQ], w[:, 2:3], g[:, 0:SEQ - 1], ALU.mult, ALU.add).then_inc(up_shift, 1)

        def product(p, par):
            b = HALF * (4 * (1 - par) + 2)
            if st.conv:
                dve.wait_ge(up_act, 3 * p)
                dve.wait_ge(up_shift, 4 * p)
                left, right = gate[2 * (1 - par)][:], gate[2 * (1 - par) + 1][:]
            else:
                dve.wait_ge(up_act, st.acts + p)
                dve.wait_ge(w_mm, st.base + 2 * p)
                left, right = gate[1 - par][:], psum[:, b:b + SEQ]
            v.tensor_tensor(hidden[:, p - 1, :], left, right, ALU.mult).then_inc(up_prod, 1)

        def pair(p, par):
            up_rest(dve, st, p, 0)
            if st.conv:
                up_taps(dve, st, p, par)
                shifts(p, par)
            else:
                product(p, par)
            up_rest(dve, st, p, 1)
            if st.conv:
                product(p, par)

        up_pairs(dve, pair)
        down_rest(dve, down, 0, 0, down.order[0], down.base, 0)
        if st.conv:
            shifts(NF, 0)
        product(NF, 0)

    def up_unit(st, p, par, u, halves):
        t = nc.tensor
        for k in range(KD):
            cols = slice(P * k, P * (k + 1))
            for m, (l, r) in enumerate(((split_hi, x_hi), (split_hi, x_lo), (split_lo, x_hi))):
                for half in halves:
                    ins = t.matmul(bank(4 * par + 2 * u + half), l[u][:, cols], r[:, k, HALF * half:HALF * (half + 1)],
                                   start=(k == 0 and m == 0), stop=(k == KD - 1 and m == 2))
        return ins

    def up_tensor(pe, st):
        freed, done = up_freed(st)

        def pair(p, par):
            for u in range(2):
                pe.wait_ge(w_lo, st.base + 2 * p + u + 1)
                up_unit(st, p, par, u, range(2)).then_inc(w_mm, 1)

        pair(1, 1)
        with pe.Fori(0, (NF - 2) // 2) as i:
            for u in range(2):
                pe.wait_ge(freed, done(2 * i + u + 1))
                pair(2 * i + 2 + u, u)


    Y_SCALE = {2: 0.5 / ALPHA, 3: 1.0 / ALPHA, 4: 0.5 / ALPHA}
    roots = {"act": 0, "dve": 0}

    def take_root(act, cols=slice(0, NT)):
        roots["act"] += 1
        act.wait_ge(var_ready, roots["act"])
        nc.scalar.activation(stat_b[:, cols], stat_a[:, NT + cols.start:NT + cols.stop], ACT.Sqrt).then_inc(std_ready, 1)

    def end_root(dve, v, steps, cols=slice(0, NT), ask=True):
        roots["dve"] += 1
        if ask:
            dve.sem_inc(var_ready, 1)
        dve.wait_ge(std_ready, roots["dve"])
        inverse_root(v, steps, stat_a[:, NT + cols.start:NT + cols.stop], cols)

    def norm_factors(dve, v, steps, sums, cols):
        steps.add(v.tensor_scalar(stat_a[:, NT + cols.start:NT + cols.stop], sums, 1.0 / D, RMS_EPS, ALU.mult, ALU.add))
        steps.settle()
        end_root(dve, v, steps, cols)

    def begin_layer_factors(v, steps, cols):
        steps.add(v.tensor_scalar(stat_a[:, NT + cols.start:NT + cols.stop], mean_var[:, cols, 1], LN_EPS / ALPHA ** 2, None, ALU.add))
        steps.settle()

    def layer_factors(dve, v, steps, cols):
        begin_layer_factors(v, steps, cols)
        end_root(dve, v, steps, cols)
        steps.add(v.scalar_tensor_tensor(stat_c[:, cols], mean_var[:, cols, 0], -1.0, stat_b[:, NT + cols.start:NT + cols.stop],
                                         ALU.mult, ALU.mult))
        steps.settle()

    def rows_of(half):
        return range(HN * half, HN * (half + 1))

    def cols_of(half):
        return slice(HN * half, HN * (half + 1))

    def rstd(n):
        return stat_b[:, NT + n:NT + n + 1]

    def end_store(sp, e, half):
        dst = row_view(res_dram[e] if e < 4 else out[0])
        for n in rows_of(half):
            sp.wait_ge(row_ready, NT * e + n + 1)
            sp.dma_start(dst[n], res(n)).then_inc(res_out, 16)

    def load_gains(sp, g_name, b_name):
        sp.dma_start(row_a[:], a[g_name].to_broadcast([P, D])).then_inc(gain_in, 16)
        sp.dma_start(row_b[:], a[b_name].to_broadcast([P, D])).then_inc(gain_in, 16)

    GAINS_IN = {2: 32, 3: 64, 4: 96}
    SQUARES = {0: 0, 1: 2 * NT}

    def square_row(act, e, n, again):
        m = SQUARES[e] + (2 * HN * (n // HN) + n % HN + (HN if again else 0) if e == 0 else n)
        if again:
            act.wait_ge(row_ready, n + 1)
        if m:
            act.wait_ge(sq_done, m)
        src, dst = (res(n), stat_c[:, n:n + 1]) if again else (y_row(n), stat_a[:, n:n + 1])
        nc.scalar.activation(sq_junk[:], src, ACT.Square, accum_out=dst).then_inc(sq_done, 1)

    def end_piece_scalar(act, st, i):
        e = st.e
        if e < 2:
            if i == 0:
                act.wait_ge(evac_act, st.evacs + 2)
                act.wait_ge(evac_dve, st.evacs + 2)
                for n in (0, 1):
                    square_row(act, e, n, False)
            elif i == 1:
                for n in (2, 3):
                    square_row(act, e, n, False)
                take_root(act, cols_of(0))
            elif e == 0 and 3 <= i < 7:
                square_row(act, e, i - 3, True)
                if i == 6:
                    take_root(act, cols_of(0))
        elif i == 4:
            take_root(act, cols_of(0))
        elif i in (5, 6):
            centre(act, e, range(2 * i - 10, 2 * i - 8))

    def centre(act, e, rows):
        for n in rows:
            if n == 0:
                act.wait_ge(factors_ready, e - 1)
            nc.scalar.activation(res(n), res(n), ACT.Identity, scale=rstd(n), bias=stat_c[:, n:n + 1]).then_inc(row_centred, 1)

    def end_piece_vector(dve, v, steps, st, i):
        e = st.e
        if e < 2:
            if i == 1:
                dve.wait_ge(sq_done, SQUARES[e] + HN)
                norm_factors(dve, v, steps, stat_a[:, cols_of(0)], cols_of(0))
            elif 2 <= i < 6:
                add_branch(dve, v, steps, e, i - 2)
            elif e == 0 and i == 6:
                dve.wait_ge(sq_done, 2 * HN)
                norm_factors(dve, v, steps, stat_c[:, cols_of(0)], cols_of(0))
            elif e == 0 and i == 7:
                scale_rows(v, 0)
        elif 0 <= i < 4:
            dve.wait_ge(res_in, 16 * (NT * e + i + 1))
            if i == 0:
                dve.wait_ge(evac_act, st.evacs + 2)
                dve.wait_ge(evac_dve, st.evacs + 2)
            steps.add(v.scalar_tensor_tensor(res(i), y_row(i), Y_SCALE[e], res(i), ALU.mult, ALU.add))
            steps.settle()
            row_moments(v, steps, i)
        elif i == 4:
            layer_factors(dve, v, steps, cols_of(0))
            dve.sem_inc(factors_ready, 1)
        elif i in (6, 7):
            gain_rows(dve, v, steps, e, range(2 * i - 12, 2 * i - 10))

    def add_branch(dve, v, steps, e, n):
        row = wide(row_a if e == 0 else row_b)
        for c in range(2):
            steps.add(v.scalar_tensor_tensor(y_row(n)[:, c], y_row(n)[:, c], rstd(n), row[:, c], ALU.mult, ALU.mult))
        steps.settle()
        dve.wait_ge(res_in, 16 * (NT * e + n + 1))
        v.tensor_tensor(res(n), res(n), y_row(n), ALU.add).then_inc(row_ready, 1)

    def scale_rows(v, half):
        for n in rows_of(half):
            v.tensor_scalar(scaled_row(n), res(n), rstd(n), None, ALU.mult).then_inc(row_scaled, 1)

    def row_moments(v, steps, n):
        for c in range(2):
            steps.add(v.bn_stats(moments[:, n, c, :], res(n)[:, c]))
        steps.settle()
        steps.add(v.bn_aggr(mean_var[:, n, :], moments[:, n].rearrange("p a b -> p (a b)")))
        steps.settle()

    def gain_rows(dve, v, steps, e, rows):
        dve.wait_ge(gain_in, GAINS_IN[e])
        for n in rows:
            dve.wait_ge(row_centred, HN * (e - 2) + n + 1)
            steps.add(v.tensor_tensor(res(n), res(n), wide(row_a), ALU.mult))
        steps.settle()
        for n in rows:
            v.tensor_tensor(res(n), res(n), wide(row_b), ALU.add).then_inc(row_ready, 1)

    def end_scalar(act, st, begin):
        s, e = nc.scalar, st.e
        if e < 2:
            act.wait_ge(w_mm, st.end)
            for n in range(HN, NT, 2):
                s.copy(y_row(n), y_banks(n)).then_inc(evac_act, 1)
        if begin:
            begin()
            upper_columns(act, e, 0)
        if e < 2:
            take_root(act, cols_of(1))
            if e == 0:
                for n in rows_of(1):
                    square_row(act, e, n, True)
                take_root(act, cols_of(1))
        else:
            take_root(act, cols_of(1))
        if begin:
            upper_columns(act, e, 1)

    def end_vector(dve, v, steps, st, begin):
        e = st.e
        dve.wait_ge(w_mm, st.end)
        if e < 2:
            for n in range(HN + 1, NT, 2):
                v.tensor_copy(y_row(n), y_banks(n)).then_inc(evac_dve, 1)
        else:
            dve.wait_ge(res_in, 16 * NT * (e + 1))
            for n in rows_of(1):
                v.scalar_tensor_tensor(res(n), y_banks(n), Y_SCALE[e], res(n), ALU.mult, ALU.add).then_inc(y_used, 1)
        if begin:
            begin()
            split_columns(dve, v, e, 0)
        if e < 2:
            dve.wait_ge(evac_act, st.evacs + 4)
            dve.wait_ge(evac_dve, st.evacs + 4)
            dve.wait_ge(sq_done, SQUARES[e] + (3 * HN if e == 0 else NT))
            norm_factors(dve, v, steps, stat_a[:, cols_of(1)], cols_of(1))
            for n in rows_of(1):
                add_branch(dve, v, steps, e, n)
            if e == 0:
                dve.wait_ge(sq_done, 2 * NT)
                norm_factors(dve, v, steps, stat_c[:, cols_of(1)], cols_of(1))
                scale_rows(v, 1)
        else:
            dve.wait_ge(y_used, NT // 2 * (e - 1))
            for n in rows_of(1):
                row_moments(v, steps, n)
            begin_layer_factors(v, steps, cols_of(1))
            dve.sem_inc(var_ready, 1)
            dve.wait_ge(gain_in, GAINS_IN[e])
            for n in rows_of(1):
                steps.add(v.scalar_tensor_tensor(res(n), res(n), mean_var[:, n, 0:1], wide(row_a), ALU.subtract, ALU.mult))
            end_root(dve, v, steps, cols_of(1), False)
            for n in rows_of(1):
                v.scalar_tensor_tensor(res(n), res(n), rstd(n), wide(row_b), ALU.mult, ALU.add).then_inc(row_ready, 1)
        if begin:
            split_columns(dve, v, e, 1)

    def column_bank(half, k):
        return bank(4 * half + k % 4)

    def upper_columns(act, e, half):
        def modulate(k):
            i = KD * half + k
            act.wait_ge(cols_turned, i + 1)
            act.wait_ge(cols_ready, i - 3)
            nc.scalar.activation(split_tmp[k % 4][:], column_bank(half, k), ACT.Identity, scale=mod_cols[:, 3, k:k + 1],
                                 bias=mod_cols[:, 2, k:k + 1]).then_inc(cols_tmp, 1)
        if e == 0 and half:
            modulate(0)
        for k in range(KD):
            i = 2 * KD * e + KD * half + k
            dst = x_hi[:, k, HALF * half:HALF * (half + 1)]
            if e == 0:
                if half and k + 1 < KD:
                    modulate(k + 1)
                act.wait_ge(cols_tmp, i + 1)
                nc.scalar.copy(dst, split_tmp[k % (4 if half else 2)][:]).then_inc(cols_hi, 1)
            else:
                act.wait_ge(cols_turned, i + 1)
                nc.scalar.copy(dst, column_bank(half, k)).then_inc(cols_hi, 1)
            if e < 2 and half == 0 and k % 2:
                if k == 1:
                    act.wait_ge(evac_act, 4 * e + 4)
                    act.wait_ge(evac_dve, 4 * e + 4)
                square_row(act, e, HN + k // 2, False)

    def split_columns(dve, v, e, half):
        dst = slice(HALF * half, HALF * (half + 1))

        def rest(k):
            i = 2 * KD * e + KD * half + k
            dve.wait_ge(cols_hi, i + 1)
            src = split_tmp[k % (4 if half else 2)][:] if e == 0 else column_bank(half, k)
            v.tensor_tensor(x_lo[:, k, dst], src, x_hi[:, k, dst], ALU.subtract).then_inc(cols_ready, 1)
        if e == 0 and half == 0:
            for k in range(KD):
                dve.wait_ge(cols_turned, k + 1)
                if k >= 2:
                    dve.wait_ge(cols_ready, k - 1)
                v.tensor_scalar(split_tmp[k % 2][:], column_bank(half, k), mod_cols[:, 3, k:k + 1], mod_cols[:, 2, k:k + 1],
                                ALU.mult, ALU.add).then_inc(cols_tmp, 1)
                if k:
                    rest(k - 1)
            rest(KD - 1)
        else:
            for k in range(KD):
                rest(k)

    def end_tensor(pe, st, wait_unit, unit, unit_done):
        t, e = nc.tensor, st.e
        for half in range(2):
            if e == 0:
                pe.wait_ge(row_scaled, HN * (half + 1))
            else:
                pe.wait_ge(row_ready, NT * e + HN * (half + 1))
            for k in range(KD):
                i = 2 * KD * e + KD * half + k
                if k >= 4:
                    pe.wait_ge(cols_ready, i - 3)
                elif k % 2 == 0:
                    n = 2 * half + k // 2
                    if e < 2:
                        pe.wait_ge((evac_act, evac_dve)[n % 2], st.evacs + 3 + n // 2)
                    else:
                        pe.wait_ge(y_used, HN * (e - 2) + n + 1)
                for n in range(HN):
                    row = scaled_block(HN * half + n, k) if e == 0 else res_block(HN * half + n, k)
                    ins = t.transpose(column_bank(half, k)[:, P * n:P * (n + 1)], row, ident[:])
                ins.then_inc(cols_turned, 1)
            pe.wait_ge(cols_ready, 2 * KD * e + KD * (half + 1))
            for u in range(2):
                if half == 0:
                    wait_unit(u)
                ins = unit(u, [half])
                if half:
                    unit_done(ins)

    def end_tensor_up(pe, st, up):
        end_tensor(pe, st, lambda u: pe.wait_ge(w_lo, up.base + u + 1), lambda u, halves: up_unit(up, 0, 0, u, halves),
                   lambda ins: ins.then_inc(w_mm, 1))

    def up_begin_scalar(act, st):
        for u in range(2):
            up_split(act, st, 0, u)

    def up_begin_vector(dve, st):
        for u in range(2):
            up_rest(dve, st, 0, u)
        if st.conv:
            up_taps(dve, st, 0, 0)

    def feed_sync(sp, st, up, begun=False):
        down_sync(sp, st, begun)
        up_first(sp, up)
        for half in range(2):
            end_store(sp, st.e, half)

    def blocks_sync(sp):
        sp.wait_ge(y_mm, 6)
        feed_sync(sp, down_mix, up_conv)
        up_sync(sp, up_conv)
        feed_sync(sp, down_conv, up_1)
        load_gains(sp, "ln1_g_2", "ln1_b_2")
        up_sync(sp, up_1)
        down_sync(sp, down_1)
        mix2_first(sp)
        for half in range(2):
            end_store(sp, 2, half)
        mix2_sync(sp)
        feed_sync(sp, down_mix2, up_2, True)
        load_gains(sp, "ln3_g_2", "ln3_b_2")
        up_sync(sp, up_2)
        down_sync(sp, down_2)
        for half in range(2):
            end_store(sp, 4, half)
        sp.wait_ge(res_out, 16 * NT * 5)

    def blocks_scalar(act, steps):
        act.wait_ge(glu_ready, 6)
        down_scalar(act, down_mix)
        end_scalar(act, down_mix, lambda: up_begin_scalar(act, up_conv))
        up_scalar(act, up_conv, down_conv)
        down_scalar(act, down_conv, 1)
        end_scalar(act, down_conv, lambda: up_begin_scalar(act, up_1))
        up_scalar(act, up_1, down_1)
        down_scalar(act, down_1, 1)
        end_scalar(act, down_1, lambda: mix2_begin_scalar(act))
        mix2_scalar(act, steps)
        down_scalar(act, down_mix2)
        end_scalar(act, down_mix2, lambda: up_begin_scalar(act, up_2))
        up_scalar(act, up_2, down_2)
        down_scalar(act, down_2, 1)
        end_scalar(act, down_2, None)

    def blocks_vector(dve, v, steps):
        down_vector(dve, down_mix, steps)
        end_vector(dve, v, steps, down_mix, lambda: up_begin_vector(dve, up_conv))
        dve.wait_ge(res_out, 16 * NT)
        up_vector(dve, up_conv, down_conv)
        down_vector(dve, down_conv, steps, 1)
        end_vector(dve, v, steps, down_conv, lambda: up_begin_vector(dve, up_1))
        dve.wait_ge(res_out, 16 * NT * 2)
        up_vector(dve, up_1, down_1)
        down_vector(dve, down_1, steps, 1)
        end_vector(dve, v, steps, down_1, lambda: None)
        mix2_vector(dve, v, steps)
        down_vector(dve, down_mix2, steps)
        end_vector(dve, v, steps, down_mix2, lambda: up_begin_vector(dve, up_2))
        dve.wait_ge(res_out, 16 * NT * 4)
        up_vector(dve, up_2, down_2)
        down_vector(dve, down_2, steps, 1)
        end_vector(dve, v, steps, down_2, None)

    def blocks_gpsimd(pool, steps):
        mix2_gpsimd(pool, steps)

    def blocks_tensor(pe, t):
        down_tensor(pe, down_mix)
        end_tensor_up(pe, down_mix, up_conv)
        up_tensor(pe, up_conv)
        down_tensor(pe, down_conv, up_conv)
        end_tensor_up(pe, down_conv, up_1)
        up_tensor(pe, up_1)
        down_tensor(pe, down_1, up_1)
        mix2_begin_tensor(pe, t)
        mix2_tensor(pe, t)
        down_tensor(pe, down_mix2)
        end_tensor_up(pe, down_mix2, up_2)
        up_tensor(pe, up_2)
        down_tensor(pe, down_2, up_2)

    TOP = 256
    A_HEADS, I_HEADS = 8, 4
    LAT = 128
    MLP = 512
    q2, c2 = 0, A_HEADS * HEAD
    qi2 = c2 + LAT
    ki2 = qi2 + I_HEADS * HEAD
    wi2 = ki2 + HEAD
    u2 = wi2 + I_HEADS
    v2 = u2 + MLP
    qi_t = place("qi_t", [P, 2, SEQ], GR + 32 * KB)
    ki_t = place("ki_t", [P, SEQ], GR + 40 * KB)
    wi_t = place("wi_t", [HEAD + I_HEADS, SEQ], GR + 44 * KB)
    lat_t = place("lat_t", [P, SEQ], GR + 48 * KB)
    q2_t = place("q2_t", [P, 4, SEQ], GR + 52 * KB)
    mlp_v_t = place("mlp_v_t", [P, 4, SEQ], GR)
    mlp_u_t = place("mlp_u_t", [P, 4, SEQ], GR + 16 * KB)
    mlp_v = place("mlp_v", [P, NT, MLP], GR + 32 * KB)
    q_abs = [place(f"q_abs{i}", [P, 4, SEQ], GR + 32 * KB * i) for i in range(2)]
    sel_at = [P * b * (b + 1) // 2 for b in range(NT + 1)]
    select = place("select", [P, sel_at[NT]], GR + 68 * KB)
    tops = place("tops", [P, sel_at[NT] - sel_at[2]], GR + 32 * KB, mybir.dt.bfloat16)
    count_junk = [place(f"count_junk{i}", [P, SEQ], RR + 32 * KB + 2 * KB * i, mybir.dt.bfloat16) for i in range(2)]
    sq_two = place("sq_two", [P, D], RR + 28 * KB)
    relu_tmp = [place(f"relu_tmp{i}", [P, SEQ], RR + 28 * KB + 4 * KB * i) for i in range(2)]
    equal, ranks = (place(n, [P, SEQ], RR + 28 * KB + 4 * KB * i) for i, n in enumerate(("equal", "ranks")))
    lat = place("lat", [P, NT, LAT], RR + 24 * KB)
    lat_n_t = place("lat_n_t", [P, SEQ], RR + 40 * KB)
    kv_gain = place("kv_gain", [P, LAT], RR + 38 * KB)
    causal = place("causal", [P, P], RR + 38 * KB + 512)
    wi_rows = place("wi_rows", [P, NT, I_HEADS], RR + 39 * KB)
    limit = place("limit", [P, 6], RR + 39 * KB + 128, I32)
    trial = place("trial", [P, 6], RR + 39 * KB + 160, I32)
    keep = place("keep", [P, 6], RR + 39 * KB + 192, I32)
    bit = place("bit", [P, 2], RR + 39 * KB + 224, I32)
    counts = place("counts", [P, 6], RR + 39 * KB + 256)
    wanted = place("wanted", [P, 6], RR + 39 * KB + 288)
    one_col = place("one_col", [P, 1], RR + 39 * KB + 320)
    v_sum = place("v_sum", [P, NT], RR + 39 * KB + 352)
    v_mean_neg = place("v_mean_neg", [P, NT], RR + 39 * KB + 384)
    row_max = place("row_max", [P, NT * A_HEADS], RR + 39 * KB + 416)
    row_sum = place("row_sum", [P, NT * A_HEADS], RR + 39 * KB + 672)
    uk_raw = place("uk_raw", [P, A_HEADS, HEAD], RR)
    w_uv = place("w_uv", [P, A_HEADS, HEAD], RR + 22 * KB)
    ws_raw = place("ws_raw", [P, 8, P], RR + 4 * KB)
    ws_t = place("ws_t", [P, 8, P], RR + 8 * KB)
    bs_rows = place("bs_rows", [P, 4, P], RR + 12 * KB)
    upper = place("upper", [P, P], RR + 14 * KB)
    ones_head = place("ones_head", [P, HEAD], RR + 14 * KB + 512)
    shift_rows = place("shift_rows", [P, 4, P], RR + 20 * KB)
    mlp_rows = place("mlp_rows", [8, P], RR + 15 * KB)
    mlp_cols = place("mlp_cols", [P, 2, 4], RR + 39 * KB + 928)
    gm_tmp = [place(f"gm_tmp{i}", [P, 4, P], RR + 16 * KB + 2 * KB * i) for i in range(2)]
    uk_t = place("uk_t", [P, 4, LAT], RR + 36 * KB)
    p2 = [place(f"p2_{i}", [P, SEQ], XR + 32 * KB + 4 * KB * i) for i in range(3)] + [place("p2_3", [P, SEQ], RR + 4 * KB)]
    p2_t = place("p2_t", [P, NT, 4, P], XR + 44 * KB)
    o_lat = [place(f"o_lat{i}", [P, 4, P], XR + 60 * KB + 2 * KB * i) for i in range(2)]

    a_hi, a_lo, a_mm, a_evac = (sem(n) for n in ("a_hi", "a_lo", "a_mm", "a_evac"))
    a_in = [sem(f"a_in{i}") for i in range(2)]
    small2_in, lat_turned, lat_sq, lat_ready, lat_back = (sem(n) for n in ("small2_in", "lat_turned", "lat_sq", "lat_ready", "lat_back"))
    logit_mm, relu_done, score_added, bits_done, mask_ready = (
        sem(n) for n in ("logit_mm", "relu_done", "score_added", "bits_done", "mask_ready"))
    mix2_in, mix2_turned, ws_copied, ws_ready = (sem(n) for n in ("mix2_in", "mix2_turned", "ws_copied", "ws_ready"))
    mv_turned, mv_copied, mv_mean, mv_sq, mv_scaled, mv_ready = (
        sem(n) for n in ("mv_turned", "mv_copied", "mv_mean", "mv_sq", "mv_scaled", "mv_ready"))
    sv_mm, sv_copied, gm_ready, qa_mm, qa_ready = (sem(n) for n in ("sv_mm", "sv_copied", "gm_ready", "qa_mm", "qa_ready"))
    bs_in, keys_ready, keys_in, shift_mm, shift_scaled = (sem(n) for n in ("bs_in", "keys_ready", "keys_in", "shift_mm", "shift_scaled"))
    mlp_cols_turned, mlp_cols_ready = sem("mlp_cols_turned"), sem("mlp_cols_ready")
    ol_mm, ol_ready, sum_ready = sem("ol_mm"), sem("ol_ready"), sem("sum_ready")

    GELU = ACT.Gelu_apprx_tanh
    a_units = [([(qi2, P)], qi_t[:, 0, :], None), ([(ki2, HEAD + I_HEADS)], None, None), ([(qi2 + P, P)], qi_t[:, 1, :], None),
               ([(c2, LAT)], lat_t[:, :], None)]
    a_units += [([(q2 + P * i, P)], q2_t[:, i, :], None) for i in range(4)]
    a_units += [([(v2 + P * i, P)], mlp_v_t[:, i, :], GELU) for i in range(4)]
    a_units += [([(u2 + P * i, P)], mlp_u_t[:, i, :], GELU) for i in range(4)]
    A_UNITS = len(a_units)
    a_counts, a_landed = [], [0, 0]
    for n, (cols, _, _) in enumerate(a_units):
        a_landed[n % 2] += 16 * len(cols)
        a_counts.append(a_landed[n % 2])
    A_KEYS = 1
    LOGITS = [(h, b) for h in range(I_HEADS) for b in range(2, NT)]
    BITS_LATENTS, BITS_GATED = 13, 25
    BITS_TOP = 15
    SEARCHED = range(2, NT)
    BITS_STEPS = len(SEARCHED) + 4

    def width(b):
        return P * (b + 1)

    def top(b):
        return tops[:, sel_at[b] - sel_at[2]:sel_at[b + 1] - sel_at[2]]

    def sel(b):
        return select[:, sel_at[b]:sel_at[b + 1]]

    def a_load(sp, n):
        at_col = 0
        for c, m in a_units[n][0]:
            sp.dma_start(tile_of(raw[n % 2], P)[:, :, at_col:at_col + m],
                         a["w_in_2"][0].rearrange("(k p) n -> p k n", p=P)[:, :, c:c + m]).then_inc(a_in[n % 2], 16)
            at_col += m

    def a_width(n):
        return sum(m for _, m in a_units[n][0])

    def tile_of(buf, m):
        return buf[:].rearrange("p (k c) -> p k c", c=P)[:, :, 0:m]

    def mix2_first(sp):
        for n in range(2):
            sp.wait_ge(w_lo, down_1.end - 1 + n)
            a_load(sp, n)

    def mix2_sync(sp):
        sp.dma_start(kv_gain[:], a["kv_norm_g_2"].to_broadcast([P, LAT])).then_inc(small2_in, 16)
        sp.dma_start(causal[:], a["causal"]).then_inc(small2_in, 16)
        for n in range(2, A_UNITS):
            sp.wait_ge(a_lo, n - 1)
            a_load(sp, n)
            if n == A_KEYS + 1:
                sp.wait_ge(keys_ready, 1)
                sp.dma_start(ki_t[HEAD:P, :], ki_t[0:HEAD, :]).then_inc(keys_in, 16)
        sp.wait_ge(a_lo, A_UNITS)
        sp.dma_start(uk_raw[:], a["w_uk_2"][0].rearrange("h c d -> c h d")).then_inc(mix2_in, 16)
        sp.dma_start(ws_raw[:], a["gmlp_ws_2"][0].rearrange("g t s -> t g s")).then_inc(mix2_in, 16)
        sp.wait_ge(a_mm, A_UNITS)
        sp.dma_start(w_uv[:], a["w_uv_2"][0].rearrange("h c d -> c h d")).then_inc(bs_in, 16)
        for i, name in enumerate(("gmlp_ln_g_2", "gmlp_ln_b_2")):
            sp.dma_start(mlp_rows[4 * i:4 * i + 4, :], a[name].rearrange("o (i p) -> (o i) p", p=P)).then_inc(bs_in, 16)
        sp.dma_start(upper[:], a["upper"]).then_inc(bs_in, 16)
        for g in range(8):
            sp.dma_start(bs_rows[HEAD * (g % 2):HEAD * (g % 2 + 1), g // 2, :],
                         a["gmlp_bs_2"][0, g:g + 1, :].to_broadcast([HEAD, P])).then_inc(bs_in, 16)
        load_gains(sp, "ln2_g_2", "ln2_b_2")
        sp.wait_ge(mix2_turned, 1)
        down_first(sp, down_mix2)
        sp.wait_ge(att_ready, 2 * NT)
        sp.wait_ge(gm_ready, NT)

    def a_unit(n, halves):
        t, m, slot = nc.tensor, a_width(n), n % 2
        for k in range(KD):
            for i, (l, r) in enumerate(((split_hi, x_hi), (split_hi, x_lo), (split_lo, x_hi))):
                for half in halves:
                    ins = t.matmul(bank(2 * slot + half)[0:m], l[slot][:, P * k:P * k + m], r[:, k, HALF * half:HALF * (half + 1)],
                                   start=(k == 0 and i == 0), stop=(k == KD - 1 and i == 2))
        return ins

    def a_split(act, n):
        m, slot = a_width(n), n % 2
        if n >= 2:
            act.wait_ge(a_mm, n - 1)
        else:
            act.wait_ge(w_mm, down_1.end)
        act.wait_ge(a_in[slot], a_counts[n])
        nc.scalar.copy(tile_of(split_hi[slot], m), tile_of(raw[slot], m)).then_inc(a_hi, 1)

    def mix2_begin_scalar(act):
        for n in range(2):
            a_split(act, n)

    def mix2_begin_tensor(pe, t):
        end_tensor(pe, down_1, lambda n: pe.wait_ge(a_lo, n + 1), a_unit, lambda ins: ins.then_inc(a_mm, 1))

    def mix2_tensor(pe, t):
        def unit(n):
            pe.wait_ge(a_lo, n + 1)
            if n >= 2:
                pe.wait_ge(a_evac, n - 1)
            a_unit(n, range(2)).then_inc(a_mm, 1)

        def turn_values(n):
            if n >= 4:
                pe.wait_ge(mv_copied, n - 3)
            for i in range(4):
                ins = t.transpose(bank(4 + n % 4, P, P * i), mlp_v_t[:, i, P * n:P * (n + 1)], ident[:])
            ins.then_inc(mv_turned, 1)

        unit(2)
        pe.wait_ge(a_evac, A_KEYS + 1)
        for b in range(NT):
            ins = t.transpose(bank(6, I_HEADS, I_HEADS * b), wi_t[HEAD:HEAD + I_HEADS, P * b:P * (b + 1)],
                              ident[HEAD:HEAD + I_HEADS, HEAD:HEAD + I_HEADS])
        ins.then_inc(lat_turned, 1)
        for i, (h, b) in enumerate(LOGITS):
            if i == 1:
                pe.wait_ge(lat_ready, 1)
            elif i >= 2:
                pe.wait_ge(relu_done, i - 1)
            if h == 1 and b == SEARCHED[0]:
                pe.wait_ge(keys_in, 16)
            if h == 2 and b == SEARCHED[0]:
                pe.wait_ge(a_evac, 3)
            rows = slice(HEAD * (h % 2), HEAD * (h % 2 + 1))
            for s0 in range(0, width(b), HALF):
                n = min(HALF, width(b) - s0)
                ins = t.matmul(bank(4 + 2 * (i % 2) + s0 // HALF, n), qi_t[rows, h // 2, P * b:P * (b + 1)], ki_t[rows, s0:s0 + n],
                               start=True, stop=True)
            ins.then_inc(logit_mm, 1)
        unit(3)
        unit(4)
        pe.wait_ge(a_evac, 4)
        pe.wait_ge(relu_done, len(LOGITS))
        for b in range(NT):
            ins = t.transpose(bank(4 + b // 4, P, P * (b % 4)), lat_t[:, P * b:P * (b + 1)], ident[:])
        ins.then_inc(lat_turned, 1)
        for n in range(5, A_UNITS):
            unit(n)
            if n == 9:
                pe.wait_ge(lat_ready, NT + 1)
                for b in range(NT):
                    ins = t.transpose(bank(4 + b // 4, P, P * (b % 4)), lat[:, b, :], ident[:])
                ins.then_inc(lat_turned, 1)
            elif n == 12:
                pe.wait_ge(lat_back, 2)
                pe.wait_ge(a_evac, 12)
                for b in range(4):
                    turn_values(b)
            elif n == 13:
                for b in range(4, NT):
                    turn_values(b)
        pe.wait_ge(mix2_in, 16 * 2)
        pe.wait_ge(mv_copied, NT)
        for i in range(4):
            ins = t.transpose(bank(6, P, P * i), uk_raw[:, 2 * i:2 * i + 2, :].rearrange("c h d -> c (h d)"), ident[:])
        ins.then_inc(mix2_turned, 1)
        for g in range(8):
            ins = t.transpose(bank(4 + g // 4, P, P * (g % 4)), ws_raw[:, g, :], ident[:])
        ins.then_inc(mix2_turned, 1)
        pe.wait_ge(a_evac, A_UNITS)
        pe.wait_ge(ws_copied, 2)

        def queries(h):
            rows = slice(HEAD * (h % 2), HEAD * (h % 2 + 1))
            for half in range(2):
                i = 2 * h + half
                if i >= 4:
                    pe.wait_ge(qa_ready, i - 3)
                t.matmul(bank(i % 4), uk_t[rows, h // 2, :], q2_t[rows, h // 2, HALF * half:HALF * (half + 1)],
                         start=True, stop=True).then_inc(qa_mm, 1)

        for h in range(4):
            queries(h)
        pe.wait_ge(ws_ready, 1)
        pe.wait_ge(bs_in, 16 * 12)
        t.transpose(bank(6, 8), mlp_rows[:], ident[0:8, 0:8]).then_inc(mlp_cols_turned, 1)
        for g in range(8):
            ins = t.matmul(bank(7, P, P * (g // 2))[HEAD * (g % 2):HEAD * (g % 2 + 1)], ones_head[:], ws_t[:, g, :],
                           start=True, stop=True)
        ins.then_inc(shift_mm, 1)
        for n in range(NT):
            pe.wait_ge(mv_ready, n + 1)
            if n == 2:
                pe.wait_ge(mlp_cols_ready, 1)
            if n == 3:
                pe.wait_ge(shift_scaled, 4)
            if n >= 4:
                pe.wait_ge(sv_copied, 4 * (n - 3))
            for g in range(8):
                ins = t.matmul(bank(4 + n % 4, P, P * (g // 2))[HEAD * (g % 2):HEAD * (g % 2 + 1)],
                               mlp_v[:, n, HEAD * g:HEAD * (g + 1)], ws_t[:, g, :], start=True, stop=True)
            ins.then_inc(sv_mm, 1)
        for h in range(4, A_HEADS):
            queries(h)

        def scores(i):
            b, h = i // A_HEADS, i % A_HEADS
            if i >= 2:
                pe.wait_ge(max_ready, NT + i - 1)
            for s0 in range(0, width(b), HALF):
                n = min(HALF, width(b) - s0)
                ins = t.matmul(bank(2 * (i % 2) + s0 // HALF, n), q_abs[h // 4][:, h % 4, P * b:P * (b + 1)], lat_n_t[:, s0:s0 + n],
                               start=True, stop=True)
            ins.then_inc(scores_mm, 1)

        def turn_probs(i):
            b = i // A_HEADS
            pe.wait_ge(probs_ready, ITEMS + i + 1)
            if i:
                pe.wait_ge(probs_t_ready, ITEMS + i)
            for k in range(b + 1):
                ins = t.transpose(bank(4 + k // 4, P, P * (k % 4)), p2[i % 4][:, P * k:P * (k + 1)], ident[:])
            ins.then_inc(probs_turned, 1)

        def values(i):
            b, half = i // 2, i % 2
            pe.wait_ge(probs_t_ready, ITEMS + 4 * i + 4)
            if i:
                pe.wait_ge(ol_ready, i)
            for k in range(b + 1):
                ins = t.matmul(bank(6), lat[:, k, :], p2_t[:, k].rearrange("p h q -> p (h q)"), start=(k == 0), stop=(k == b))
            ins.then_inc(ol_mm, 1)

        def outputs(i):
            b, half = i // 2, i % 2
            pe.wait_ge(ol_ready, i + 1)
            if b and half == 0:
                pe.wait_ge(att_ready, NT + b)
            for h in range(4 * half, 4 * half + 4):
                ins = t.matmul(bank(7, P, P * (h // 2))[HEAD * (h % 2):HEAD * (h % 2 + 1)], w_uv[:, h, :], o_lat[half][:, h % 4, :],
                               start=True, stop=True)
            ins.then_inc(att_mm, 1)

        pe.wait_ge(qa_ready, 2 * A_HEADS)
        pe.wait_ge(sv_copied, NT)
        for i in range(ITEMS2 + LAG + 2):
            if i < ITEMS2:
                scores(i)
            if LAG <= i < ITEMS2 + LAG:
                turn_probs(i - LAG)
            if i >= LAG + 4 and (i - LAG) % 4 == 0:
                values((i - LAG) // 4 - 1)
            if i >= LAG + 5 and (i - LAG) % 4 == 1:
                outputs((i - LAG) // 4 - 1)

    ITEMS2 = NT * A_HEADS
    LAG = 3

    def mix2_scalar(act, steps):
        s = nc.scalar

        def store(n):
            m, slot = a_width(n), n % 2
            act.wait_ge(a_mm, n + 1)
            if n == 0:
                act.wait_ge(res_out, 16 * NT * 3)
            src = psum[0:m, 2 * HALF * slot:2 * HALF * (slot + 1)]
            if n == A_KEYS:
                s.copy(ki_t[0:HEAD, :], src[0:HEAD]).then_inc(keys_ready, 1)
                s.copy(wi_t[HEAD:m, :], src[HEAD:m]).then_inc(a_evac, 1)
                return
            if a_units[n][2] is None:
                s.copy(a_units[n][1], src).then_inc(a_evac, 1)
            else:
                s.activation(a_units[n][1], src, a_units[n][2]).then_inc(a_evac, 1)

        for n in range(A_UNITS):
            if n >= 2:
                a_split(act, n)
            if n:
                store(n - 1)
            if n == 3:
                for i, (h, b) in enumerate(LOGITS):
                    act.wait_ge(logit_mm, i + 1)
                    if i >= 2:
                        act.wait_ge(score_added, i - 1)
                    src = psum[:, HALF * (4 + 2 * (i % 2)):HALF * (4 + 2 * (i % 2)) + width(b)]
                    s.activation(relu_tmp[i % 2][:, 0:width(b)], src, ACT.Relu, scale=HEAD ** -0.5).then_inc(relu_done, 1)
            elif n == 6:
                act.wait_ge(lat_turned, 2)
                for b in range(NT):
                    s.activation(lat[:, b, :], bank(4 + b // 4, P, P * (b % 4)), ACT.Square,
                                 accum_out=stat_a[:, b:b + 1]).then_inc(lat_sq, 1)
            elif n == 9:
                take_root(act)
            elif n == 11:
                act.wait_ge(lat_turned, 3)
                for i in range(2):
                    s.copy(lat_n_t[:, HALF * i:HALF * (i + 1)], bank(4 + i)).then_inc(lat_back, 1)
            elif n in (13, 14):
                act.wait_ge(bits_done, BITS_STEPS * BITS_TOP)
                for b in range(4 * (n - 13), 4 * (n - 12)):
                    act.wait_ge(mv_turned, b + 1)
                    s.activation(mlp_v[:, b, :], bank(4 + b % 4), ACT.Copy, accum_out=v_sum[:, b:b + 1]).then_inc(mv_copied, 1)
                if n == 14:
                    act.wait_ge(mv_mean, 1)
                    act.wait_ge(score_added, len(LOGITS))
                    for b in range(NT):
                        if b >= 2:
                            act.wait_ge(mv_sq, b - 1)
                        s.activation(sq_two[:, MLP * (b % 2):MLP * (b % 2 + 1)], mlp_v[:, b, :], ACT.Square,
                                     bias=v_mean_neg[:, b:b + 1], accum_out=stat_a[:, b:b + 1]).then_inc(mv_sq, 1)
        store(A_UNITS - 1)
        act.wait_ge(mix2_turned, 1)
        s.copy(uk_t[:].rearrange("p a c -> p (a c)"), bank(6)).then_inc(ws_copied, 2)
        act.wait_ge(mix2_turned, 2)
        s.copy(ws_t[:].rearrange("p g t -> p (g t)"), psum[:, 4 * HALF:6 * HALF]).then_inc(ws_copied, 1)

        def queries(h):
            for half in range(2):
                i = 2 * h + half
                act.wait_ge(qa_mm, i + 1)
                s.mul(q_abs[h // 4][:, h % 4, HALF * half:HALF * (half + 1)], bank(i % 4), HEAD ** -0.5).then_inc(qa_ready, 1)

        for h in range(4):
            queries(h)
        take_root(act)
        act.wait_ge(mv_scaled, 1)
        for n in range(NT):
            s.activation(mlp_v[:, n, :], mlp_v[:, n, :], ACT.Identity, scale=stat_b[:, NT + n:NT + n + 1],
                         bias=stat_c[:, n:n + 1]).then_inc(mv_ready, 1)
        act.wait_ge(mlp_cols_turned, 1)
        s.copy(mlp_cols[:].rearrange("p a i -> p (a i)"), bank(6, 8)).then_inc(mlp_cols_ready, 1)
        act.wait_ge(shift_mm, 1)
        act.wait_ge(mlp_cols_ready, 1)
        for i in range(4):
            s.mul(shift_rows[:, i, :], bank(7, P, P * i), mlp_cols[:, 1, i:i + 1]).then_inc(shift_scaled, 1)
        for n in range(NT):
            act.wait_ge(sv_mm, n + 1)
            if n >= 2:
                act.wait_ge(gm_ready, n - 1)
            for i in range(4):
                s.mul(gm_tmp[n % 2][:, i, :], bank(4 + n % 4, P, P * i), mlp_cols[:, 0, i:i + 1]).then_inc(sv_copied, 1)
        for h in range(4, A_HEADS):
            queries(h)

        def exponentials(i):
            w = width(i // A_HEADS)
            act.wait_ge(max_ready, NT + i + 1)
            p = p2[i % 4][:, 0:w]
            s.activation(p, p, ACT.Exp, bias=row_max[:, i:i + 1], accum_out=row_sum[:, i:i + 1]).then_inc(exp_ready, 1)

        def copy_probs(i):
            b, h = i // A_HEADS, i % A_HEADS
            act.wait_ge(probs_turned, ITEMS + i + 1)
            if h % 4 == 0 and i:
                act.wait_ge(ol_mm, i // 4)
            s.copy(p2_t[:, 0:b + 1, h % 4, :], psum[:, 4 * HALF:4 * HALF + width(b)].rearrange("p (k q) -> p k q", q=P)).then_inc(probs_t_ready, 1)

        def finish(i):
            b, half = i // 2, i % 2
            act.wait_ge(ol_mm, i + 1)
            if i >= 2:
                act.wait_ge(att_mm, ITEMS + i - 1)
            s.copy(o_lat[half][:].rearrange("p h q -> p (h q)"), bank(6)).then_inc(ol_ready, 1)
            if i % 2 == 0 and i:
                last(b - 1)

        def last(b):
            act.wait_ge(att_mm, ITEMS + 2 * b + 2)
            s.copy(yc_t[:, 0:4, P * b:P * (b + 1)], bank(7).rearrange("p (k q) -> p k q", q=P)).then_inc(att_ready, 1)

        for i in range(ITEMS2 + LAG + 1):
            if i < ITEMS2:
                exponentials(i)
            if LAG <= i < ITEMS2 + LAG:
                copy_probs(i - LAG)
            if i >= LAG + 4 and (i - LAG) % 4 == 0:
                finish((i - LAG) // 4 - 1)
        last(NT - 1)
        act.wait_ge(gm_ready, NT)
        act.wait_ge(att_ready, 2 * NT)

    def mix2_vector(dve, v, steps):
        one = steps.add
        dve.wait_ge(lat_turned, 1)
        one(v.tensor_scalar(wi_rows[:].rearrange("p n h -> p (n h)"), bank(6, NT * I_HEADS), I_HEADS ** -0.5, None, ALU.mult))
        one(v.memset(one_col[:], 1.0))
        steps.settle()
        dve.sem_inc(lat_ready, 1)
        n_b = len(SEARCHED)
        for i, (h, b) in enumerate(LOGITS):
            dve.wait_ge(relu_done, i + 1)
            r, w = relu_tmp[i % 2][:, 0:width(b)], wi_rows[:, b, h:h + 1]
            if h == 0:
                v.tensor_scalar(sel(b), r, w, None, ALU.mult).then_inc(score_added, 1)
            else:
                dve.wait_ge(score_added, i - n_b + 1)
                v.scalar_tensor_tensor(sel(b), r, w, sel(b), ALU.mult, ALU.add).then_inc(score_added, 1)
        dve.wait_ge(score_added, len(LOGITS))
        dve.wait_ge(small2_in, 32)
        for b in SEARCHED:
            diagonal = select[:, sel_at[b + 1] - P:sel_at[b + 1]]
            one(v.tensor_tensor(diagonal, diagonal, causal[:], ALU.add))
        steps.settle()
        limits = limit[:].bitcast(F32)

        def count_all(op, against):
            for j, b in enumerate(SEARCHED):
                if j >= 2:
                    dve.wait_ge(dve_steps, steps.n - 1)
                one(v.tensor_scalar(count_junk[j % 2][:, 0:width(b)], sel(b), against[j], 0.0, op, ALU.add, counts[:, j:j + 1]))

        count_all(ALU.is_ge, [0.0] * n_b)
        one(v.memset(bit[:, 0:1], 1 << 30))
        one(v.tensor_copy(tops[:], select[:, sel_at[2]:sel_at[NT]].bitcast(mybir.dt.bfloat16)[:, 1::2]))
        steps.settle()
        one(v.tensor_scalar(limit[:], counts[:], float(TOP), -1.0, ALU.is_lt, ALU.mult))
        steps.settle()
        per = BITS_STEPS

        def next_bit(i, keys):
            done = per * i
            v.tensor_tensor(trial[:], limit[:], bit[:, 0:1].to_broadcast([P, n_b]), ALU.bitwise_xor).then_inc(bits_done, 1)
            dve.wait_ge(bits_done, done + 1)
            for j, b in enumerate(SEARCHED):
                if j >= 2:
                    dve.wait_ge(bits_done, done + j)
                v.tensor_scalar(count_junk[j % 2][:, 0:width(b)], keys(b), trial[:, j:j + 1].bitcast(F32), 0.0, ALU.is_ge, ALU.add,
                                counts[:, j:j + 1]).then_inc(bits_done, 1)
            dve.wait_ge(bits_done, done + n_b + 1)
            v.tensor_scalar(keep[:], counts[:], float(TOP), -1.0, ALU.is_ge, ALU.mult).then_inc(bits_done, 1)
            dve.wait_ge(bits_done, done + n_b + 2)
            v.scalar_tensor_tensor(limit[:], keep[:], bit[:, 0:1], limit[:], ALU.bitwise_and, ALU.bitwise_xor).then_inc(bits_done, 1)
            dve.wait_ge(bits_done, done + n_b + 3)
            v.tensor_scalar(bit[:, 0:1], bit[:, 0:1], 1, None, ALU.logical_shift_right).then_inc(bits_done, 1)
            dve.wait_ge(bits_done, done + n_b + 4)

        with dve.Fori(0, BITS_LATENTS) as i:
            next_bit(i, top)
        dve.wait_ge(lat_sq, NT)
        one(v.tensor_scalar(stat_a[:, NT:2 * NT], stat_a[:, 0:NT], 1.0 / LAT, LN_EPS, ALU.mult, ALU.add))
        steps.settle()
        end_root(dve, v, steps)
        dve.wait_ge(small2_in, 32)
        for b in range(NT):
            v.scalar_tensor_tensor(lat[:, b, :], bank(4 + b // 4, P, P * (b % 4)), stat_b[:, NT + b:NT + b + 1], kv_gain[:],
                                   ALU.mult, ALU.mult).then_inc(lat_ready, 1)
        with dve.Fori(BITS_LATENTS, BITS_TOP) as i:
            next_bit(i, top)
        with dve.Fori(BITS_TOP, BITS_GATED) as i:
            next_bit(i, sel)
        dve.wait_ge(mv_sq, NT)
        one(v.tensor_scalar(stat_a[:, NT:2 * NT], stat_a[:, 0:NT], 1.0 / MLP, LN_EPS, ALU.mult, ALU.add))
        steps.settle()
        end_root(dve, v, steps)
        one(v.tensor_tensor(stat_c[:, 0:NT], v_mean_neg[:], stat_b[:, NT:2 * NT], ALU.mult))
        steps.settle()
        dve.sem_inc(mv_scaled, 1)
        with dve.Fori(BITS_GATED, 31) as i:
            next_bit(i, sel)

        def choose(b, part):
            j = b - SEARCHED[0]
            eq, rank, lim, need = equal[:, 0:width(b)], ranks[:, 0:width(b)], limits[:, j:j + 1], wanted[:, j:j + 1]
            steps.settle()
            if part == 0:
                one(v.tensor_scalar(count_junk[j % 2][:, 0:width(b)], sel(b), lim, 0.0, ALU.is_gt, ALU.add, counts[:, j:j + 1]))
                one(v.tensor_scalar(eq, sel(b), lim, None, ALU.is_equal))
            elif part == 1:
                one(v.tensor_scalar(need, counts[:, j:j + 1], -1.0, float(TOP), ALU.mult, ALU.add))
                one(v.tensor_tensor_scan(rank, one_col[:].to_broadcast([P, width(b)]), eq, 0.0, ALU.mult, ALU.add))
            elif part == 2:
                one(v.scalar_tensor_tensor(eq, rank, need, eq, ALU.is_le, ALU.mult))
            elif part == 3:
                one(v.scalar_tensor_tensor(sel(b), sel(b), lim, eq, ALU.is_gt, ALU.add))
            elif part == 4:
                one(v.tensor_scalar(sel(b), sel(b), -NEG, NEG, ALU.mult, ALU.add))

        def maximum(i):
            b = i // A_HEADS
            w = width(b)
            dve.wait_ge(scores_mm, ITEMS + i + 1)
            if i >= 4:
                dve.wait_ge(probs_turned, ITEMS + i - 3)
            if i % A_HEADS == 0:
                dve.wait_ge(mask_ready, 1)
            one(v.tensor_tensor_reduce(p2[i % 4][:, 0:w], psum[:, 2 * HALF * (i % 2):2 * HALF * (i % 2) + w], sel(b), 1.0, NEG,
                                       ALU.add, ALU.max, row_max[:, i:i + 1]))
            steps.settle()
            v.tensor_scalar(row_max[:, i:i + 1], row_max[:, i:i + 1], -1.0, None, ALU.mult).then_inc(max_ready, 1)

        def reciprocal(i):
            dve.wait_ge(exp_ready, ITEMS + i + 1)
            v.reciprocal(row_sum[:, i:i + 1], row_sum[:, i:i + 1]).then_inc(sum_ready, 1)

        for i in range(ITEMS2 + 1):
            if i < ITEMS2:
                maximum(i)
            if i:
                reciprocal(i - 1)
            b, h = i // A_HEADS + 1, i % A_HEADS
            if b in SEARCHED:
                choose(b, h)

    def mix2_gpsimd(pool, steps):
        g = nc.gpsimd
        for n in range(A_UNITS):
            m, slot = a_width(n), n % 2
            pool.wait_ge(a_hi, n + 1)
            g.tensor_tensor(tile_of(split_lo[slot], m), tile_of(raw[slot], m), tile_of(split_hi[slot], m), ALU.subtract).then_inc(a_lo, 1)
            if n == 1:
                pool.wait_ge(small2_in, 32)
                steps.add(g.memset(select[:, sel_at[1]:sel_at[1] + P], 0.0))
                steps.add(g.tensor_copy(select[:, 0:P], causal[:]))
                steps.add(g.tensor_copy(select[:, sel_at[1] + P:sel_at[2]], causal[:]))
                steps.settle()
                pool.sem_inc(mask_ready, 1)
            elif n == 14:
                pool.wait_ge(mv_copied, NT)
                g.tensor_scalar(v_mean_neg[:], v_sum[:], -1.0 / MLP, 1.0, ALU.mult, ALU.mult).then_inc(mv_mean, 1)
        pool.wait_ge(ws_copied, 3)
        pool.wait_ge(bs_in, 16 * 12)
        steps.add(g.memset(ones_head[:], 1.0))
        steps.settle()
        g.tensor_tensor(ws_t[:], ws_t[:], upper[:].unsqueeze(1).to_broadcast([P, 8, P]), ALU.mult).then_inc(ws_ready, 1)
        pool.wait_ge(shift_scaled, 4)
        steps.add(g.tensor_tensor(bs_rows[:], bs_rows[:], shift_rows[:], ALU.add))
        steps.settle()
        for n in range(NT):
            pool.wait_ge(sv_copied, 4 * n + 4)
            tmp = gm_tmp[n % 2]
            steps.add(g.tensor_tensor(tmp[:], tmp[:], bs_rows[:], ALU.add))
            steps.settle()
            g.tensor_tensor(yc_t[:, 4:8, P * n:P * (n + 1)], tmp[:], mlp_u_t[:, :, P * n:P * (n + 1)], ALU.mult).then_inc(gm_ready, 1)
        for i in range(ITEMS2):
            w = width(i // A_HEADS)
            pool.wait_ge(sum_ready, i + 1)
            p = p2[i % 4][:, 0:w]
            g.tensor_scalar(p, p, row_sum[:, i:i + 1], 1.0, ALU.mult, ALU.mult).then_inc(probs_ready, 1)

    block = ctx.enter_context(nc.Block())

    N_ADA = 6 * D // HALF

    @block.sync
    def _(sp):
        sp.dma_start(c_cols[:], a["c"].rearrange("o (p k) -> (o p) k", k=KD)).then_inc(small_in, 16)
        sp.dma_start(ident[:], a["ident"]).then_inc(ident_in, 16)
        w_ada = a["w_ada"][0].rearrange("(p k) n -> p k n", k=KD)
        for j in range(N_ADA):
            if j >= 3:
                sp.wait_ge(ada_mm, j - 2)
            cols = slice(HALF * j, HALF * (j + 1))
            sp.dma_start(ada_w[j % 3][:], w_ada[:, :, cols]).then_inc(ada_in[j % 3], 16)
            sp.dma_start(ada_b[j % 3][:], a["b_ada"][:, cols]).then_inc(ada_in[j % 3], 16)
        w_in = a["w_in"][0].rearrange("(k p) n -> p k n", p=P)

        def load_unit(n):
            at_col = 0
            for c, m in win_units[n][0]:
                dst = win_raw[n % 2][:].rearrange("p (k c) -> p k c", c=P)
                sp.dma_start(dst[:, :, at_col:at_col + m], w_in[:, :, c:c + m]).then_inc(win_in[n % 2], 16)
                at_col += m

        sp.wait_ge(vec_used, 1)
        sp.wait_ge(carry_ready, 2)
        for n in range(4):
            if n >= 2:
                sp.wait_ge(win_lo, n - 1)
            load_unit(n)
        taps = GROUPS * GC
        sp.wait_ge(k_ready, 1)
        sp.dma_start(k_shift[7 * GC:8 * GC, :], k_sum[0:GC, 1, :]).then_inc(k_shift_in, 16)
        sp.wait_ge(k_ready, 2)
        for s in range(CH):
            sp.dma_start(toep_dram[14 - s], k_sum[GC * s:GC * (s + 1), 0, :]).then_inc(k_in_dram, 16)
            if s:
                sp.dma_start(toep_dram[7 - s], k_sum[GC * s:GC * (s + 1), 1, :]).then_inc(k_in_dram, 16)
        sp.wait_ge(k_in_dram, 16 * 15)
        for s in range(CH):
            sp.dma_start(toep[GC * s:GC * (s + 1), :, :],
                         toep_dram[7 - s:15 - s].rearrange("t c n -> c t n")).then_inc(toep_in, 16)
        for n in range(4, len(win_units)):
            sp.wait_ge(win_lo, n - 1)
            load_unit(n)
        mix_sync(sp)

    @block.scalar
    def _(act):
        steps = Steps(act, act_steps)
        lam = lam_rows
        act.dma_start(lam[:, 0, :], a["lam_re"][0].rearrange("d (q e) p -> (d q) (e p)", e=2)).then_inc(ssm_in, 16)
        act.dma_start(lam[:, 1, :], a["lam_im"][0].rearrange("d (q e) p -> (d q) (e p)", e=2)).then_inc(ssm_in, 16)
        act.dma_start(log_dt_rows[:], a["log_dt"][0].rearrange("d (q e) -> (d q) e", e=2)).then_inc(ssm_in, 16)
        for i, name in enumerate(("b_re", "b_im")):
            for d in range(2):
                act.dma_start(b_raw[:, i, d, :, :],
                              a[name][0, d].rearrange("(q e) p c -> (e p) q c", e=2)).then_inc(ssm_in, 16)
        for i, name in enumerate(("c_re", "c_im")):
            for twice in range(2):
                act.dma_start(c_rows[:, i, :, twice, :],
                              a[name][0].rearrange("(b g) c p -> (g c) b p", b=3)).then_inc(ssm_in, 16)
        act.dma_start(dskip_rows[:], a["d_skip"][0].rearrange("(g c) -> g c", c=GC)).then_inc(ssm_in, 16)
        wide = 2 * D_FF // P
        for i, src in enumerate((a["conv_w"][0, 0], a["conv_w"][0, 1])):
            act.dma_start(vec_rows[0][wide * i:wide * (i + 1), :], src.rearrange("(f p) -> f p", p=P)).then_inc(vec_in, 16)
        for i, src in enumerate((a["conv_w"][0, 2], a["conv_b"][0])):
            act.dma_start(vec_rows[1][wide * i:wide * (i + 1), :], src.rearrange("(f p) -> f p", p=P)).then_inc(vec_in, 16)
        for i, name in enumerate(("g_pre_mix", "g_pre_ffn")):
            at_row = 2 * wide + KD * i
            act.dma_start(vec_rows[0][at_row:at_row + KD, :], a[name][0].rearrange("(k p) -> k p", p=P)).then_inc(vec_in, 16)
        x = a["x"][0].rearrange("(n p) d -> p n d", p=P)
        for n in range(NT):
            act.dma_start(x_rows[:, n, :], x[:, n, :]).then_inc(x_in, 16)
        act.dma_start(row_a[:], a["g_post_mix"].to_broadcast([P, D])).then_inc(bc_in, 16)
        act.dma_start(row_b[:], a["g_post_ffn"].to_broadcast([P, D])).then_inc(bc_in, 16)
        act.dma_start(sink_row[:], a["sink"].to_broadcast([P, Q_HEADS])).then_inc(bc_in, 16)

        act.wait_ge(prm_angle, 1)
        nc.scalar.activation(prm[:, 10, :], prm[:, 7, :], ACT.Sin).then_inc(prm_trig, 1)
        nc.scalar.activation(prm[:, 11, :], prm[:, 7, :], ACT.Sin, scale=0.5).then_inc(prm_trig, 1)

        act.wait_ge(x_in, 16 * NT)
        for n in range(NT):
            if n:
                act.wait_ge(x_sq, n)
            nc.scalar.activation(junk[:], x_rows[:, n, :], ACT.Square, accum_out=stat_a[:, n:n + 1]).then_inc(x_sq, 1)
        act.wait_ge(x_var, 1)
        nc.scalar.activation(stat_b[:, 0:NT], stat_a[:, NT:2 * NT], ACT.Sqrt).then_inc(x_std, 1)
        for i in range(12):
            act.wait_ge(win_turned, i + 1)
            ri, d, q = i // 6, i // 3 % 2, 4 * (i % 3)
            nc.scalar.copy(state_in[:, ri, d, q:q + 4, :], bank(4 + i % 2).rearrange("p (q m) -> p q m", q=4)).then_inc(win_ready, 1)
        def split(n):
            if n >= 2:
                act.wait_ge(win_mm, n - 1)
            act.wait_ge(win_in[n % 2], win_counts[n])
            nc.scalar.copy(win_upper[n % 2][:], win_raw[n % 2][:]).then_inc(win_hi, 1)

        def store(n):
            act.wait_ge(win_mm, n + 1)
            nc.scalar.copy(win_units[n][1], psum[:, 2 * HALF * (1 + n % 3):2 * HALF * (2 + n % 3)]).then_inc(z_ready, 1)

        act.wait_ge(mod_ready, 1)
        for n in range(2):
            split(n)
        for i in range(2 * KD):
            k = i // 2
            act.wait_ge(x_turned, i + 1)
            if i >= 2:
                act.wait_ge(h_ready, i - 1)
            nc.scalar.activation(h_tmp[i % 2][:], bank(i % 2), ACT.Identity,
                                 scale=mod_cols[:, 1, k:k + 1], bias=mod_cols[:, 0, k:k + 1]).then_inc(h_made, 1)
        for n in range(2, len(win_units)):
            split(n)
            store(n - 2)
        for n in range(len(win_units) - 2, len(win_units)):
            store(n)
        mix_scalar(act, steps)

    def inverse_root(v, steps, var, cols=slice(0, NT)):
        root, y = stat_b[:, cols], stat_b[:, NT + cols.start:NT + cols.stop]
        steps.add(v.reciprocal(y, root))
        steps.settle()
        steps.add(v.tensor_tensor(root, y, y, ALU.mult))
        steps.settle()
        steps.add(v.tensor_tensor(root, root, var, ALU.mult))
        steps.settle()
        steps.add(v.tensor_scalar(root, root, -0.5, 1.5, ALU.mult, ALU.add))
        steps.settle()
        steps.add(v.tensor_tensor(y, y, root, ALU.mult))
        steps.settle()

    def x_norm(dve, v, steps):
        dve.wait_ge(x_sq, NT)
        steps.add(v.tensor_scalar(stat_a[:, NT:2 * NT], stat_a[:, 0:NT], 1.0 / D, RMS_EPS, ALU.mult, ALU.add))
        steps.settle()
        dve.sem_inc(x_var, 1)
        dve.wait_ge(x_std, 1)
        inverse_root(v, steps, stat_a[:, NT:2 * NT])
        for n in range(NT):
            v.tensor_scalar(x_rows[:, n, :], x_rows[:, n, :], stat_b[:, NT + n:NT + n + 1], None, ALU.mult).then_inc(x_scaled, 1)


    @block.vector
    def _(dve):
        steps = Steps(dve, dve_steps)
        v = nc.vector
        v.memset(ones_row[:], 1.0).then_inc(c_spread, 1)
        dve.wait_ge(small_in, 16)
        v.tensor_copy(c_bcast[:], c_cols[:].unsqueeze(2).to_broadcast([P, KD, P])).then_inc(c_spread, 1)
        dve.wait_ge(ssm_in, 16 * 12)
        v.tensor_copy(lam_rows[:, 2, :].rearrange("r (e p) -> r e p", e=2),
                      log_dt_rows[:].unsqueeze(2).to_broadcast([GROUPS, 2, STATE])).then_inc(dt_spread, 1)
        dve.wait_ge(rows_turned, 1)
        wide = 2 * D_FF // P
        for i in range(4):
            src = bank(2 + i // 2, wide, wide * (i % 2)).rearrange("p (g f) -> p f g", g=2)
            steps.add(v.tensor_copy(conv_cols[:, :, :, i], src))
        steps.add(v.tensor_copy(norm_cols[:].rearrange("p a k -> p (a k)"), bank(2, 2 * KD, 2 * wide)))
        steps.settle()
        dve.sem_inc(vec_used, 1)
        dve.wait_ge(c_turned, 2)
        steps.add(v.memset(c_pad[:], 0.0))
        steps.settle()
        for e in range(2):
            half = slice(STATE * e, STATE * (e + 1))
            for i, sign in enumerate((1.0, -1.0)):
                src = bank(4 + i, GROUPS * GC)[half].rearrange("p (q e c) -> p q e c", e=2, c=GC)[:, :, e, :]
                steps.add(v.tensor_scalar(c_plain[half, i], src, sign, None, ALU.mult))
                steps.add(v.tensor_scalar(c_pad[half, i, :, e, :], src, sign, None, ALU.mult))
        steps.settle()
        dve.sem_inc(c_ready, 2)
        dve.wait_ge(lam_turned, 1)
        steps.add(v.tensor_copy(dskip_cols[:], bank(7, GROUPS, 96)[0:GC]))
        steps.add(v.tensor_copy(prm[:, 0:3, :], bank(7, 96).rearrange("p (a c) -> p a c", a=3)[:, :, 0:2 * PAIRS]))
        steps.settle()
        col = lambda i: prm[:, i, :]

        def exponential(dst, src, t0, t1, t_int):
            one = steps.add
            one(v.tensor_scalar(t0, src, -87.0, 88.0, ALU.max, ALU.min))
            steps.settle()
            one(v.tensor_scalar(t1, t0, 1 / math.log(2), ROUND, ALU.mult, ALU.add))
            steps.settle()
            one(v.tensor_scalar(t1, t1, -ROUND, None, ALU.add))
            steps.settle()
            one(v.scalar_tensor_tensor(t0, t1, -LN2_HI, t0, ALU.mult, ALU.add))
            one(v.tensor_scalar(t_int, t1, 127.0, None, ALU.add))
            steps.settle()
            one(v.scalar_tensor_tensor(t0, t1, -LN2_LO, t0, ALU.mult, ALU.add))
            one(v.tensor_scalar(t_int, t_int, 23, None, ALU.logical_shift_left))
            steps.settle()
            one(v.tensor_scalar(dst, t0, 1 / math.factorial(8), 1 / math.factorial(7), ALU.mult, ALU.add))
            for n in range(6, -1, -1):
                steps.settle()
                one(v.tensor_tensor(dst, dst, t0, ALU.mult))
                steps.settle()
                one(v.tensor_scalar(dst, dst, 1 / math.factorial(n), None, ALU.add))
            steps.settle()
            one(v.tensor_tensor(dst, dst, t_int.bitcast(F32), ALU.mult))
            steps.settle()

        exponential(col(3), col(2), col(22), col(23), prm_int[:])
        steps.add(v.tensor_tensor(col(4), col(0), col(3), ALU.mult))
        steps.add(v.tensor_tensor(col(5), col(1), col(3), ALU.mult))
        steps.settle()
        steps.add(v.tensor_scalar(col(6), col(5), 1 / (2 * math.pi), ROUND, ALU.mult, ALU.add))
        steps.settle()
        steps.add(v.tensor_scalar(col(6), col(6), -ROUND, None, ALU.add))
        steps.settle()
        steps.add(v.scalar_tensor_tensor(col(7), col(6), -TWO_PI_HI, col(5), ALU.mult, ALU.add))
        steps.settle()
        steps.add(v.scalar_tensor_tensor(col(7), col(6), -TWO_PI_LO, col(7), ALU.mult, ALU.add))
        steps.settle()
        v.tensor_scalar(col(7), col(7), PI_DOWN, -PI_DOWN, ALU.min, ALU.max).then_inc(prm_angle, 1)
        exponential(col(8), col(4), col(22), col(23), prm_int[:])
        steps.add(v.tensor_tensor(col(9), col(8), col(8), ALU.mult))
        for _ in range(2):
            steps.settle()
            steps.add(v.tensor_tensor(col(9), col(9), col(9), ALU.mult))
        dve.wait_ge(prm_trig, 2)
        steps.add(v.tensor_tensor(col(12), col(11), col(11), ALU.mult))
        steps.settle()
        steps.add(v.tensor_scalar(col(12), col(12), -2.0, 1.0, ALU.mult, ALU.add))
        steps.add(v.tensor_tensor(col(14), col(8), col(10), ALU.mult))
        steps.settle()
        steps.add(v.tensor_tensor(col(13), col(8), col(12), ALU.mult))
        steps.settle()
        dve.sem_inc(prm_lam, 1)
        steps.add(v.tensor_tensor(col(15), col(0), col(0), ALU.mult))
        steps.add(v.tensor_tensor(col(16), col(1), col(1), ALU.mult))
        steps.add(v.tensor_scalar(col(17), col(13), -1.0, None, ALU.add))
        steps.settle()
        steps.add(v.tensor_tensor(col(15), col(15), col(16), ALU.add))
        steps.add(v.tensor_tensor(col(18), col(17), col(0), ALU.mult))
        steps.add(v.tensor_tensor(col(19), col(14), col(1), ALU.mult))
        steps.add(v.tensor_tensor(col(20), col(14), col(0), ALU.mult))
        steps.add(v.tensor_tensor(col(21), col(17), col(1), ALU.mult))
        steps.settle()
        steps.add(v.reciprocal(col(15), col(15)))
        steps.add(v.tensor_tensor(col(18), col(18), col(19), ALU.add))
        steps.add(v.tensor_tensor(col(20), col(20), col(21), ALU.subtract))
        steps.settle()
        steps.add(v.tensor_tensor(col(18), col(18), col(15), ALU.mult))
        steps.add(v.tensor_tensor(col(20), col(20), col(15), ALU.mult))
        steps.settle()

        def spread(i, d):
            return prm[:, i, PAIRS * d:PAIRS * (d + 1)].unsqueeze(2).to_broadcast([P, PAIRS, GC])

        def complex_step(dst, src, re, im):
            for d in range(2):
                t = w_tmp[:, d]
                sr, si = src[d]
                steps.add(v.tensor_tensor(t[:, 0], sr, spread(re, d), ALU.mult))
                steps.add(v.tensor_tensor(t[:, 1], si, spread(im, d), ALU.mult))
                steps.add(v.tensor_tensor(t[:, 2], sr, spread(im, d), ALU.mult))
                steps.add(v.tensor_tensor(t[:, 3], si, spread(re, d), ALU.mult))
            steps.settle()
            for d in range(2):
                t = w_tmp[:, d]
                dr, di = dst[d]
                steps.add(v.tensor_tensor(dr, t[:, 0], t[:, 1], ALU.subtract))
                steps.add(v.tensor_tensor(di, t[:, 2], t[:, 3], ALU.add))
            steps.settle()

        def modulation_used(j):
            dve.wait_ge(ada_mm, j + 1)
            part, half = j // 2, j % 2
            ps = bank(j % 4)
            if part in (2, 5):
                row = row_a if part == 2 else row_b
                cols = slice(HALF * half, HALF * (half + 1))
                v.tensor_tensor(row[:, cols], row[:, cols], ps, ALU.mult).then_inc(ada_used, 1)
                return
            kind = {0: 0, 1: 1, 3: 2, 4: 3}[part]
            for k in range(4):
                kk = 4 * half + k
                dst = stat_c[:, kk:kk + 1] if kind % 2 else mod_cols[:, kind, kk:kk + 1]
                ins = v.tensor_tensor_reduce(junk2[:], ps[:, P * k:P * (k + 1)], ident[:], 1.0, 0.0, ALU.mult, ALU.add, dst)
                if k < 3:
                    steps.add(ins)
                    steps.settle()
            ins.then_inc(ada_used, 1)
            dve.wait_ge(ada_used, j + 1)
            if kind % 2 and half == 1:
                steps.add(v.scalar_tensor_tensor(mod_cols[:, kind, :], stat_c[:, 0:KD], 1.0,
                                                 norm_cols[:, kind // 2, :], ALU.add, ALU.mult))
                steps.settle()

        dve.wait_ge(bc_in, 48)
        def lam_b_at(k):
            return [(lam_b[:, 0, d, :, s, :], lam_b[:, 1, d, :, s, :]) for d, s in ((0, CH - 1 - k), (1, k))]

        complex_step(lam_b_at(0), [(b_raw[:, 0, d], b_raw[:, 1, d]) for d in range(2)], 18, 20)
        for k in range(1, CH):
            modulation_used(k - 1)
            complex_step(lam_b_at(k), lam_b_at(k - 1), 13, 14)
        dve.sem_inc(lam_b_ready, 1)
        x_norm(dve, v, steps)
        for j in range(CH - 1, N_ADA):
            modulation_used(j)
        dve.wait_ge(ada_used, N_ADA)
        dve.sem_inc(mod_ready, 1)

        def split(n):
            dve.wait_ge(win_hi, n + 1)
            v.tensor_tensor(win_lower[n % 2][:], win_raw[n % 2][:], win_upper[n % 2][:], ALU.subtract).then_inc(win_lo, 1)

        for n in range(2):
            split(n)
        for i in range(2 * KD):
            k, cols = i // 2, slice(HALF * (i % 2), HALF * (i % 2 + 1))
            dve.wait_ge(h_made, i + 1)
            steps.add(v.tensor_copy(x_hi[:, k, cols], h_tmp[i % 2][:]))
            steps.settle()
            v.tensor_tensor(x_lo[:, k, cols], h_tmp[i % 2][:], x_hi[:, k, cols], ALU.subtract).then_inc(h_ready, 1)
        def square(dr, di, sr, si):
            steps.add(v.tensor_tensor(col(22), sr, sr, ALU.mult))
            steps.add(v.tensor_tensor(col(23), si, si, ALU.mult))
            steps.add(v.scalar_tensor_tensor(col(24), sr, 2.0, si, ALU.mult, ALU.mult))
            steps.settle()
            steps.add(v.tensor_tensor(dr, col(22), col(23), ALU.subtract))
            steps.add(v.tensor_copy(di, col(24)))
            steps.settle()

        square(pw[:, 0, 1], pw[:, 1, 1], col(12), col(10))
        square(pw[:, 0, 2], pw[:, 1, 2], pw[:, 0, 1], pw[:, 1, 1])
        square(pw[:, 0, 0], pw[:, 1, 0], pw[:, 0, 2], pw[:, 1, 2])
        for m in range(6):
            square(pw[:, 0, m + 1], pw[:, 1, m + 1], pw[:, 0, m], pw[:, 1, m])
        split(2)
        dve.wait_ge(k_mm, 1)
        taps = GROUPS * GC
        steps.add(v.memset(k_shift[:], 0.0))
        dsk = k_sum[0:GC, 0, :].rearrange("c (g o) -> c g o", g=GROUPS)
        steps.add(v.tensor_tensor(dsk, ident[0:GC, 0:GC].unsqueeze(1).to_broadcast([GC, GROUPS, GC]),
                                  dskip_cols[:].unsqueeze(2).to_broadcast([GC, GROUPS, GC]), ALU.mult))
        steps.add(v.tensor_copy(k_sum[:, 1, :], bank(7, taps)))
        steps.settle()
        steps.add(v.tensor_tensor(k_sum[0:GC, 1, :], k_sum[0:GC, 1, :], k_sum[0:GC, 0, :], ALU.add))
        steps.settle()
        dve.sem_inc(k_ready, 1)
        dve.wait_ge(k_shift_in, 16)
        v.tensor_tensor(k_sum[:, 0, :], bank(6, taps), k_shift[:], ALU.add).then_inc(k_ready, 1)
        for n in range(3, len(win_units)):
            split(n)

        mix_vector(dve, v, steps)

    @block.gpsimd
    def _(pool):
        steps = Steps(pool, pool_steps)
        g = nc.gpsimd
        pool.wait_ge(prm_lam, 1)
        pool.wait_ge(c_ready, 2)
        for d in range(2):
            re = prm[:, 13, PAIRS * d:PAIRS * (d + 1)].unsqueeze(2).to_broadcast([P, PAIRS, GC])
            im = prm[:, 14, PAIRS * d:PAIRS * (d + 1)].unsqueeze(2).to_broadcast([P, PAIRS, GC])
            src_r, src_n = c_plain[:, 0], c_plain[:, 1]
            for k in range(1, CH + 1):
                t = k - 1 if d == 0 else CH - k
                dst_r, dst_n = carry_out[:, d, 0, :, t, :], carry_out[:, d, 1, :, t, :]
                steps.add(g.tensor_tensor(e_tmp[:, 0], src_r, re, ALU.mult))
                steps.add(g.tensor_tensor(e_tmp[:, 1], src_n, im, ALU.mult))
                steps.add(g.tensor_tensor(e_tmp[:, 2], src_n, re, ALU.mult))
                steps.add(g.tensor_tensor(e_tmp[:, 3], src_r, im, ALU.mult))
                steps.settle()
                steps.add(g.tensor_tensor(dst_r, e_tmp[:, 0], e_tmp[:, 1], ALU.add))
                steps.add(g.tensor_tensor(dst_n, e_tmp[:, 2], e_tmp[:, 3], ALU.subtract))
                steps.settle()
                src_r, src_n = dst_r, dst_n
            pool.sem_inc(carry_ready, 1)
        mix_gpsimd(pool, steps)

    @block.tensor
    def _(pe):
        t = nc.tensor
        pe.wait_ge(ident_in, 16)
        pe.wait_ge(vec_in, 16 * 6)
        wide = 2 * D_FF // P
        t.transpose(bank(2, 2 * wide + 2 * KD), vec_rows[0][0:2 * wide + 2 * KD, :], ident[0:2 * wide + 2 * KD, 0:2 * wide + 2 * KD])
        t.transpose(bank(3, 2 * wide), vec_rows[1][0:2 * wide, :], ident[0:2 * wide, 0:2 * wide]).then_inc(rows_turned, 1)
        pe.wait_ge(ssm_in, 16 * 12)
        pe.wait_ge(dt_spread, 1)
        for i in range(3):
            t.transpose(bank(7, GROUPS, 32 * i), lam_rows[:, i, :], ident[0:GROUPS, 0:GROUPS])
        ins = t.transpose(bank(7, GROUPS, 96)[0:GC], dskip_rows[:], ident[0:GROUPS, 0:GROUPS])
        ins.then_inc(lam_turned, 1)
        for i in range(2):
            for b in range(3):
                ins = t.transpose(bank(4 + i, P, P * b), c_rows[:, i, b].rearrange("r t p -> r (t p)"), ident[:])
            ins.then_inc(c_turned, 1)

        def modulation(j):
            pe.wait_ge(ada_in[j % 3], 32 * (j // 3 + 1))
            if j == 2:
                pe.wait_ge(vec_used, 1)
            elif j >= 4:
                pe.wait_ge(ada_used, j - 3)
            for k in range(KD):
                t.matmul(bank(j % 4), c_bcast[:, k, :], ada_w[j % 3][:, k, :], start=(k == 0), stop=False)
            t.matmul(bank(j % 4), ones_row[:], ada_b[j % 3][:], start=False, stop=True).then_inc(ada_mm, 1)

        pe.wait_ge(c_spread, 2)
        for j in range(N_ADA - 2):
            modulation(j)
        pe.wait_ge(lam_b_ready, 1)
        pe.wait_ge(c_ready, 2)
        for d in range(2):
            for q in range(PAIRS):
                for ri in range(2):
                    ins = t.matmul(bank(6 + d, 2 * GC, 2 * GC * q), lam_b[:, ri, d, q].rearrange("p s c -> p (s c)"),
                                   c_pad[:, ri, q].rearrange("p e c -> p (e c)"), start=(ri == 0), stop=(ri == 1))
        ins.then_inc(k_mm, 1)
        for j in range(N_ADA - 2, N_ADA):
            modulation(j)
        for i in range(12):
            ri, d, q = i // 6, i // 3 % 2, 4 * (i % 3)
            if i >= 2:
                pe.wait_ge(win_ready, i - 1)
            for n in range(4):
                ins = t.transpose(bank(4 + i % 2, P, P * n), lam_b[:, ri, d, q + n].rearrange("p s c -> p (s c)"), ident[:])
            ins.then_inc(win_turned, 1)
        def unit_step(n, k):
            cols = slice(P * k, P * (k + 1))
            for m, (l, r) in enumerate(((win_upper, x_hi), (win_upper, x_lo), (win_lower, x_hi))):
                for half in range(2):
                    ins = t.matmul(bank(2 + 2 * (n % 3) + half), l[n % 2][:, cols], r[:, k, HALF * half:HALF * (half + 1)],
                                   start=(k == 0 and m == 0), stop=(k == KD - 1 and m == 2))
            return ins

        pe.wait_ge(ada_used, N_ADA)
        for k in range(KD + 1):
            for half in range(2 if k < KD else 0):
                i = 2 * k + half
                pe.wait_ge(x_scaled, 4 * (half + 1))
                if i >= 2:
                    pe.wait_ge(h_made, i - 1)
                for n in range(4):
                    ins = t.transpose(bank(i % 2, P, P * n), x_rows[:, 4 * half + n, P * k:P * (k + 1)], ident[:])
                ins.then_inc(x_turned, 1)
            if k:
                if k == 1:
                    pe.wait_ge(win_lo, 1)
                pe.wait_ge(h_ready, 2 * k)
                ins = unit_step(0, k - 1)
        ins.then_inc(win_mm, 1)
        for n in range(1, len(win_units)):
            pe.wait_ge(win_lo, n + 1)
            if n == 1:
                pe.wait_ge(win_ready, 12)
            elif n == 2:
                pe.wait_ge(k_ready, 2)
            elif n >= 3:
                pe.wait_ge(z_ready, n - 2)
            for k in range(KD):
                ins = unit_step(n, k)
            ins.then_inc(win_mm, 1)
        mix_tensor(pe, t)


def constants():
    n = np.arange(SEQ, dtype=np.int64)
    turn = 2 * np.pi / SEQ * ((n[:, None] * n[None, :]) % SEQ)
    m = np.arange(HEAD, dtype=np.int64)
    turn_d = 2 * np.pi / HEAD * ((m[:, None] * m[None, :]) % HEAD)
    dft = np.stack([np.cos(turn), np.sin(turn)], 1) / 32.0
    eye2 = np.eye(2)
    dft_d = np.stack([np.kron(eye2, np.cos(turn_d)), np.kron(eye2, -np.sin(turn_d))], 1) / 8.0
    dist = np.abs(np.arange(P)[:, None] + P - np.arange(SPAN)[None, :])
    slopes = np.exp2(np.float32(-8.0) * np.arange(1, Q_HEADS + 1, dtype=np.float32) / np.float32(Q_HEADS)).astype(np.float32)
    bias = -slopes[None, :, None] * dist[:, None, :].astype(np.float32)
    bias = np.where(dist[:, None, :] <= P, bias * np.float32(8.0), np.float32(8 * NEG))
    row, col = np.arange(P)[:, None], np.arange(P)[None, :]
    return {
        "ident": np.eye(P, dtype=np.float32),
        "dft": dft.astype(np.float32),
        "dft_d": dft_d.astype(np.float32),
        "att_bias": bias.astype(np.float32),
        "causal": np.where(col <= row, 0.0, NEG).astype(np.float32),
        "upper": (row <= col).astype(np.float32),
    }


_INS = ["x", "c", "w_ada", "b_ada", "g_pre_mix", "g_post_mix", "g_pre_ffn", "g_post_ffn", "w_in", "lam_re", "lam_im",
        "log_dt", "b_re", "b_im", "c_re", "c_im", "d_skip", "w_glu", "w_fft", "sink", "w_out", "w_up", "conv_w", "conv_b",
        "w_down", "ffn1_w1_2", "ffn1_w3_2", "ffn1_w2_2", "ln1_g_2", "ln1_b_2", "w_in_2", "kv_norm_g_2", "w_uk_2",
        "w_uv_2", "gmlp_ln_g_2", "gmlp_ln_b_2", "gmlp_ws_2", "gmlp_bs_2", "w_out_2", "ln2_g_2", "ln2_b_2",
        "ffn2_w1_2", "ffn2_w3_2", "ffn2_w2_2", "ln3_g_2", "ln3_b_2"]


def kernel(**inputs):
    import concourse.bacc as bacc
    from concourse.bass_utils import run_bass_kernel_spmd

    nc = bacc.Bacc("TRN2", target_bir_lowering=False, num_devices=1)
    arrays = {name: np.ascontiguousarray(inputs[name]) for name in _INS}
    arrays.update(constants())
    arrays = {f"in_{name}": array for name, array in arrays.items()}
    a = {name[3:]: nc.dram_tensor(name, array.shape, mybir.dt.from_np(array.dtype), kind="ExternalInput").ap()
         for name, array in arrays.items()}
    out = nc.dram_tensor("out", (1, SEQ, D), F32, kind="ExternalOutput").ap()
    build(nc, a, out)
    got = run_bass_kernel_spmd(nc, [arrays], core_ids=[0])
    return got.results[0]["out"]
```
